# Optimizing a Trainium2 kernel written in Bass

```python
import math
import jax, jax.numpy as jnp
from jax import lax
import numpy as np

'''One inference step of a hybrid decoder trunk (DEPTH layers), serving a prompt group and a
sample group with the same weights.

Per layer (parallel Griffin-style branches on one normalised input):
  h = RMSNorm(x)
  [q_d,k_d,v_d | q_s,k_s,v_s | q_idx,k_idx,w_idx | gate_d,gate_s] = h @ W_in   (single combined projection)
  y_d = DiffAttn(q_d,k_d,v_d) @ W_od ; y_s = DSA(q_s,k_s,v_s; indexer) @ W_os
  x = x + (sigmoid(gate_d) * y_d + sigmoid(gate_s) * y_s) @ W_out
  x = x + HierMoE(RMSNorm(x))   (top-1 expert group, then top-2 experts inside it)

Inputs:
  x_prompt (BATCH, SEQ, D_MODEL)          positions 0..SEQ-1
  x_sample (DEC_BATCH, DEC_SEQ, D_MODEL)  positions PAST_LEN..PAST_LEN+DEC_SEQ-1
  cache_diff_k (DEPTH, N_POOL, PAGE_SIZE, H_DIFF, 2, DH_DIFF)  paged (two key components per head)
  cache_diff_v (DEPTH, N_POOL, PAGE_SIZE, H_DIFF, 2*DH_DIFF)   paged
  cache_dsa_k  (DEPTH, N_POOL, PAGE_SIZE, H_DSA, DH_DSA)       paged
  cache_dsa_v  (DEPTH, N_POOL, PAGE_SIZE, H_DSA, DH_DSA)       paged
  cache_idx_k  (DEPTH, N_POOL, PAGE_SIZE, DH_IDX)              paged indexer keys
  page_table   (DEC_BATCH, N_PAGES) int32, N_PAGES = PAST_LEN // PAGE_SIZE
  weights, each with a leading DEPTH axis.
Keys are stored after QK-norm and rotary.
Output tuple:
  y_prompt (BATCH, SEQ, D_MODEL), y_sample (DEC_BATCH, DEC_SEQ, D_MODEL),
  new_diff_k_prompt (DEPTH, BATCH, SEQ, H_DIFF, 2, DH_DIFF), new_diff_v_prompt (DEPTH, BATCH, SEQ, H_DIFF, 2*DH_DIFF),
  new_dsa_k_prompt (DEPTH, BATCH, SEQ, H_DSA, DH_DSA), new_dsa_v_prompt (DEPTH, BATCH, SEQ, H_DSA, DH_DSA),
  new_idx_k_prompt (DEPTH, BATCH, SEQ, DH_IDX),
  new_diff_k_sample (DEPTH, DEC_BATCH, DEC_SEQ, H_DIFF, 2, DH_DIFF), new_diff_v_sample (DEPTH, DEC_BATCH, DEC_SEQ, H_DIFF, 2*DH_DIFF),
  new_dsa_k_sample (DEPTH, DEC_BATCH, DEC_SEQ, H_DSA, DH_DSA), new_dsa_v_sample (DEPTH, DEC_BATCH, DEC_SEQ, H_DSA, DH_DSA),
  new_idx_k_sample (DEPTH, DEC_BATCH, DEC_SEQ, DH_IDX).
'''

D_MODEL = 1024
BATCH = 1
SEQ = 512
DEPTH = 1
DEC_BATCH = 8
DEC_SEQ = 1
PAST_LEN = 512
PAGE_SIZE = 128

H_DIFF = 4
DH_DIFF = 64
H_DSA = 8
DH_DSA = 64
H_IDX = 8
DH_IDX = 64
TOPK_MAX = 256
N_GROUPS = 4
EXPERTS_PER_GROUP = 8
N_EXPERTS = N_GROUPS * EXPERTS_PER_GROUP
D_EXPERT = 512
TOP_K_EXPERTS = 2
ROPE_THETA = 10000.0
EPS = 1e-6
Q_BLOCK = 128
DSA_Q_BLOCK = 64

W_DIFF = H_DIFF * 2 * DH_DIFF
W_DSA = H_DSA * DH_DSA
W_IDX_Q = H_IDX * DH_IDX
SPLIT_SIZES = (W_DIFF, W_DIFF, W_DIFF, W_DSA, W_DSA, W_DSA, W_IDX_Q, DH_IDX, H_IDX, D_MODEL, D_MODEL)
P_TOTAL = 3 * W_DIFF + 3 * W_DSA + W_IDX_Q + DH_IDX + H_IDX + 2 * D_MODEL

kernel_name = 'diffattn_dsa_hiermoe_step'

def rmsnorm(x, g):
    xf = x.astype(jnp.float32)
    y = xf * lax.rsqrt(jnp.mean(xf * xf, axis=-1, keepdims=True) + EPS)
    return (y * g.astype(jnp.float32)).astype(x.dtype)

def rope(x, pos):
    half = x.shape[-1] // 2
    inv_freq = jnp.power(ROPE_THETA, -jnp.arange(half, dtype=jnp.float32) / half)
    ang = pos.astype(jnp.float32)[:, None] * inv_freq[None, :]
    cos = jnp.cos(ang)[:, None, :]
    sin = jnp.sin(ang)[:, None, :]
    xf = x.astype(jnp.float32)
    x1, x2 = xf[..., :half], xf[..., half:]
    return jnp.concatenate([x1 * cos - x2 * sin, x2 * cos + x1 * sin], axis=-1).astype(x.dtype)

def to_blocks(a, block):
    b, t = a.shape[:2]
    return jnp.moveaxis(a.reshape((b, t // block, block) + a.shape[2:]), 1, 0)

def from_blocks(a):
    a = jnp.moveaxis(a, 0, 1)
    return a.reshape((a.shape[0], a.shape[1] * a.shape[2]) + a.shape[3:])

def gather_pages(cache, page_table):
    g = cache[page_table]
    return g.reshape((g.shape[0], g.shape[1] * g.shape[2]) + g.shape[3:])

def diff_attention(q, k, v, q_pos, lam):
    s = jnp.einsum('bqhcd,bkhcd->bhcqk', q, k).astype(jnp.float32) * (DH_DIFF ** -0.5)
    causal = jnp.arange(k.shape[1])[None, :] <= q_pos[:, None]
    p = jax.nn.softmax(jnp.where(causal, s, -jnp.inf), axis=-1)
    a = p[:, :, 0] - lam * p[:, :, 1]
    return jnp.einsum('bhqk,bkhe->bqhe', a.astype(v.dtype), v)

def dsa_attention(q, k, v, q_idx, k_idx, w_idx, q_pos, k_sel):
    causal = jnp.arange(k.shape[1])[None, :] <= q_pos[:, None]
    dots = jnp.einsum('bqhd,bkd->bqhk', q_idx, k_idx).astype(jnp.float32) * (DH_IDX ** -0.5)
    score = jnp.einsum('bqhk,bqh->bqk', jax.nn.relu(dots), w_idx.astype(jnp.float32))
    score = jnp.where(causal[None], score, -jnp.inf)
    _, idx = lax.top_k(score, k_sel)
    valid = idx <= q_pos[None, :, None]
    k_g = jax.vmap(lambda rows, ii: rows[ii])(k, idx)
    v_g = jax.vmap(lambda rows, ii: rows[ii])(v, idx)
    s = jnp.einsum('bqhd,bqkhd->bhqk', q, k_g).astype(jnp.float32) * (DH_DSA ** -0.5)
    p = jax.nn.softmax(jnp.where(valid[:, None], s, -jnp.inf), axis=-1)
    return jnp.einsum('bhqk,bqkhd->bqhd', p.astype(v.dtype), v_g)

def token_mixing(x, pos, past, lam_init, k_sel, q_block, dsa_block,
                 g_mix, w_in, g_q_diff, g_k_diff, lam_q1, lam_k1, lam_q2, lam_k2, g_subln,
                 g_q_dsa, g_k_dsa, w_o_diff, w_o_dsa, w_out):
    b, t, _ = x.shape
    h = rmsnorm(x, g_mix)
    proj = h @ w_in
    points = np.cumsum(SPLIT_SIZES)[:-1].tolist()
    (q_d, k_d, v_d, q_s, k_s, v_s, q_i, k_i, w_i, gt_d, gt_s) = jnp.split(proj, points, axis=-1)
    q_d = rope(rmsnorm(q_d.reshape(b, t, 2 * H_DIFF, DH_DIFF), g_q_diff), pos).reshape(b, t, H_DIFF, 2, DH_DIFF)
    k_d = rope(rmsnorm(k_d.reshape(b, t, 2 * H_DIFF, DH_DIFF), g_k_diff), pos).reshape(b, t, H_DIFF, 2, DH_DIFF)
    v_d = v_d.reshape(b, t, H_DIFF, 2 * DH_DIFF)
    q_s = rope(rmsnorm(q_s.reshape(b, t, H_DSA, DH_DSA), g_q_dsa), pos)
    k_s = rope(rmsnorm(k_s.reshape(b, t, H_DSA, DH_DSA), g_k_dsa), pos)
    v_s = v_s.reshape(b, t, H_DSA, DH_DSA)
    q_i = rope(q_i.reshape(b, t, H_IDX, DH_IDX), pos)
    k_i = rope(k_i[:, :, None, :], pos)[:, :, 0]
    w_i = w_i * (H_IDX ** -0.5)
    rows = (k_d, v_d, k_s, v_s, k_i)
    if past is None:
        kd_all, vd_all, ks_all, vs_all, ki_all = rows
    else:
        kd_all = jnp.concatenate([past[0], k_d.astype(past[0].dtype)], axis=1)
        vd_all = jnp.concatenate([past[1], v_d.astype(past[1].dtype)], axis=1)
        ks_all = jnp.concatenate([past[2], k_s.astype(past[2].dtype)], axis=1)
        vs_all = jnp.concatenate([past[3], v_s.astype(past[3].dtype)], axis=1)
        ki_all = jnp.concatenate([past[4], k_i.astype(past[4].dtype)], axis=1)
    f32 = jnp.float32
    lam = (jnp.exp(jnp.sum(lam_q1.astype(f32) * lam_k1.astype(f32)))
           - jnp.exp(jnp.sum(lam_q2.astype(f32) * lam_k2.astype(f32))) + lam_init)
    if q_block is None:
        o_d = diff_attention(q_d, kd_all, vd_all, pos, lam)
        o_s = dsa_attention(q_s, ks_all, vs_all, q_i, ki_all, w_i, pos, k_sel)
    else:
        o_d = from_blocks(lax.map(
            lambda a: diff_attention(a[0], kd_all, vd_all, a[1], lam),
            (to_blocks(q_d, q_block), pos.reshape(-1, q_block))))
        o_s = from_blocks(lax.map(
            lambda a: dsa_attention(a[0], ks_all, vs_all, a[1], ki_all, a[2], a[3], k_sel),
            (to_blocks(q_s, dsa_block), to_blocks(q_i, dsa_block), to_blocks(w_i, dsa_block),
             pos.reshape(-1, dsa_block))))
    o_d = rmsnorm(o_d, g_subln) * (1.0 - lam_init)
    y_d = o_d.reshape(b, t, W_DIFF) @ w_o_diff
    y_s = o_s.reshape(b, t, W_DSA) @ w_o_dsa
    merged = jax.nn.sigmoid(gt_d) * y_d + jax.nn.sigmoid(gt_s) * y_s
    return x + merged @ w_out, rows

def hier_moe(x, g_ffn, w_group, w_router, w_gate, w_up, w_down):
    b, t, d = x.shape
    h = rmsnorm(x, g_ffn).reshape(b * t, d)
    g_logits = jnp.dot(h, w_group).astype(jnp.float32)
    g_prob = jax.nn.softmax(g_logits, axis=-1)
    g_sel = jnp.argmax(g_logits, axis=-1)
    g_w = jnp.take_along_axis(g_prob, g_sel[:, None], axis=-1)
    e_logits = jnp.dot(h, w_router).astype(jnp.float32).reshape(-1, N_GROUPS, EXPERTS_PER_GROUP)
    e_in_group = jnp.take_along_axis(e_logits, g_sel[:, None, None], axis=1)[:, 0]
    top_val, top_idx = lax.top_k(e_in_group, TOP_K_EXPERTS)
    top_w = jax.nn.softmax(top_val, axis=-1) * g_w
    expert_id = g_sel[:, None] * EXPERTS_PER_GROUP + top_idx
    combine = jnp.einsum('nk,nke->en', top_w,
                         jax.nn.one_hot(expert_id, N_EXPERTS, dtype=jnp.float32)).astype(h.dtype)

    def add_expert(acc, params):
        wg, wu, wd, c = params
        act = jax.nn.silu(h @ wg) * (h @ wu)
        return acc + (act @ wd) * c[:, None], None

    out, _ = lax.scan(add_expert, jnp.zeros_like(h), (w_gate, w_up, w_down, combine))
    return out.reshape(b, t, d)

def setup_inputs(seed: int = 0) -> dict:
    key = jax.random.key(seed)
    ks = jax.random.split(key, 32)
    n_pages = PAST_LEN // PAGE_SIZE
    n_used = DEC_BATCH * n_pages
    n_pool = n_used + max(1, n_used // 4)
    page_table = jax.random.permutation(ks[0], n_pool)[:n_used].reshape(DEC_BATCH, n_pages).astype(jnp.int32)

    def normal(k, shape, scale=1.0):
        return scale * jax.random.normal(k, shape, jnp.float32)

    def gain(k, shape):
        return 1.0 + 0.02 * jax.random.normal(k, shape, jnp.float32)

    return {
        'x_prompt': normal(ks[1], (BATCH, SEQ, D_MODEL)),
        'x_sample': normal(ks[2], (DEC_BATCH, DEC_SEQ, D_MODEL)),
        'cache_diff_k': normal(ks[3], (DEPTH, n_pool, PAGE_SIZE, H_DIFF, 2, DH_DIFF)),
        'cache_diff_v': normal(ks[4], (DEPTH, n_pool, PAGE_SIZE, H_DIFF, 2 * DH_DIFF)),
        'cache_dsa_k': normal(ks[5], (DEPTH, n_pool, PAGE_SIZE, H_DSA, DH_DSA)),
        'cache_dsa_v': normal(ks[6], (DEPTH, n_pool, PAGE_SIZE, H_DSA, DH_DSA)),
        'cache_idx_k': normal(ks[7], (DEPTH, n_pool, PAGE_SIZE, DH_IDX)),
        'page_table': page_table,
        'g_mix': gain(ks[8], (DEPTH, D_MODEL)),
        'w_in': normal(ks[9], (DEPTH, D_MODEL, P_TOTAL), D_MODEL ** -0.5),
        'g_q_diff': gain(ks[10], (DEPTH, DH_DIFF)),
        'g_k_diff': gain(ks[11], (DEPTH, DH_DIFF)),
        'lam_q1': normal(ks[12], (DEPTH, DH_DIFF), 0.1),
        'lam_k1': normal(ks[13], (DEPTH, DH_DIFF), 0.1),
        'lam_q2': normal(ks[14], (DEPTH, DH_DIFF), 0.1),
        'lam_k2': normal(ks[15], (DEPTH, DH_DIFF), 0.1),
        'g_subln': gain(ks[16], (DEPTH, 2 * DH_DIFF)),
        'g_q_dsa': gain(ks[17], (DEPTH, DH_DSA)),
        'g_k_dsa': gain(ks[18], (DEPTH, DH_DSA)),
        'w_o_diff': normal(ks[19], (DEPTH, W_DIFF, D_MODEL), W_DIFF ** -0.5),
        'w_o_dsa': normal(ks[20], (DEPTH, W_DSA, D_MODEL), W_DSA ** -0.5),
        'w_out': normal(ks[21], (DEPTH, D_MODEL, D_MODEL), D_MODEL ** -0.5),
        'g_ffn': gain(ks[22], (DEPTH, D_MODEL)),
        'w_group': normal(ks[23], (DEPTH, D_MODEL, N_GROUPS), D_MODEL ** -0.5),
        'w_router': normal(ks[24], (DEPTH, D_MODEL, N_EXPERTS), D_MODEL ** -0.5),
        'w_gate': normal(ks[25], (DEPTH, N_EXPERTS, D_MODEL, D_EXPERT), D_MODEL ** -0.5),
        'w_up': normal(ks[26], (DEPTH, N_EXPERTS, D_MODEL, D_EXPERT), D_MODEL ** -0.5),
        'w_down': normal(ks[27], (DEPTH, N_EXPERTS, D_EXPERT, D_MODEL), D_EXPERT ** -0.5),
    }

def reference(x_prompt, x_sample, cache_diff_k, cache_diff_v, cache_dsa_k, cache_dsa_v, cache_idx_k,
              page_table, g_mix, w_in, g_q_diff, g_k_diff, lam_q1, lam_k1, lam_q2, lam_k2, g_subln,
              g_q_dsa, g_k_dsa, w_o_diff, w_o_dsa, w_out, g_ffn, w_group, w_router, w_gate, w_up, w_down):
    seq = x_prompt.shape[1]
    dec_seq = x_sample.shape[1]
    past_len = page_table.shape[1] * cache_diff_k.shape[2]
    pos_p = jnp.arange(seq, dtype=jnp.int32)
    pos_s = past_len + jnp.arange(dec_seq, dtype=jnp.int32)
    k_sel_p = min(TOPK_MAX, seq // 4)
    k_sel_s = min(TOPK_MAX, (past_len + dec_seq) // 4)
    y_p, y_s = x_prompt, x_sample
    rows_p, rows_s = [], []
    for l in range(DEPTH):
        lam_init = 0.8 - 0.6 * math.exp(-0.3 * l)
        mix_params = (g_mix[l], w_in[l], g_q_diff[l], g_k_diff[l], lam_q1[l], lam_k1[l], lam_q2[l], lam_k2[l],
                      g_subln[l], g_q_dsa[l], g_k_dsa[l], w_o_diff[l], w_o_dsa[l], w_out[l])
        moe_params = (g_ffn[l], w_group[l], w_router[l], w_gate[l], w_up[l], w_down[l])
        past = (gather_pages(cache_diff_k[l], page_table), gather_pages(cache_diff_v[l], page_table),
                gather_pages(cache_dsa_k[l], page_table), gather_pages(cache_dsa_v[l], page_table),
                gather_pages(cache_idx_k[l], page_table))
        y_p, r_p = token_mixing(y_p, pos_p, None, lam_init, k_sel_p, Q_BLOCK, DSA_Q_BLOCK, *mix_params)
        y_p = y_p + hier_moe(y_p, *moe_params)
        y_s, r_s = token_mixing(y_s, pos_s, past, lam_init, k_sel_s, None, None, *mix_params)
        y_s = y_s + hier_moe(y_s, *moe_params)
        rows_p.append(r_p)
        rows_s.append(r_s)
    new_diff_k_p = jnp.stack([r[0] for r in rows_p])
    new_diff_v_p = jnp.stack([r[1] for r in rows_p])
    new_dsa_k_p = jnp.stack([r[2] for r in rows_p])
    new_dsa_v_p = jnp.stack([r[3] for r in rows_p])
    new_idx_k_p = jnp.stack([r[4] for r in rows_p])
    new_diff_k_s = jnp.stack([r[0] for r in rows_s])
    new_diff_v_s = jnp.stack([r[1] for r in rows_s])
    new_dsa_k_s = jnp.stack([r[2] for r in rows_s])
    new_dsa_v_s = jnp.stack([r[3] for r in rows_s])
    new_idx_k_s = jnp.stack([r[4] for r in rows_s])
    return (y_p, y_s, new_diff_k_p, new_diff_v_p, new_dsa_k_p, new_dsa_v_p, new_idx_k_p,
            new_diff_k_s, new_diff_v_s, new_dsa_k_s, new_dsa_v_s, new_idx_k_s)


_drawn_inputs = setup_inputs


def setup_inputs(seed=0):
    import zlib

    import numpy as np

    out = dict(_drawn_inputs(seed))
    spreads = {}
    factors = {'g_k_diff': 2.704, 'lam_q2': 20.354, 'g_q_dsa': 8.0, 'g_k_dsa': 2.853, 'g_subln': 3.162}
    for name, (base, spread) in spreads.items():
        noise = np.random.default_rng([zlib.crc32(name.encode()), seed]).standard_normal(out[name].shape)
        drawn = base * np.exp(spread * noise) if base else spread * noise
        out[name] = __import__('jax').numpy.asarray(drawn.astype(out[name].dtype))
    for name, factor in factors.items():
        out[name] = (out[name] * factor).astype(out[name].dtype)
    return out
```

```python
import concourse.bass as bass
from concourse import mybir
from contextlib import ExitStack
import numpy as np

F32, I32 = mybir.dt.float32, mybir.dt.int32
ALU = mybir.AluOpType
ACT = mybir.ActivationFunctionType
AX = mybir.AxisListType

D = 1024
KD = D // 128
SEQ, NS = 512, 8
NT = SEQ // 128
TILES = NT + 1
TOK = SEQ + NS
ROWS = [128] * NT + [NS]
H, DH = 8, 64
W = H * DH
NB = W // 128
PAGE, NPAGE = 128, 4
PAST = PAGE * NPAGE
TOPK = 128
P_TOTAL = 7 * W + DH + H + 2 * D
OFF = dict(qd=0, kd=W, vd=2 * W, qs=3 * W, ks=4 * W, vs=5 * W, qi=6 * W, kw=7 * W,
           gd=7 * W + DH + H, gs=7 * W + DH + H + D)
NG, EG = 4, 8
NE = NG * EG
DE = 512
CAP = 64
NX = 2 * TOK // CAP
NBLK = NE + NX
EPS = 1e-6
LAM_INIT = 0.2
MASKED, TAKEN = -2.0e38, -3.0e38

C_ID, C_LT, C_ONE, C_CM = 0, 128, 256, 384
C_E, C_ET, C_HM, C_IOTA, C_TOK, C_THR, C_MH, C_PAR, C_END = 896, 960, 968, 976, 1040, 1045, 1061, 1069, 1070


def constants():
    c = np.zeros((128, C_END), np.float32)
    p = np.arange(128)
    c[:, C_ID:C_LT] = np.eye(128)
    c[:, C_LT:C_ONE] = p[:, None] < p[None, :]
    c[:, C_ONE:C_CM] = 1
    c[:, C_CM + 384:C_E] = np.where(p[None, :] <= p[:, None], 0, MASKED)
    for b in range(NS):
        c[b, C_E + 8 * b:C_E + 8 * b + 8] = 1
    c[:64, C_ET:C_HM] = (p[:64, None] // 8) == np.arange(8)
    c[:64, C_HM:C_IOTA] = (p[:64, None] % 8) == np.arange(8)
    c[:, C_IOTA:C_TOK] = np.arange(64)
    c[:, C_TOK:C_THR] = p[:, None] + 128 * np.arange(TILES)
    c[:, C_THR:C_MH] = CAP * (1 + np.arange(16))
    c[:, C_MH:C_PAR] = -0.5
    c[:, C_PAR] = p % 2
    return c


def rope_table():
    pos = np.full(128 * TILES, PAST, np.float32)
    pos[:SEQ] = np.arange(SEQ)
    inv = np.power(np.float32(10000.0), -np.arange(DH // 2, dtype=np.float32) / np.float32(DH // 2))
    ang = (pos[:, None] * inv[None]).astype(np.float32)
    t = np.stack([np.cos(ang), np.cos(ang), np.sin(ang), np.sin(ang)], 1).astype(np.float32)
    return np.ascontiguousarray(t.reshape(TILES, 128, 2, DH).transpose(1, 2, 0, 3).reshape(128, -1))


class Chain:

    def __init__(self, eng, sem):
        self.eng, self.sem, self.n = eng, sem, 0

    def __call__(self, ins):
        self.n += 1
        ins.then_inc(self.sem, 1)
        self.eng.wait_ge(self.sem, self.n)


def bcast(ap, n, axis):
    shape = list(ap.shape)
    return ap.unsqueeze(axis).to_broadcast(shape[:axis] + [n] + shape[axis:])


ORDER = ["qi", "kw", "ks", "qs", "vs", "kd", "qd", "vd"]
UNITS = [(k, i) for k in ORDER for i in range(TILES)]
NORMED = ("ks", "qs", "kd", "qd")
TURNED = ("qi", "kw") + NORMED
STORED = ("kw", "ks", "kd", "vs", "vd")
WIDTH = {k: W for k in ORDER} | {"kw": DH + H}


def is_turned(unit):
    return unit[0] in TURNED and (unit[1] < NT or unit[0] in ("qi", "kw"))


def turned_before(u):
    return sum(is_turned(v) for v in UNITS[:u])


def normed_before(u):
    return sum(k in NORMED for k, _ in UNITS[:u])


def small_product(nc, bank, xT, w, steps):
    for j in range(steps):
        for g in range(NB):
            last = nc.tensor.matmul(bank[32 * g:32 * g + NS, 0:128], xT[:, j, 0:NS], w[:, j, 128 * g:128 * g + 128],
                                    start=j == 0, stop=j == steps - 1)
    return last


def normalise_inputs(nc, io, s):
    with ExitStack() as ctx:
        sq = ctx.enter_context(nc.sbuf_tensor("n_sq", [128, D], F32))
        ms = ctx.enter_context(nc.sbuf_tensor("n_ms", [128, TILES], F32))
        rs = ctx.enter_context(nc.sbuf_tensor("n_rs", [128, TILES], F32))
        xn = ctx.enter_context(nc.sbuf_tensor("n_xn", [128, 2, D], F32))
        tp = ctx.enter_context(nc.psum_tensor("n_tp", [128, 2, 4, 128], F32))
        sem = lambda n: ctx.enter_context(nc.semaphore("n_" + n))
        x_in, consts_in, x_sq, rms, x_scaled, turned, evicted, tables_in, chain = map(
            sem, ["x_in", "consts_in", "x_sq", "rms", "x_scaled", "turned", "evicted", "tables_in", "chain"])
        block = ctx.enter_context(nc.Block())

        @block.sync
        def _(sp):
            sp.dma_start(s.x[:, 0:NT, :], io["x_prompt"][0].rearrange("(i p) d -> p i d", p=128)).then_inc(x_in, 16)
            sp.dma_start(s.x[0:NS, NT, :], io["x_sample"][:, 0, :]).then_inc(x_in, 16)
            sp.dma_start(s.c[:], io["consts"]).then_inc(consts_in, 16)
            sp.dma_start(s.gmix[:], io["g_mix"][0].rearrange("(j p) -> p j", p=128), allow_slow_non_contiguous=True).then_inc(consts_in, 16)
            sp.dma_start(s.rope[:], io["rope"]).then_inc(tables_in, 16)
            for n, g in enumerate(("g_k_dsa", "g_q_dsa", "g_k_diff", "g_q_diff")):
                sp.dma_start(s.gains[:, n, :], io[g].to_broadcast([128, DH])).then_inc(tables_in, 16)
            for n in range(2):
                k = ORDER[n]
                sp.dma_start(s.w[:, n, :, 0:WIDTH[k]], io["w_in"][0][:, OFF[k]:OFF[k] + WIDTH[k]]
                             .rearrange("(j p) c -> p j c", p=128)).then_inc(s.w_in[n], 16)

        @block.scalar
        def _(act):
            act.wait_ge(x_in, 32)
            for i, p in enumerate(ROWS):
                if i:
                    act.wait_ge(x_sq, i)
                nc.scalar.activation(sq[0:p, :], s.x[0:p, i, :], ACT.Square, accum_out=ms[0:p, i:i + 1]).then_inc(x_sq, 1)

        @block.gpsimd
        def _(pool):
            pool.wait_ge(consts_in, 32)
            for i, p in enumerate(ROWS):
                pool.wait_ge(x_sq, i + 1)
                nc.gpsimd.tensor_scalar(rs[0:p, i:i + 1], ms[0:p, i:i + 1], 1.0 / D, EPS, ALU.mult, ALU.add).then_inc(chain, 1)
                pool.wait_ge(chain, 2 * i + 1)
                nc.gpsimd.tensor_tensor(rs[0:p, i:i + 1], rs[0:p, i:i + 1], s.c[0:p, C_MH:C_MH + 1], ALU.pow).then_inc(chain, 1)
                pool.wait_ge(chain, 2 * i + 2)
                pool.sem_inc(rms, 1)

        @block.vector
        def _(dve):
            dve.wait_ge(x_in, 32)
            for i, p in enumerate(ROWS):
                dve.wait_ge(rms, i + 1)
                if i >= 2:
                    dve.wait_ge(turned, 2 * (i - 1))
                nc.vector.tensor_scalar(xn[0:p, i % 2, :], s.x[0:p, i, :], rs[0:p, i:i + 1], None, ALU.mult).then_inc(x_scaled, 1)
                for h in range(2):
                    dve.wait_ge(turned, 2 * i + h + 1)
                    nc.vector.tensor_tensor(s.xT[:, 4 * h:4 * h + 4, 128 * i:128 * i + p], tp[:, h, :, 0:p],
                                            bcast(s.gmix[:, 4 * h:4 * h + 4], p, 2), ALU.mult).then_inc(evicted, 1)
            dve.wait_ge(tables_in, 80)
            for n in range(4):
                for t in range(2):
                    nc.vector.tensor_tensor(s.rg[:, n, t], s.rope[:, t], bcast(s.gains[:, n, :], TILES, 1), ALU.mult)

        @block.tensor
        def _(pe):
            pe.wait_ge(consts_in, 32)
            for i, p in enumerate(ROWS):
                pe.wait_ge(x_scaled, i + 1)
                for h in range(2):
                    if i:
                        pe.wait_ge(evicted, 2 * (i - 1) + h + 1)
                    for j in range(4):
                        last = nc.tensor.transpose(tp[:, h, j, 0:p], xn[0:p, i % 2, (4 * h + j) * 128:(4 * h + j + 1) * 128],
                                                   s.ident[0:p, 0:p])
                    last.then_inc(turned, 1)


IDX_FROM = 12
IDX_STEPS = [(t, h) for t in range(1, NT) for h in range(H)]
TK_ROUNDS = TOPK // 8


def project(nc, io, s):
    U = len(UNITS)
    with ExitStack() as ctx:
        sb = lambda n, sh, dt=F32: ctx.enter_context(nc.sbuf_tensor("p_" + n, sh, dt))
        ps = lambda n, sh: ctx.enter_context(nc.psum_tensor("p_" + n, sh, F32))
        sem = lambda n: ctx.enter_context(nc.semaphore("p_" + n))
        sq = sb("sq", [128, 2, W])
        ms, rs = sb("ms", [128, 2, H]), sb("rs", [128, 2, H])
        t0, ta, tb = sb("t0", [128, W]), sb("ta", [128, W]), sb("tb", [128, W])
        y = sb("y", [128, 4, W])
        qiT, kiT = sb("qiT", [128, NB, SEQ]), sb("kiT", [128, SEQ])
        kiTs = sb("kiTs", [128, NS])
        wi = sb("wi", [128, TILES, H])
        relu = sb("relu", [128, 2, W])
        m8 = sb("m8", [128, 8])
        score, score_s = [t for t in s.sel[1:]], s.sel_s
        zs = sb("zs", [NS, W])
        pages_i = s.oT["d"][:].rearrange("p j t -> p (j t)")[:, 0:NS * NPAGE * DH].rearrange("p (b n d) -> p b n d", b=NS, n=NPAGE)
        kTi = s.oT["s"][0:DH].rearrange("p j t -> p (j t)")[:, 0:2 * PAST].rearrange("p (a k) -> p a k", a=2)
        qblk = sb("qblk", [DH, 72 * NS])
        relu_s = sb("relu_s", [64, PAST + 1])
        wcol, wtmp, ew = sb("wcol", [64, 1]), sb("wtmp", [64, H]), sb("ew", [64, NS])
        ptab = sb("ptab", [1, NS * NPAGE], I32)
        z = [ps(f"z{n}", [128, W]) for n in range(3)]
        tp = [ps(f"tp{n}", [128, W]) for n in range(2)]
        xs = [ps(f"xs{n}", [128, W]) for n in range(2)]
        ss = ps("ss", [64, PAST])
        (proj, z_free, squared, ms_ready, rs_ready, y_ready, turned, turn_out, pool_chain, chain, x_ready, x_free, relu_done, relu_used,
         wi_ready, ptab_in, pages_in, kTi_ready, ss_ready, samp, blk0, zs_ready) = map(sem, (
             "proj z_free squared ms_ready rs_ready y_ready turned turn_out pool_chain chain x_ready x_free relu_done "
             "relu_used wi_ready ptab_in pages_in kTi_ready ss_ready samp blk0 zs_ready").split())
        stored = [sem(f"stored{n}") for n in range(4)]
        v_stored, zeroed, rest_zeroed = sem("v_stored"), sem("zeroed"), sem("rest_zeroed")
        zero = s.oT["s"][:].rearrange("p j t -> p (j t)")[:, 2 * PAST:2 * PAST + 256]
        block = ctx.enter_context(nc.Block())
        extras = {IDX_FROM + n // 3: IDX_STEPS[n:n + 3] for n in range(0, len(IDX_STEPS), 3)}
        SAMPLE_AT = IDX_FROM + len(IDX_STEPS) // 3
        y_of = {}
        slot_stores = [0, 0, 0, 0]
        for u, (k, i) in enumerate(UNITS):
            if k in STORED and k[0] == "k":
                slot_stores[u % 4] += 1
            y_of[u] = slot_stores[u % 4]
        out_of = dict(kw="ki", ks="ks", kd="kd", vs="vs", vd="vd")

        @block.sync
        def _(sp):
            sp.dma_start(ptab[:], io["page_table"].rearrange("b n -> (b n)").unsqueeze(0)).then_inc(ptab_in, 16)
            sp.wait_ge(ptab_in, 16)
            n_v = 0
            for b in range(NS):
                for n in range(NPAGE):
                    page = sp.value_load(ptab[0:1, b * NPAGE + n:b * NPAGE + n + 1], min_val=0, max_val=s.pool - 1)
                    sp.dma_start(pages_i[:, b, n, :], io["cache_idx_k"][0, page]).then_inc(pages_in, 16)
            for u, (k, i) in enumerate(UNITS):
                p = ROWS[i]
                if k in STORED:
                    sp.wait_ge(y_ready, u + 1)
                    dst = io["new_%s_%s" % (out_of[k], "p" if i < NT else "s")]
                    dst = dst[128 * i:128 * i + p] if i < NT else dst[:]
                    if k[0] == "v":
                        sp.dma_start(dst, s.v[k][:, i, :] if i < NT else s.row[k][:]).then_inc(v_stored, 16)
                        n_v += 1
                    else:
                        n = DH if k == "kw" else W
                        sp.dma_start(dst, y[0:p, u % 4, 0:n]).then_inc(stored[u % 4], 16)
                c = u // TILES
                if i == NT and c + 2 < len(ORDER):
                    sp.wait_ge(proj, u + 1)
                    k2 = ORDER[c + 2]
                    sp.dma_start(s.w[:, c % 2, :, 0:WIDTH[k2]], io["w_in"][0][:, OFF[k2]:OFF[k2] + WIDTH[k2]]
                                 .rearrange("(j p) c -> p j c", p=128)).then_inc(s.w_in[c % 2], 16)
            for n, k in enumerate(("gd", "gs")):
                sp.wait_ge(proj, U if n else U - TILES)
                sp.dma_start(s.w[:, n], io["w_in"][0][:, OFF[k]:OFF[k] + W].rearrange("(j p) c -> p j c", p=128)).then_inc(s.w_in[n], 16)
            for n in range(4):
                sp.wait_ge(stored[n], 16 * slot_stores[n])
            sp.wait_ge(v_stored, 16 * n_v)

        @block.tensor
        def _(pe):
            nt = ne = 0

            def turn(u):
                nonlocal nt
                if u < 0 or not is_turned(UNITS[u]):
                    return
                k, i = UNITS[u]
                p = ROWS[i]
                pe.wait_ge(y_ready, u + 1)
                if nt >= 2:
                    pe.wait_ge(turn_out, nt - 1)
                bank = tp[nt % 2]
                if k == "qi" and i == NT:
                    for h in range(H):
                        last = nc.tensor.transpose(bank[0:DH, NS * h:NS * h + NS], y[0:p, u % 4, DH * h:DH * h + DH], s.ident[0:p, 0:p])
                else:
                    for j in range(1 if k == "kw" else NB):
                        last = nc.tensor.transpose(bank[:, p * j:p * j + p], y[0:p, u % 4, 128 * j:128 * j + 128], s.ident[0:p, 0:p])
                last.then_inc(turned, 1)
                nt += 1

            def take_bank():
                nonlocal ne
                n_p = len(IDX_STEPS)
                if 2 <= ne < n_p + 2:
                    pe.wait_ge(x_free, ne - 1)
                elif n_p + 2 <= ne < n_p + NS + 2:
                    pe.wait_ge(kTi_ready, ne - 1 - n_p)
                elif ne >= n_p + NS + 2:
                    pe.wait_ge(x_free, ne - 1 - NS)
                ne += 1
                return xs[(ne - 1) % 2]

            for u in range(U + 2):
                if u < U:
                    k, i = UNITS[u]
                    c, p = u // TILES, ROWS[i]
                    if i == 0:
                        pe.wait_ge(s.w_in[c % 2], 16 * (c // 2 + 1))
                    if u >= 3:
                        pe.wait_ge(z_free, u - 2)
                    if i == NT and k != "kw":
                        last = small_product(nc, z[u % 3], s.xT[:, :, SEQ:TOK], s.w[:, c % 2], KD)
                    else:
                        for j in range(KD):
                            last = nc.tensor.matmul(z[u % 3][0:p, 0:WIDTH[k]], s.xT[:, j, 128 * i:128 * i + p],
                                                    s.w[:, c % 2, j, 0:WIDTH[k]], start=j == 0, stop=j == KD - 1)
                    last.then_inc(proj, 1)
                turn(u - 2)
                if u == IDX_FROM:
                    pe.wait_ge(turn_out, turned_before(2 * TILES))
                for t, h in extras.get(u, ()):
                    bank, r = take_bank(), 64 * (h % 2)
                    nc.tensor.matmul(bank[:, 0:128 * (t + 1)], qiT[r:r + 64, h // 2, 128 * t:128 * t + 128],
                                     kiT[r:r + 64, 0:128 * (t + 1)], start=True, stop=True).then_inc(x_ready, 1)
                if u == SAMPLE_AT:
                    pe.wait_ge(pages_in, 16 * NS * NPAGE)
                    pe.wait_ge(blk0, 2)
                    for b in range(NS):
                        bank = take_bank()
                        for n in range(NPAGE):
                            last = nc.tensor.transpose(bank[0:DH, 128 * n:128 * n + 128], pages_i[:, b, n, :], s.ident[:])
                        last.then_inc(x_ready, 1)
                        pe.wait_ge(kTi_ready, b + 1)
                        last = nc.tensor.matmul(ss[:], qblk[:, 64 * b:64 * b + 64], kTi[:, b % 2, :], start=b == 0, stop=b == NS - 1)
                        last.then_inc(ss_ready, 1)
                    bank = take_bank()
                    for b in range(NS):
                        nc.tensor.matmul(bank[0:64, 0:1], qblk[:, 64 * b:64 * b + 64], kiTs[0:DH, b:b + 1], start=b == 0, stop=b == NS - 1)
                    pe.wait_ge(wi_ready, TILES)
                    nc.tensor.matmul(bank[0:64, 8:16], s.c[0:NS, C_E:C_ET], wi[0:NS, NT, :], start=True, stop=True).then_inc(x_ready, 1)
                    pe.wait_ge(samp, 3)
                    bank = take_bank()
                    nc.tensor.matmul(bank[0:NS, :], ew[:], relu_s[:, 0:PAST], start=True, stop=True).then_inc(x_ready, 1)
                    bank = take_bank()
                    nc.tensor.matmul(bank[0:NS, 0:1], ew[:], relu_s[:, PAST:PAST + 1], start=True, stop=True).then_inc(x_ready, 1)

        @block.scalar
        def _(act):
            ns = nt = nx = nz = 0
            for u in range(U + 2):
                if u < U and UNITS[u][1] == NT and UNITS[u][0] != "kw":
                    act.wait_ge(proj, u + 1)
                    if u >= TILES:
                        act.wait_ge(y_ready, u - TILES + 1)
                    for g in range(NB):
                        nc.scalar.copy(zs[:, 128 * g:128 * g + 128], z[u % 3][32 * g:32 * g + NS, 0:128]).then_inc(zs_ready, 1)
                    nz += NB
                    act.wait_ge(zs_ready, nz)
                if u < U and UNITS[u][0] in NORMED:
                    p = ROWS[UNITS[u][1]]
                    act.wait_ge(proj, u + 1)
                    if ns >= 2:
                        act.wait_ge(ms_ready, ns - 1)
                    nc.scalar.activation(sq[0:p, ns % 2, :], (z[u % 3][0:p, :] if p > NS else zs[:]), ACT.Square).then_inc(squared, 1)
                    ns += 1
                v = u - 2
                if v >= 0 and is_turned(UNITS[v]):
                    k, i = UNITS[v]
                    p = ROWS[i]
                    act.wait_ge(turned, nt + 1)
                    bank = tp[nt % 2]
                    if k == "kw":
                        ins = nc.scalar.copy(kiT[:, 128 * i:128 * i + 128] if i < NT else kiTs[:], bank[:, 0:p])
                    elif k == "qi" and i == NT:
                        act.wait_ge(blk0, 1)
                        ins = nc.scalar.copy(qblk[:].rearrange("d (b c) -> d b c", c=72)[:, :, 0:H],
                                             bank[0:DH, 0:NS * H].rearrange("d (h b) -> d b h", h=H))
                        ins.then_inc(blk0, 1)
                    else:
                        dst = (qiT if k == "qi" else s.T[k])[:, :, 128 * i:128 * i + p]
                        ins = nc.scalar.copy(dst, bank[:, 0:NB * p].rearrange("f (j t) -> f j t", j=NB))
                    if not (k == "qi" and i == NT):
                        ins.then_inc(turn_out, 1)
                    else:
                        act.wait_ge(blk0, 2)
                        act.sem_inc(turn_out, 1)
                    nt += 1
                for t, h in extras.get(u, ()):
                    act.wait_ge(x_ready, nx + 1)
                    if nx >= 2:
                        act.wait_ge(relu_used, nx - 1)
                    n = 128 * (t + 1)
                    nc.scalar.activation(relu[:, nx % 2, 0:n], xs[nx % 2][:, 0:n], ACT.Relu, scale=DH ** -0.5).then_inc(relu_done, 1)
                    nx += 1
                if u == SAMPLE_AT:
                    for b in range(NS):
                        act.wait_ge(x_ready, nx + 1)
                        if b >= 2:
                            act.wait_ge(ss_ready, b - 1)
                        nc.scalar.copy(kTi[:, b % 2, :], xs[nx % 2][0:DH, :]).then_inc(kTi_ready, 1)
                        nx += 1
                    act.wait_ge(ss_ready, NS)
                    nc.scalar.activation(relu_s[:, 0:PAST], ss[:], ACT.Relu, scale=DH ** -0.5).then_inc(samp, 1)
                    act.wait_ge(x_ready, nx + 1)
                    nc.scalar.activation(relu_s[:, PAST:PAST + 1], xs[nx % 2][0:64, 0:1], ACT.Relu, scale=DH ** -0.5).then_inc(samp, 1)

        @block.gpsimd
        def _(pool):
            n = 0
            nc.gpsimd.memset(qblk[:], 0.0).then_inc(blk0, 1)
            nc.gpsimd.memset(zero, 0.0).then_inc(zeroed, 1)
            pool.wait_ge(zeroed, 1)
            rest = s.eout[NE * CAP:NBLK * CAP, :].rearrange("(p r) (q c) -> p (r q) c", p=128, c=256)
            pool.dma_start(rest, bcast(zero, rest.shape[1], 1)).then_inc(rest_zeroed, 16)
            for u, (k, i) in enumerate(UNITS):
                if k in NORMED:
                    p = ROWS[i]
                    pool.wait_ge(ms_ready, n + 1)
                    if n >= 2:
                        pool.wait_ge(z_free, u - 1)
                    nc.gpsimd.tensor_scalar(rs[0:p, n % 2, :], ms[0:p, n % 2, :], 1.0 / DH, EPS, ALU.mult, ALU.add).then_inc(pool_chain, 1)
                    pool.wait_ge(pool_chain, n + 1)
                    nc.gpsimd.tensor_tensor(rs[0:p, n % 2, :], rs[0:p, n % 2, :], s.c[0:p, C_MH:C_MH + H], ALU.pow).then_inc(rs_ready, 1)
                    n += 1
            pool.wait_ge(rest_zeroed, 16)

        @block.vector
        def _(dve):
            link = Chain(dve, chain)
            nm = nr = nx = 0
            nturn = 0
            heads = lambda ap: ap.rearrange("p (h d) -> p h d", h=H)

            def sums(u):
                nonlocal nm
                k, i = UNITS[u]
                if k in NORMED:
                    p = ROWS[i]
                    dve.wait_ge(squared, nm + 1)
                    if nm >= 2:
                        dve.wait_ge(rs_ready, nm - 1)
                    nc.vector.tensor_reduce(ms[0:p, nm % 2, :], heads(sq[0:p, nm % 2, :]), AX.X, ALU.add).then_inc(ms_ready, 1)
                    nm += 1

            def finish(u):
                nonlocal nr
                k, i = UNITS[u]
                p = ROWS[i]
                bank = z[u % 3]
                dve.wait_ge(proj, u + 1)
                if i == NT and k != "kw":
                    bank = zs
                    dve.wait_ge(zs_ready, NB * sum(j == NT and q != "kw" for q, j in UNITS[:u + 1]))
                if u >= 4:
                    dve.wait_ge(turned, turned_before(u - 3))
                    if y_of[u - 4]:
                        dve.wait_ge(stored[u % 4], 16 * y_of[u - 4])
                if k[0] == "v":
                    nc.vector.tensor_copy(s.v[k][:, i, :] if i < NT else s.row[k][:], bank[0:p, :]).then_inc(z_free, 1)
                    dve.wait_ge(z_free, u + 1)
                    dve.sem_inc(y_ready, 1)
                    return
                if k == "kw":
                    n, hh = DH, 1
                    src = bank[0:p, 0:DH].unsqueeze(1)
                    cos, sin = s.rope[0:p, 0, i, :], s.rope[0:p, 1, i, :]
                elif k == "qi":
                    n, hh = W, H
                    src = heads(bank[0:p, :])
                    cos, sin = s.rope[0:p, 0, i, :], s.rope[0:p, 1, i, :]
                else:
                    n, hh = W, H
                    g = ("ks", "qs", "kd", "qd").index(k)
                    cos, sin = s.rg[0:p, g, 0, i, :], s.rg[0:p, g, 1, i, :]
                    dve.wait_ge(rs_ready, nr + 1)
                    nc.vector.tensor_tensor(heads(t0[0:p, :]), heads(bank[0:p, :]), bcast(rs[0:p, nr % 2, :], DH, 2), ALU.mult).then_inc(z_free, 1)
                    dve.wait_ge(z_free, u + 1)
                    nr += 1
                    src = heads(t0[0:p, :])
                va = ta[0:p, 0:n].rearrange("p (h d) -> p h d", h=hh)
                vb = tb[0:p, 0:n].rearrange("p (h d) -> p h d", h=hh)
                vy = y[0:p, u % 4, 0:n].rearrange("p (h d) -> p h d", h=hh)
                nc.vector.tensor_tensor(va, src, bcast(cos, hh, 1), ALU.mult)
                if k == "kw":
                    nc.vector.tensor_scalar(wi[0:p, i, :], bank[0:p, DH:DH + H], float(np.float32(H ** -0.5)), None, ALU.mult).then_inc(wi_ready, 1)
                last = nc.vector.tensor_tensor(vb, src, bcast(sin, hh, 1), ALU.mult)
                if k in NORMED:
                    link(last)
                else:
                    last.then_inc(z_free, 1)
                    dve.wait_ge(z_free, u + 1)
                hd = DH // 2
                link(nc.vector.tensor_tensor(vy[:, :, 0:hd], va[:, :, 0:hd], vb[:, :, hd:DH], ALU.subtract))
                link(nc.vector.tensor_tensor(vy[:, :, hd:DH], va[:, :, hd:DH], vb[:, :, 0:hd], ALU.add))
                if k == "kw":
                    link(nc.vector.tensor_copy(y[0:p, u % 4, DH:2 * DH], y[0:p, u % 4, 0:DH]))
                if i == NT and k in NORMED:
                    link(nc.vector.tensor_copy(s.row[k][:], y[0:NS, u % 4, :]))
                dve.sem_inc(y_ready, 1)

            rounds = []

            def take8(buf):
                link(nc.vector.max(m8[0:buf.shape[0], :], buf))
                link(nc.vector.match_replace(buf, m8[0:buf.shape[0], :], buf, TAKEN))

            for u in range(U + 1):
                if u < U:
                    sums(u)
                if u >= 1:
                    finish(u - 1)
                for t, h in extras.get(u, ()):
                    n = 128 * (t + 1)
                    if nx == 0:
                        dve.wait_ge(wi_ready, TILES)
                    dve.wait_ge(relu_done, nx + 1)
                    acc = score[t - 1]
                    ins = nc.vector.scalar_tensor_tensor(acc[:], relu[:, nx % 2, 0:n], wi[:, t, h:h + 1],
                                                         s.c[:, C_E - n:C_E] if h == 0 else acc[:], ALU.mult, ALU.add)
                    ins.then_inc(relu_used, 1)
                    dve.wait_ge(relu_used, nx + 1)
                    dve.sem_inc(x_free, 1)
                    nx += 1
                    if h == H - 1:
                        rounds += [score[t - 1][:]] * TK_ROUNDS
                if u == SAMPLE_AT:
                    nx += NS
                    dve.wait_ge(x_ready, nx + 1)
                    dve.wait_ge(samp, 2)
                    link(nc.vector.tensor_tensor(wtmp[:], xs[nx % 2][0:64, 8:16], s.c[0:64, C_HM:C_IOTA], ALU.mult))
                    link(nc.vector.tensor_reduce(wcol[:], wtmp[:], AX.X, ALU.add))
                    link(nc.vector.tensor_scalar(ew[:], s.c[0:64, C_ET:C_HM], wcol[:], None, ALU.mult))
                    dve.sem_inc(samp, 1)
                    dve.sem_inc(x_free, 1)
                    dve.wait_ge(x_ready, nx + 2)
                    link(nc.vector.tensor_copy(score_s[:, 0:PAST], xs[(nx + 1) % 2][0:NS, :]))
                    dve.wait_ge(x_ready, nx + 3)
                    link(nc.vector.tensor_copy(score_s[:, PAST:PAST + 1], xs[nx % 2][0:NS, 0:1]))
                    rounds += [score_s[:]] * TK_ROUNDS
                for _ in range(3):
                    if rounds:
                        take8(rounds.pop(0))
            while rounds:
                take8(rounds.pop(0))
            for t in range(1, NT):
                nc.vector.tensor_scalar(score[t - 1][:], score[t - 1][:], TAKEN, MASKED, ALU.not_equal, ALU.mult)
            nc.vector.tensor_scalar(score_s[:], score_s[:], TAKEN, MASKED, ALU.not_equal, ALU.mult)


KQV = dict(d=("qd", "kd", "vd"), s=("qs", "ks", "vs"))
A_UNITS = [(t, kind, h) for t in range(NT) for kind in "ds" for h in range(H)]
JOBS = [(t, kind, h if kind == "s" else h // 2, n) for n, (t, kind, h) in enumerate(A_UNITS) if kind == "s" or h % 2]
JOB_OF = {n: next(q for q, j in enumerate(JOBS) if j[3] >= n) for n in range(len(A_UNITS))}
LAG = 3


def attend_prompt(nc, io, s):
    UN, JN = len(A_UNITS), len(JOBS)
    with ExitStack() as ctx:
        sb = lambda n, sh, dt=F32: ctx.enter_context(nc.sbuf_tensor("a_" + n, sh, dt))
        ps = lambda n, sh: ctx.enter_context(nc.psum_tensor("a_" + n, sh, F32))
        sem = lambda n: ctx.enter_context(nc.semaphore("a_" + n))
        lams, lprod, lsum, lexp = sb("lams", [128, 4, DH]), sb("lprod", [128, 2, DH]), sb("lsum", [128, 2]), sb("lexp", [128, 2])
        masked, prob, mix, pT = sb("masked", [128, 3, W]), sb("prob", [128, 4, W]), sb("mix", [128, 2, W]), sb("pT", [128, 2, W])
        scaled = sb("scaled", [128, W])
        mx, nb, sums, inv = (sb(n, [128, UN]) for n in ("mx", "nb", "sums", "inv"))
        osq, on = sb("osq", [128, W]), sb("on", [128, 2, W])
        oms, ors = sb("oms", [128, 4]), sb("ors", [128, 4])
        S = [ps(f"S{n}", [128, W]) for n in range(3)]
        T = [ps(f"T{n}", [128, W]) for n in range(2)]
        O = [ps(f"O{n}", [128, W]) for n in range(2)]
        OT = ps("OT", [128, W])
        (lams_in, lam_sum, lam_exp, chain, scored, max_ready, p_ready, combined, turned, copied, pv_done, o_sq, o_ms, o_rs,
         pool_chain, o_ready, o_turned, o_done) = map(sem, (
             "lams_in lam_sum lam_exp chain scored max_ready p_ready combined turned copied pv_done o_sq o_ms o_rs "
             "pool_chain o_ready o_turned o_done").split())
        block = ctx.enter_context(nc.Block())
        pairs_before = lambda n: sum(k == "d" and h % 2 for _, k, h in A_UNITS[:n])
        last_job = {g: max(q for q, j in enumerate(JOBS) if 2 * j[0] + (j[1] == "s") == g) for g in range(2 * NT)}

        @block.sync
        def _(sp):
            for n, l in enumerate(("lam_q1", "lam_q2", "lam_k1", "lam_k2")):
                sp.dma_start(lams[:, n, :], io[l].to_broadcast([128, DH])).then_inc(lams_in, 16)
            sp.dma_start(s.gsub[:], io["g_subln"].rearrange("a p -> p a"), allow_slow_non_contiguous=True).then_inc(lams_in, 16)

        @block.tensor
        def _(pe):
            def turn(q):
                t, kind, h, n = JOBS[q]
                if kind == "d":
                    pe.wait_ge(combined, pairs_before(n + 1))
                    src = mix[:, (pairs_before(n + 1) - 1) % 2, :]
                else:
                    pe.wait_ge(p_ready, n + 1)
                    src = prob[:, n % 4, :]
                if q >= 2:
                    pe.wait_ge(copied, q - 1)
                for b in range(t + 1):
                    last = nc.tensor.transpose(T[q % 2][:, 128 * b:128 * b + 128], src[:, 128 * b:128 * b + 128], s.ident[:])
                last.then_inc(turned, 1)

            def values(q):
                t, kind, h, n = JOBS[q]
                g = 2 * t + (kind == "s")
                pe.wait_ge(copied, q + 1)
                if h == 0 and g >= 2:
                    pe.wait_ge(o_ready, g - 1)
                w = W // (4 if kind == "d" else 8)
                for b in range(t + 1):
                    last = nc.tensor.matmul(O[g % 2][:, w * h:w * h + w], pT[:, q % 2, 128 * b:128 * b + 128],
                                            s.v[KQV[kind][2]][:, b, w * h:w * h + w], start=b == 0, stop=b == t)
                last.then_inc(pv_done, 1)

            def turn_output(g):
                pe.wait_ge(o_ready, g + 1)
                if g:
                    pe.wait_ge(o_done, g)
                for j in range(NB):
                    last = nc.tensor.transpose(OT[:, 128 * j:128 * j + 128], on[:, g % 2, 128 * j:128 * j + 128], s.ident[:])
                last.then_inc(o_turned, 1)

            q = 0
            late = {}
            for n in range(UN + LAG + 1):
                if n < UN:
                    t, kind, h = A_UNITS[n]
                    kq, kk, _ = KQV[kind]
                    r = 64 * (h % 2)
                    if n >= 3:
                        pe.wait_ge(max_ready, n - 2)
                    nc.tensor.matmul(S[n % 3][:, 0:128 * (t + 1)], s.T[kq][r:r + 64, h // 2, 128 * t:128 * t + 128],
                                     s.T[kk][r:r + 64, h // 2, 0:128 * (t + 1)], start=True, stop=True).then_inc(scored, 1)
                while q < JN and JOBS[q][3] <= n - LAG:
                    turn(q)
                    if q:
                        values(q - 1)
                    q += 1
                    for g in [g for g in range(2 * NT) if last_job[g] == q - 4]:
                        turn_output(g)
            values(JN - 1)
            for g in [g for g in range(2 * NT) if last_job[g] > JN - 4]:
                turn_output(g)

        @block.scalar
        def _(act):
            act.wait_ge(lam_sum, 1)
            nc.scalar.activation(lexp[:], lsum[:], ACT.Exp).then_inc(lam_exp, 1)
            q = 0

            def copy(q):
                t = JOBS[q][0]
                act.wait_ge(turned, q + 1)
                if q >= 2:
                    act.wait_ge(pv_done, q - 1)
                nc.scalar.copy(pT[:, q % 2, 0:128 * (t + 1)], T[q % 2][:, 0:128 * (t + 1)]).then_inc(copied, 1)

            def square(g):
                act.wait_ge(pv_done, last_job[g] + 1)
                if g >= 2:
                    act.wait_ge(o_ms, g // 2)
                nc.scalar.activation(osq[:], O[g % 2][:], ACT.Square).then_inc(o_sq, 1)

            for n in range(UN + LAG + 1):
                if n < UN:
                    t, kind, h = A_UNITS[n]
                    act.wait_ge(max_ready, n + 1)
                    if n >= 4:
                        if A_UNITS[n - 4][1] == "d":
                            act.wait_ge(combined, pairs_before(n - 3) + (A_UNITS[n - 4][2] % 2 == 0))
                        else:
                            act.wait_ge(turned, JOB_OF[n - 4] + 1)
                    w = 128 * (t + 1)
                    nc.scalar.activation(prob[:, n % 4, 0:w], masked[:, n % 3, 0:w], ACT.Exp, bias=nb[:, n:n + 1], scale=DH ** -0.5,
                                         accum_out=sums[:, n:n + 1]).then_inc(p_ready, 1)
                while q < JN and JOBS[q][3] <= n - LAG:
                    copy(q)
                    q += 1
                    for g in [g for g in range(0, 2 * NT, 2) if last_job[g] == q - 3]:
                        square(g)

        @block.gpsimd
        def _(pool):
            for t in range(NT):
                pool.wait_ge(o_ms, t + 1)
                if t:
                    pool.wait_ge(o_ready, 2 * t - 1)
                nc.gpsimd.tensor_scalar(ors[:], oms[:], 1.0 / (2 * DH), EPS, ALU.mult, ALU.add).then_inc(pool_chain, 1)
                pool.wait_ge(pool_chain, t + 1)
                nc.gpsimd.tensor_tensor(ors[:], ors[:], s.c[:, C_MH:C_MH + 4], ALU.pow).then_inc(o_rs, 1)

        @block.vector
        def _(dve):
            link = Chain(dve, chain)
            dve.wait_ge(lams_in, 80)
            link(nc.vector.tensor_tensor(lprod[:], lams[:, 0:2, :], lams[:, 2:4, :], ALU.mult))
            nc.vector.tensor_reduce(lsum[:], lprod[:], AX.X, ALU.add).then_inc(lam_sum, 1)
            dve.wait_ge(lam_exp, 1)
            link(nc.vector.tensor_tensor(s.neglam[:], lexp[:, 1:2], lexp[:, 0:1], ALU.subtract))
            link(nc.vector.tensor_scalar(s.neglam[:], s.neglam[:], -LAM_INIT, None, ALU.add))
            link(nc.vector.tensor_scalar(s.gsub[:], s.gsub[:], 1.0 - LAM_INIT, None, ALU.mult))

            def combine(n):
                t, w = A_UNITS[n][0], 128 * (A_UNITS[n][0] + 1)
                m = pairs_before(n + 1)
                dve.wait_ge(p_ready, n + 1)
                if m > 2:
                    q2 = [q for q, j in enumerate(JOBS) if j[1] == "d"][m - 3]
                    dve.wait_ge(turned, q2 + 1)
                link(nc.vector.reciprocal(inv[:, n - 1:n + 1], sums[:, n - 1:n + 1]))
                link(nc.vector.tensor_scalar(inv[:, n:n + 1], inv[:, n:n + 1], s.neglam[:], None, ALU.mult))
                link(nc.vector.tensor_scalar(scaled[:, 0:w], prob[:, n % 4, 0:w], inv[:, n:n + 1], None, ALU.mult))
                nc.vector.scalar_tensor_tensor(mix[:, (m - 1) % 2, 0:w], prob[:, (n - 1) % 4, 0:w], inv[:, n - 1:n], scaled[:, 0:w],
                                               ALU.mult, ALU.add).then_inc(combined, 1)

            def output(g):
                t, d = g // 2, g % 2 == 0
                if d:
                    dve.wait_ge(o_sq, t + 1)
                    nc.vector.tensor_reduce(oms[:], osq[:].rearrange("p (h e) -> p h e", h=4), AX.X, ALU.add).then_inc(o_ms, 1)
                    dve.wait_ge(o_rs, t + 1)
                    scale, w = ors[:], 2 * DH
                else:
                    dve.wait_ge(pv_done, last_job[g] + 1)
                    n = 16 * t + 8
                    link(nc.vector.reciprocal(inv[:, n:n + H], sums[:, n:n + H]))
                    scale, w = inv[:, n:n + H], DH
                if g >= 2:
                    dve.wait_ge(o_turned, g - 1)
                nc.vector.tensor_tensor(on[:, g % 2, :].rearrange("p (h e) -> p h e", e=w), O[g % 2][:].rearrange("p (h e) -> p h e", e=w),
                                        bcast(scale, w, 2), ALU.mult).then_inc(o_ready, 1)

            def output_turned(g):
                t, d = g // 2, g % 2 == 0
                dve.wait_ge(o_turned, g + 1)
                dst = s.oT["ds"[g % 2]][:, :, 128 * t:128 * t + 128]
                src = OT[:].rearrange("p (j q) -> p j q", j=NB)
                if d:
                    nc.vector.tensor_scalar(dst, src, s.gsub[:], None, ALU.mult).then_inc(o_done, 1)
                else:
                    nc.vector.tensor_copy(dst, src).then_inc(o_done, 1)

            q = 0
            for n in range(UN + LAG + 1):
                if n < UN:
                    t, kind, h = A_UNITS[n]
                    w = 128 * (t + 1)
                    dve.wait_ge(scored, n + 1)
                    if n >= 3:
                        dve.wait_ge(p_ready, n - 2)
                    mask = s.sel[t][:] if kind == "s" and t else s.c[:, C_E - w:C_E]
                    link(nc.vector.tensor_tensor_reduce(out=masked[:, n % 3, 0:w], in0=S[n % 3][:, 0:w], in1=mask, scale=1.0, scalar=-3.4e38,
                                                        op0=ALU.add, op1=ALU.max, accum_out=mx[:, n:n + 1]))
                    nc.vector.tensor_scalar(nb[:, n:n + 1], mx[:, n:n + 1], -DH ** -0.5, None, ALU.mult).then_inc(max_ready, 1)
                if n >= 1 and n - 1 < UN and A_UNITS[n - 1][1] == "d" and A_UNITS[n - 1][2] % 2:
                    combine(n - 1)
                while q < JN and JOBS[q][3] <= n - LAG:
                    q += 1
                    for g in [g for g in range(2 * NT) if last_job[g] == q - 3]:
                        output(g)
                    for g in [g for g in range(2 * NT) if last_job[g] == q - 5]:
                        output_turned(g)
            for g in [g for g in range(2 * NT) if last_job[g] > JN - 3]:
                output(g)
            for g in [g for g in range(2 * NT) if last_job[g] > JN - 5]:
                output_turned(g)


PASSES = [(k, c) for c in range(2) for k in range(2)]
SLOTS_A = len(PASSES) * NT
RING = 3
PRODUCTS = [(q, i, r) for q in range(4) for i, r in [(i, r) for i in range(NT) for r in "gy"] + [(NT, "g")]]
PRODUCTS += [(q, NT, "y") for q in range(4)]
PLACES = 8
CACHE = dict(kd="cache_diff_k", ks="cache_dsa_k", vd="cache_diff_v", vs="cache_dsa_v")
KEYS_AT = {sl: ("kd", [sl]) for sl in range(8)} | {8 + b: ("ks", [b]) for b in range(8)}
VALUES_AT = {10: ("vd", [0, 1]), 11: ("vd", [2]), 12: ("vd", [3]), 13: ("vd", [4, 5]), 14: ("vd", [6]), 15: ("vd", [7]),
             18: ("vs", [0, 1, 2, 3]), 19: ("vs", [4, 5, 6, 7])}
SOFTMAX_AT = {8: "d", 16: "s"}
PAGES = [(c, b, n) for sl in range(SLOTS_A + NT) for c, bs in [at[sl] for at in (KEYS_AT, VALUES_AT) if sl in at]
         for b in bs for n in range(NPAGE)]
K_PAGES, V_PAGES = ([m for m, pg in enumerate(PAGES) if pg[0][0] == x] for x in "kv")


def merge(nc, io, s):
    R = NS * H
    with ExitStack() as ctx:
        sb = lambda n, sh, dt=F32: ctx.enter_context(nc.sbuf_tensor("g_" + n, sh, dt))
        ps = lambda n, sh: ctx.enter_context(nc.psum_tensor("g_" + n, sh, F32))
        sem = lambda n: ctx.enter_context(nc.semaphore("g_" + n))
        wo = [sb("wo" + k, [128, NB, D]) for k in "ds"]
        merged = sb("merged", [128, NT, D])
        merged_s = sb("merged_s", [NS, D])
        mT = sb("mT", [128, KD, 128])
        gate = sb("gate", [128, 2, W])
        gate_s = sb("gate_s", [NS, 4, W])
        branch = sb("branch", [128, W])
        ring = [ps(f"ring{n}", [128, W]) for n in range(RING)]
        B = [ps(f"B{n}", [128, W]) for n in range(2)]
        page = sb("page", [128, PLACES, W])
        ptab = sb("ptab", [1, NS * NPAGE], I32)
        prod = sb("prod", [128, W])
        sT = {k: sb("sT" + k, [128, NPAGE, R]) for k in "ds"}
        nk, nkh, snew = sb("nk", [NS, 2, H]), sb("nkh", [R, 2, H]), sb("snew", [R, 2])
        sc, pr, selb = sb("sc", [R, PAST + 1]), sb("pr", [R, PAST + 1]), sb("selb", [R, PAST + 1])
        aT = dict(d=sb("aTd", [128, NPAGE, R // 2]), s=sb("aTs", [128, NPAGE, R]))
        aN = dict(d=sb("aNd", [NS, R // 2]), s=sb("aNs", [NS, R]))
        dg = sb("dg", [R, R])
        mx, nb, sm, cf = (sb(n, [R, 2]) for n in ("mx", "nb", "sm", "cf"))
        od, oq, orr, orx = (sb(n, [128, NB * NS]) for n in ("od", "oq", "orr", "orx"))
        mh = sb("mh", [128, NB * NS])
        QB, P, O = ps("QB", [128, W]), ps("P", [128, W]), ps("O", [128, W])
        (wo_in, made, g_exp, y_read, chain, merged_ready, turned, mt_out, summed, x_done, ptab_in, sel_up, sel_read, nk_ready, nk_up,
         nk_read, qb_ready, k_used, sT_ready, sc_ready, max_ready, p_ready, weights, p_turned, a_ready, v_used, o_ready, od_read,
         oq_ready, o_sum, orr_ready, o_rs, oT_ready, gates_s, ms_ready, mh_ready) = map(sem, (
             "wo_in made g_exp y_read chain merged_ready turned mt_out summed x_done ptab_in sel_up sel_read nk_ready nk_up "
             "nk_read qb_ready k_used sT_ready sc_ready max_ready p_ready weights p_turned a_ready v_used o_ready od_read "
             "oq_ready o_sum orr_ready o_rs oT_ready gates_s ms_ready mh_ready").split())
        w_more = [sem(f"w_more{n}") for n in range(2)]
        page_in = [sem(f"page_in{n}") for n in range(PLACES)]
        block = ctx.enter_context(nc.Block())
        made_after = lambda q: 9 * (q + 1)
        exps = lambda m: sum(r == "g" for _, _, r in PRODUCTS[:m])
        reads = lambda m: sum(r == "y" for _, _, r in PRODUCTS[:m])
        m_of = {pr_: m for m, pr_ in enumerate(PRODUCTS)}

        @block.sync
        def _(sp):
            sp.dma_start(ptab[:], io["page_table"].rearrange("b n -> (b n)").unsqueeze(0)).then_inc(ptab_in, 16)
            sp.wait_ge(ptab_in, 16)
            ids = [sp.value_load(ptab[0:1, x:x + 1], min_val=0, max_val=s.pool - 1) for x in range(NS * NPAGE)]
            for m, (c, b, n) in enumerate(PAGES):
                if m >= PLACES:
                    f = m - PLACES
                    if PAGES[f][0][0] == "k":
                        sp.wait_ge(k_used, K_PAGES.index(f) + 1)
                    else:
                        sp.wait_ge(v_used, V_PAGES.index(f) + 1)
                src = io[CACHE[c]][0, ids[NPAGE * b + n]]
                src = src.rearrange("p h c d -> p (h c d)") if c == "kd" else src.rearrange("p h d -> p (h d)")
                sp.dma_start(page[:, m % PLACES, :], src).then_inc(page_in[m % PLACES], 16)

        @block.gpsimd
        def _(pool):
            for k, name in enumerate(("w_o_diff", "w_o_dsa")):
                pool.dma_start(wo[k][:], io[name][0].rearrange("(j p) c -> p j c", p=128)).then_inc(wo_in, 16)
            nc.gpsimd.memset(mh[:], -0.5).then_inc(mh_ready, 1)
            for q in range(2):
                pool.wait_ge(made, made_after(q))
                off = OFF[("gd", "gs")[q]] + W
                pool.dma_start(s.w[:, q], io["w_in"][0][:, off:off + W].rearrange("(j p) c -> p j c", p=128)).then_inc(w_more[q], 16)
            for h in range(2):
                pool.wait_ge(made, made_after(2 + h))
                pool.dma_start(s.w[:, h], io["w_out"][0][:, W * h:W * h + W].rearrange("(j p) c -> p j c", p=128)).then_inc(w_more[h], 16)
            pool.wait_ge(mh_ready, 1)
            pool.wait_ge(orr_ready, 1)
            nc.gpsimd.tensor_tensor(orx[:], orr[:], mh[:], ALU.pow).then_inc(o_rs, 1)

        @block.tensor
        def _(pe):
            nbank = 0

            def product(m):
                q, i, r = PRODUCTS[m]
                k, c = PASSES[q][0], PASSES[q][1]
                f = m - RING
                if f >= 0:
                    if PRODUCTS[f][2] == "g":
                        pe.wait_ge(g_exp, exps(f + 1))
                    else:
                        pe.wait_ge(y_read, reads(f + 1))
                bank = ring[m % RING]
                if r == "g":
                    if i == 0:
                        pe.wait_ge(*((s.w_in[q], 80) if q < 2 else (w_more[q - 2], 16)))
                    x, w, steps = s.xT, s.w[:, q % 2], KD
                else:
                    if m < 2 or m == 10:
                        pe.wait_ge(wo_in, 32)
                    x, w, steps = s.oT["ds"[k]], wo[k][:, :, W * c:W * c + W], NB
                if i == NT:
                    last = small_product(nc, bank, x[:, :, SEQ:TOK], w, steps)
                else:
                    for j in range(steps):
                        last = nc.tensor.matmul(bank[:], x[:, j, 128 * i:128 * i + 128], w[:, j, :], start=j == 0, stop=j == steps - 1)
                last.then_inc(made, 1)

            def bank_free():
                m = nbank - 2
                if m >= 0:
                    i, r = m // 4, m % 4
                    if r < 2:
                        pe.wait_ge(mt_out, 2 * i + r + 1)
                    else:
                        pe.wait_ge(x_done, 2 * i + r - 1)

            def project_out(i):
                nonlocal nbank
                p = ROWS[i]
                src = merged[:, i] if i < NT else merged_s[:]
                if i < NT:
                    pe.wait_ge(merged_ready, NT + i + 1)
                else:
                    pe.wait_ge(ms_ready, 1)
                for h in range(2):
                    bank_free()
                    for j in range(4):
                        last = nc.tensor.transpose(B[nbank % 2][:, 128 * j:128 * j + p], src[:, 128 * (4 * h + j):128 * (4 * h + j) + 128],
                                                   s.ident[0:p, 0:p])
                    last.then_inc(turned, 1)
                    nbank += 1
                for h in range(2):
                    bank_free()
                    pe.wait_ge(mt_out, 2 * i + 2)
                    if i == 0:
                        pe.wait_ge(w_more[h], 32)
                    if i == NT:
                        last = small_product(nc, B[nbank % 2], mT[:], s.w[:, h], KD)
                    else:
                        for j in range(KD):
                            last = nc.tensor.matmul(B[nbank % 2][:], mT[:, j, :], s.w[:, h, j, :], start=j == 0, stop=j == KD - 1)
                    last.then_inc(summed, 1)
                    nbank += 1

            def queries(n, c, b):
                if n:
                    pe.wait_ge(k_used, NPAGE * n)
                nc.tensor.matmul(QB[:], s.ident[0:NS, b:b + 1].to_broadcast([NS, 128]), s.row["q" + c[1]][:],
                                 start=True, stop=True).then_inc(qb_ready, 1)

            def values(c, b):
                k, w = c[1], 1 if c[1] == "d" else 2
                if b == 0:
                    pe.wait_ge(a_ready, 1 + "ds".index(k))
                    if k == "s":
                        pe.wait_ge(orr_ready, 1)
                for n in range(NPAGE):
                    m = PAGES.index((c, b, n))
                    pe.wait_ge(page_in[m % PLACES], 16 * (m // PLACES + 1))
                    for j in range(NB):
                        col = w * (NS * j + b)
                        last = nc.tensor.matmul(O[:, col:col + w], page[:, m % PLACES, 128 * j:128 * j + 128],
                                                aT[k][:, n, w * (4 * b + j):w * (4 * b + j) + w], start=b == n == j == 0, stop=False,
                                                skip_group_check=True)
                    last.then_inc(v_used, 1)
                if b == NS - 1:
                    for j in range(NB):
                        rhs = aN[k][:].rearrange("q (b j w) -> q b j w", b=NS, w=w)[:, :, j, :]
                        last = nc.tensor.matmul(O[:, w * NS * j:w * NS * (j + 1)].rearrange("p (b w) -> p b w", w=w),
                                                s.row["v" + k][:, 128 * j:128 * j + 128], rhs, start=False, stop=j == NB - 1,
                                                skip_group_check=True)
                    last.then_inc(o_ready, 1)

            nc.tensor.matmul(P[0:R, :], s.c[0:NS, C_E:C_ET], s.sel_s[:, 0:PAST], start=True, stop=True)
            nc.tensor.matmul(O[0:R, 0:1], s.c[0:NS, C_E:C_ET], s.sel_s[:, PAST:PAST + 1], start=True, stop=True).then_inc(sel_up, 1)
            nq = m = 0
            for sl in range(SLOTS_A + NT):
                if sl < SLOTS_A:
                    product(m)
                    product(m + 1)
                    m += 2
                    if sl % NT == NT - 1:
                        product(m)
                        m += 1
                else:
                    project_out(sl - SLOTS_A)
                if sl in KEYS_AT:
                    for b in KEYS_AT[sl][1]:
                        queries(nq, KEYS_AT[sl][0], b)
                        nq += 1
                if sl == 1:
                    pe.wait_ge(sel_read, 1)
                    pe.wait_ge(nk_ready, 1)
                    nc.tensor.matmul(O[0:R, 16:32], s.c[0:NS, C_E:C_ET], nk[:].rearrange("b c h -> b (c h)"), start=True, stop=True).then_inc(nk_up, 1)
                if sl == SLOTS_A:
                    pe.wait_ge(oq_ready, 1)
                    nc.tensor.matmul(O[:, 256:256 + NB * NS], s.c[:, C_ONE:C_CM], oq[:], start=True, stop=True).then_inc(o_sum, 1)
                if sl in SOFTMAX_AT:
                    k = SOFTMAX_AT[sl]
                    pe.wait_ge(sT_ready, 1 + "ds".index(k))
                    for n in range(NPAGE):
                        last = nc.tensor.transpose(P[0:R, 128 * n:128 * n + 128], sT[k][:, n, :], s.ident[:])
                    last.then_inc(sc_ready, 1)
                if sl - 1 in SOFTMAX_AT:
                    i = "ds".index(SOFTMAX_AT[sl - 1])
                    pe.wait_ge(weights, 2 * i + 2)
                    for n in range(NPAGE):
                        nc.tensor.transpose(P[:, 64 * n:64 * n + R], pr[:, 128 * n:128 * n + 128], s.ident[0:R, 0:R])
                    nc.tensor.matmul(P[0:NS, 256:256 + R], s.c[0:R, C_ET:C_HM], dg[:], start=True, stop=True).then_inc(p_turned, 1)
                if sl in VALUES_AT:
                    if sl == 10:
                        pe.wait_ge(nk_read, 1)
                    for b in VALUES_AT[sl][1]:
                        values(VALUES_AT[sl][0], b)
            pe.wait_ge(oT_ready, 3)
            while m < len(PRODUCTS):
                product(m)
                m += 1
            project_out(NT)

        @block.scalar
        def _(act):
            def exp(m):
                q, i, r = PRODUCTS[m]
                act.wait_ge(made, m + 1)
                bank = ring[m % RING]
                if i < NT:
                    n = exps(m) - q
                    if n >= 2:
                        act.wait_ge(y_read, n - 1)
                    nc.scalar.activation(gate[:, n % 2, :], bank[:], ACT.Sigmoid).then_inc(g_exp, 1)
                else:
                    for g in range(NB):
                        ins = nc.scalar.activation(gate_s[:, q, 128 * g:128 * g + 128], bank[32 * g:32 * g + NS, 0:128], ACT.Sigmoid)
                    ins.then_inc(g_exp, 1)

            def copies(i):
                p = ROWS[i]
                for h in range(2):
                    act.wait_ge(turned, 2 * i + h + 1)
                    if i:
                        act.wait_ge(summed, 2 * i)
                    nc.scalar.copy(mT[:, 4 * h:4 * h + 4, 0:p], B[h][:].rearrange("p (j q) -> p j q", j=4)[:, :, 0:p]).then_inc(mt_out, 1)

            for sl in range(SLOTS_A + NT):
                if sl - 1 in SOFTMAX_AT:
                    i = "ds".index(SOFTMAX_AT[sl - 1])
                    act.wait_ge(max_ready, i + 1)
                    nc.scalar.activation(pr[:], sc[:], ACT.Exp, bias=nb[:, i:i + 1], scale=DH ** -0.5, accum_out=sm[:, i:i + 1]).then_inc(p_ready, 1)
                if sl < SLOTS_A:
                    q, i = divmod(sl, NT)
                    exp(m_of[(q, i, "g")])
                    if i == NT - 1:
                        exp(m_of[(q, NT, "g")])
                else:
                    copies(sl - SLOTS_A)
            copies(NT)

        @block.vector
        def _(dve):
            link = Chain(dve, chain)
            v = nc.vector

            def merge_tile(q, i):
                k, c = PASSES[q]
                m = m_of[(q, i, "g")]
                n = NT * q + i
                dve.wait_ge(g_exp, exps(m + 1))
                g = gate[:, n % 2, :]
                dve.wait_ge(made, m + 2)
                dst = merged[:, i, W * c:W * c + W]
                v.tensor_tensor(branch[:] if k else dst, ring[(m + 1) % RING][:], g, ALU.mult).then_inc(y_read, 1)
                if k:
                    dve.wait_ge(y_read, n + 1)
                    v.tensor_tensor(dst, dst, branch[:], ALU.add).then_inc(merged_ready, 1)

            def add_x(i):
                p = ROWS[i]
                for h in range(2):
                    dve.wait_ge(summed, 2 * i + h + 1)
                    if i < NT:
                        xs = s.x[:, i, W * h:W * h + W]
                        v.tensor_tensor(xs, B[h][:], xs, ALU.add).then_inc(x_done, 1)
                    else:
                        for g in range(NB):
                            xs = s.x[0:NS, NT, W * h + 128 * g:W * h + 128 * g + 128]
                            ins = v.tensor_tensor(xs, B[h][32 * g:32 * g + NS, 0:128], xs, ALU.add)
                        ins.then_inc(x_done, 1)

            def keys(c, b):
                k = c[1]
                dve.wait_ge(qb_ready, NS * "ds".index(k) + b + 1)
                for n in range(NPAGE):
                    m = PAGES.index((c, b, n))
                    dve.wait_ge(page_in[m % PLACES], 16 * (m // PLACES + 1))
                    v.tensor_tensor(prod[:], page[:, m % PLACES, :], QB[:], ALU.mult).then_inc(k_used, 1)
                    dve.wait_ge(k_used, K_PAGES.index(m) + 1)
                    link(v.tensor_reduce(sT[k][:, n, H * b:H * b + H], prod[:].rearrange("p (h d) -> p h d", h=H), AX.X, ALU.add))
                if b == NS - 1:
                    dve.sem_inc(sT_ready, 1)

            def largest(k):
                i = "ds".index(k)
                dve.wait_ge(sc_ready, i + 1)
                if k == "d":
                    link(v.tensor_copy(sc[:, 0:PAST], P[0:R, :]))
                    link(v.tensor_copy(sc[:, PAST:PAST + 1], snew[:, i:i + 1]))
                else:
                    link(v.tensor_tensor(sc[:, 0:PAST], P[0:R, :], selb[:, 0:PAST], ALU.add))
                    link(v.tensor_tensor(sc[:, PAST:PAST + 1], snew[:, i:i + 1], selb[:, PAST:PAST + 1], ALU.add))
                link(v.tensor_reduce(mx[:, i:i + 1], sc[:], AX.X, ALU.max))
                v.tensor_scalar(nb[:, i:i + 1], mx[:, i:i + 1], -DH ** -0.5, None, ALU.mult).then_inc(max_ready, 1)

            def weigh(k):
                i = "ds".index(k)
                dve.wait_ge(p_ready, i + 1)
                link(v.reciprocal(cf[:, i:i + 1], sm[:, i:i + 1]))
                if k == "d":
                    link(v.tensor_scalar(mx[:, 0:1], s.neglam[0:R, :], -1.0, None, ALU.add))
                    link(v.tensor_tensor(mx[:, 0:1], mx[:, 0:1], s.c[0:R, C_PAR:C_PAR + 1], ALU.mult))
                    link(v.tensor_scalar(mx[:, 0:1], mx[:, 0:1], 1.0, None, ALU.add))
                    link(v.tensor_tensor(cf[:, 0:1], cf[:, 0:1], mx[:, 0:1], ALU.mult))
                v.tensor_scalar(pr[:], pr[:], cf[:, i:i + 1], None, ALU.mult).then_inc(weights, 1)
                dve.wait_ge(weights, 2 * i + 1)
                v.tensor_scalar(dg[:], s.ident[0:R, 0:R], pr[:, PAST:PAST + 1], None, ALU.mult).then_inc(weights, 1)

            def weights_turned(k):
                dve.wait_ge(p_turned, 1 + "ds".index(k))
                if k == "d":
                    link(v.tensor_reduce(aT[k][:], P[:, 0:NPAGE * R].rearrange("p (n h c) -> p n h c", n=NPAGE, c=2), AX.X, ALU.add))
                    v.tensor_reduce(aN[k][:], P[0:NS, 256:256 + R].rearrange("p (h c) -> p h c", c=2), AX.X, ALU.add).then_inc(a_ready, 1)
                else:
                    link(v.tensor_copy(aT[k][:], P[:, 0:NPAGE * R].rearrange("p (n h) -> p n h", n=NPAGE)))
                    v.tensor_copy(aN[k][:], P[0:NS, 256:256 + R]).then_inc(a_ready, 1)

            dve.wait_ge(sel_up, 1)
            link(v.tensor_copy(selb[:, 0:PAST], P[0:R, :]))
            link(v.tensor_copy(selb[:, PAST:PAST + 1], O[0:R, 0:1]))
            dve.sem_inc(sel_read, 1)
            for i, k in enumerate("ds"):
                link(v.tensor_tensor(prod[0:NS, :], s.row["q" + k][:], s.row["k" + k][:], ALU.mult))
                link(v.tensor_reduce(nk[:, i, :], prod[0:NS, :].rearrange("p (h d) -> p h d", h=H), AX.X, ALU.add))
            dve.sem_inc(nk_ready, 1)
            jb = lambda ap: ap.rearrange("p (j b) -> p j b", j=NB)
            for sl in range(SLOTS_A + NT):
                if sl - 1 in SOFTMAX_AT:
                    largest(SOFTMAX_AT[sl - 1])
                if sl - 2 in SOFTMAX_AT:
                    weights_turned(SOFTMAX_AT[sl - 2])
                if sl < SLOTS_A:
                    merge_tile(*divmod(sl, NT))
                elif sl > SLOTS_A:
                    add_x(sl - SLOTS_A - 1)
                if sl == 2:
                    dve.wait_ge(nk_up, 1)
                    link(v.tensor_tensor(nkh[:], O[0:R, 16:32].rearrange("r (c h) -> r c h", c=2), bcast(s.c[0:R, C_HM:C_IOTA], 2, 1), ALU.mult))
                    link(v.tensor_reduce(snew[:], nkh[:], AX.X, ALU.add))
                    dve.sem_inc(nk_read, 1)
                if sl - 1 in SOFTMAX_AT:
                    weigh(SOFTMAX_AT[sl - 1])
                if sl in KEYS_AT:
                    for b in KEYS_AT[sl][1]:
                        keys(KEYS_AT[sl][0], b)
                if sl == SLOTS_A:
                    dve.wait_ge(o_ready, 1)
                    link(v.tensor_copy(od[:], O[:, 0:NB * NS]))
                    v.tensor_tensor(oq[:], od[:], od[:], ALU.mult).then_inc(oq_ready, 1)
                if sl == SLOTS_A + 1:
                    dve.wait_ge(o_sum, 1)
                    v.tensor_scalar(orr[:], O[:, 256:256 + NB * NS], 1.0 / (2 * DH), EPS, ALU.mult, ALU.add).then_inc(orr_ready, 1)
                if sl == SLOTS_A + 2:
                    dve.wait_ge(o_rs, 1)
                    link(v.tensor_scalar(orr[:], orx[:], s.gsub[:], None, ALU.mult))
                    v.tensor_tensor(s.oT["d"][:, :, SEQ:TOK], jb(od[:]), jb(orr[:]), ALU.mult).then_inc(oT_ready, 1)
            dve.wait_ge(o_ready, 2)
            for c in range(2):
                r = 64 * c
                v.tensor_copy(s.oT["s"][r:r + 64, :, SEQ:TOK],
                              O[r:r + 64, 0:2 * NB * NS].rearrange("p (j b c) -> p j b c", j=NB, c=2)[:, :, :, c]).then_inc(oT_ready, 1)
            add_x(NT - 1)
            for q, (k, c) in enumerate(PASSES):
                m = m_of[(q, NT, "y")]
                dve.wait_ge(made, m + 1)
                dst = merged_s[:, W * c:W * c + W]
                for g in range(NB):
                    cols = slice(128 * g, 128 * g + 128)
                    ins = v.tensor_tensor((branch[0:NS, :] if k else dst)[:, cols], ring[m % RING][32 * g:32 * g + NS, 0:128],
                                          gate_s[:, q, cols], ALU.mult)
                ins.then_inc(y_read, 1)
                dve.wait_ge(y_read, reads(m + 1))
                if k:
                    link(v.tensor_tensor(dst, dst, branch[0:NS, :], ALU.add))
            dve.sem_inc(ms_ready, 1)
            add_x(NT)


def route(nc, io, s):
    with ExitStack() as ctx:
        sb = lambda n, sh, dt=F32: ctx.enter_context(nc.sbuf_tensor("r_" + n, sh, dt))
        ps = lambda n, sh: ctx.enter_context(nc.psum_tensor("r_" + n, sh, F32))
        sem = lambda n: ctx.enter_context(nc.semaphore("r_" + n))
        sq = sb("sq", [128, D])
        ms, rs = sb("ms", [128, TILES]), sb("rs", [128, TILES])
        hn = sb("hn", [128, 2, KD, 128])
        hT = sb("hT", [128, 2, KD, 128])
        wr = sb("wr", [128, KD, NG + NE])
        L = sb("L", [128, TILES, NG + NE])
        T = [ps(f"T{n}", [128, 4, 128]) for n in range(2)]
        LG = ps("LG", [128, TILES, 64])
        RK, CT, TB = ps("RK", [128, TILES, NE]), ps("CT", [128, NE]), ps("TB", [CAP, NBLK])
        small = {}

        def sm(name, *shape):
            small[name] = sb(name, [128, *shape])
            return small[name]
        gm, gs, gmin, gw = (sm(n, TILES) for n in ("gm", "gs", "gmin", "gw"))
        gexp, geq, gcand, goh = (sm(n, TILES, NG) for n in ("gexp", "geq", "gcand", "goh"))
        tmp = sm("tmp", TILES, NG, EG)
        ein, eeq, ecand = (sm(n, TILES, EG) for n in ("ein", "eeq", "ecand"))
        eoh = [sm(f"eoh{k}", TILES, EG) for k in range(2)]
        ev = [sm(f"ev{k}", TILES) for k in range(2)]
        emin, dl, valid = sm("emin", TILES), sm("dl", TILES), sm("valid", TILES)
        O = [sm(f"O{k}", TILES, NE) for k in range(2)]
        C = sm("C", TILES, NE)
        cnt, xe, Xi, shift, base = (sm(n, NE) for n in ("cnt", "xe", "Xi", "shift", "base"))
        cmp = sm("cmp", NE, NX)
        row, over = sm("row", TILES, NE), sm("over", TILES, NE)
        slot = sm("slot", 2, TILES)
        blk, rk, thr = sm("blk", 2, TILES), sm("rk", 2, TILES), sm("thr", NBLK)
        cmpb = sm("cmpb", 2 * TILES, NBLK)
        Bk, Rk = sm("Bk", 2 * TILES, NBLK), sm("Rk", 2 * TILES, CAP)
        eid = sm("eid", NX + 1)
        stored = [sem(f"stored{n}") for n in range(2)]
        (wr_in, x_sq, pool_chain, rms, hn_ready, turned, hT_ready, logits, chain, gd, gx, ranked, counted, cdone, tab_in,
         tabled, elx, wx) = map(sem, ("wr_in x_sq pool_chain rms hn_ready turned hT_ready logits chain gd gx ranked counted "
                                  "cdone tab_in tabled elx wx").split())
        block = ctx.enter_context(nc.Block())

        @block.sync
        def _(sp):
            sp.dma_start(s.gffn[:], io["g_ffn"][0].rearrange("(p j) -> p j", j=KD)).then_inc(wr_in, 16)
            sp.dma_start(wr[:, :, 0:NG], io["w_group"][0].rearrange("(p j) c -> p j c", j=KD)).then_inc(wr_in, 16)
            sp.dma_start(wr[:, :, NG:NG + NE], io["w_router"][0].rearrange("(p j) c -> p j c", j=KD)).then_inc(wr_in, 16)
            for e in range(2):
                for n, wt in enumerate(("w_gate", "w_up", "w_down")):
                    sp.dma_start(s.ew[n][:, e], s.expert(io[wt], e, n)).then_inc(s.ew_in[n][e], 16)
            for i, p in enumerate(ROWS):
                sp.wait_ge(hn_ready, i + 1)
                sp.dma_start(s.rows[128 * i:128 * i + p, :], hn[0:p, i % 2].rearrange("p j q -> p (j q)")).then_inc(stored[i % 2], 16)
            for n in range(2):
                sp.wait_ge(stored[n], 16 * len(range(n, TILES, 2)))

        @block.scalar
        def _(act):
            for i, p in enumerate(ROWS):
                if i:
                    act.wait_ge(x_sq, i)
                nc.scalar.activation(sq[0:p, :], s.x[0:p, i, :], ACT.Square, accum_out=ms[0:p, i:i + 1]).then_inc(x_sq, 1)
            act.wait_ge(gd, 1)
            nc.scalar.activation(gexp[:], gexp[:], ACT.Exp).then_inc(gx, 1)
            act.wait_ge(gd, 2)
            nc.scalar.activation(dl[:], dl[:], ACT.Exp).then_inc(gx, 1)

        @block.gpsimd
        def _(pool):
            for i, p in enumerate(ROWS):
                pool.wait_ge(x_sq, i + 1)
                nc.gpsimd.tensor_scalar(rs[0:p, i:i + 1], ms[0:p, i:i + 1], 1.0 / D, EPS, ALU.mult, ALU.add).then_inc(pool_chain, 1)
                pool.wait_ge(pool_chain, i + 1)
                nc.gpsimd.tensor_tensor(rs[0:p, i:i + 1], rs[0:p, i:i + 1], s.c[0:p, C_MH:C_MH + 1], ALU.pow).then_inc(rms, 1)

        @block.tensor
        def _(pe):
            pe.wait_ge(wr_in, 48)
            for i, p in enumerate(ROWS):
                pe.wait_ge(hn_ready, i + 1)
                for h in range(2):
                    if i:
                        pe.wait_ge(hT_ready, 2 * i - 1 + h)
                    for j in range(4):
                        last = nc.tensor.transpose(T[h][:, j, 0:p], hn[0:p, i % 2, 4 * h + j, :], s.ident[0:p, 0:p])
                    last.then_inc(turned, 1)
                pe.wait_ge(hT_ready, 2 * i + 2)
                for j in range(KD):
                    last = nc.tensor.matmul(LG[0:p, i, 0:NG + NE], hT[:, i % 2, j, 0:p], wr[:, j, :], start=j == 0, stop=j == KD - 1)
                last.then_inc(logits, 1)
            pe.wait_ge(cdone, 1)
            for i in range(TILES):
                for j in range(i + 1):
                    last = nc.tensor.matmul(RK[:, i, :], s.c[:, C_LT:C_ONE] if j == i else s.c[:, C_ONE:C_CM], C[:, j, :],
                                            start=j == 0, stop=j == i)
            last.then_inc(ranked, 1)
            for j in range(TILES):
                last = nc.tensor.matmul(CT[:], s.c[:, C_ONE:C_CM], C[:, j, :], start=j == 0, stop=j == TILES - 1)
            last.then_inc(counted, 1)
            pe.wait_ge(tab_in, 1)
            for m in range(2 * TILES):
                p = ROWS[m % TILES]
                last = nc.tensor.matmul(TB[:], Rk[0:p, m, :], Bk[0:p, m, :], start=m == 0, stop=m == 2 * TILES - 1)
            last.then_inc(tabled, 1)

        @block.vector
        def _(dve):
            link = Chain(dve, chain)
            v = nc.vector
            iota = lambda n: s.c[:, C_IOTA:C_IOTA + n]
            link(v.memset(L[:], 0.0))
            dve.wait_ge(wr_in, 48)
            for i, p in enumerate(ROWS):
                dve.wait_ge(rms, i + 1)
                if i >= 2:
                    dve.wait_ge(turned, 2 * (i - 1))
                    dve.wait_ge(stored[i % 2], 16 * (i // 2))
                v.tensor_scalar(hn[0:p, i % 2], s.x[0:p, i, :].rearrange("t (p j) -> t j p", j=KD), rs[0:p, i:i + 1], None,
                                ALU.mult).then_inc(hn_ready, 1)
                for h in range(2):
                    dve.wait_ge(turned, 2 * i + h + 1)
                    if i >= 2:
                        dve.wait_ge(logits, i - 1)
                    v.tensor_tensor(hT[:, i % 2, 4 * h:4 * h + 4, 0:p], T[h][:, :, 0:p], bcast(s.gffn[:, 4 * h:4 * h + 4], p, 2),
                                    ALU.mult).then_inc(hT_ready, 1)
            dve.wait_ge(logits, TILES)
            link(v.tensor_copy(L[:, 0:NT, :], LG[:, 0:NT, 0:NG + NE]))
            link(v.tensor_copy(L[0:NS, NT, :], LG[0:NS, NT, 0:NG + NE]))
            Lg, Le = L[:, :, 0:NG], L[:, :, NG:NG + NE].rearrange("p t (g e) -> p t g e", g=NG)

            def first_max(src, n, top, eq, cand, low, onehot):
                link(v.tensor_reduce(top[:], src, AX.X, ALU.max))
                link(v.tensor_tensor(eq[:], src, bcast(top[:], n, 2), ALU.is_equal))
                link(v.tensor_scalar(eq[:], eq[:], -99.0, None, ALU.mult))
                link(v.tensor_tensor(cand[:], eq[:], bcast(iota(n), TILES, 1), ALU.add))
                link(v.tensor_reduce(low[:], cand[:], AX.X, ALU.min))
                link(v.tensor_tensor(onehot[:], cand[:], bcast(low[:], n, 2), ALU.is_equal))

            first_max(Lg, NG, gm, geq, gcand, gmin, goh)
            v.tensor_tensor(gexp[:], Lg, bcast(gm[:], NG, 2), ALU.subtract).then_inc(gd, 1)
            link(v.tensor_tensor(tmp[:], Le, bcast(goh[:], EG, 3), ALU.mult))
            link(v.tensor_reduce(ein[:], tmp[:].rearrange("p t g e -> p t e g"), AX.X, ALU.add))
            first_max(ein[:], EG, ev[0], eeq, ecand, emin, eoh[0])
            link(v.tensor_scalar(eeq[:], eoh[0][:], MASKED, None, ALU.mult))
            link(v.tensor_tensor(ein[:], ein[:], eeq[:], ALU.add))
            first_max(ein[:], EG, ev[1], eeq, ecand, emin, eoh[1])
            v.tensor_tensor(dl[:], ev[1][:], ev[0][:], ALU.subtract).then_inc(gd, 1)
            dve.wait_ge(gx, 2)
            link(v.tensor_reduce(gs[:], gexp[:], AX.X, ALU.add))
            link(v.reciprocal(gw[:], gs[:]))
            link(v.tensor_scalar(gs[:], dl[:], 1.0, None, ALU.add))
            link(v.reciprocal(gs[:], gs[:]))
            link(v.tensor_tensor(s.wt[:, 0, :], gs[:], gw[:], ALU.mult))
            link(v.tensor_tensor(s.wt[:, 1, :], s.wt[:, 0, :], dl[:], ALU.mult))
            link(v.tensor_scalar(valid[:], s.c[:, C_TOK:C_THR], float(TOK), None, ALU.is_lt))
            link(v.tensor_tensor(goh[:], goh[:], bcast(valid[:], NG, 2), ALU.mult))
            for k in range(2):
                for g in range(NG):
                    link(v.tensor_tensor(O[k][:, :, EG * g:EG * g + EG], eoh[k][:], bcast(goh[:, :, g], EG, 2), ALU.mult))
            v.tensor_tensor(C[:], O[0][:], O[1][:], ALU.add).then_inc(cdone, 1)
            dve.wait_ge(counted, 1)
            link(v.tensor_copy(cnt[:], CT[:]))
            link(v.tensor_tensor(cmp[:], bcast(cnt[:], NX, 2), bcast(s.c[:, C_THR:C_MH], NE, 1), ALU.is_gt))
            link(v.tensor_reduce(xe[:], cmp[:], AX.X, ALU.add))
            link(v.tensor_tensor_scan(Xi[:], s.c[:, C_ONE:C_ONE + NE], xe[:], 0.0, ALU.mult, ALU.add))
            link(v.tensor_tensor(shift[:], Xi[:], xe[:], ALU.subtract))
            link(v.tensor_tensor(shift[:], shift[:], iota(NE), ALU.subtract))
            link(v.tensor_scalar(shift[:], shift[:], float(NE - 1), float(CAP), ALU.add, ALU.mult))
            link(v.tensor_scalar(base[:], iota(NE), float(CAP), None, ALU.mult))
            link(v.tensor_scalar(over[:], RK[:], float(CAP), None, ALU.is_ge))
            link(v.tensor_tensor(over[:], over[:], bcast(shift[:], TILES, 1), ALU.mult))
            link(v.tensor_tensor(row[:], RK[:], bcast(base[:], TILES, 1), ALU.add))
            link(v.tensor_tensor(row[:], row[:], over[:], ALU.add))
            for k in range(2):
                link(v.tensor_tensor(over[:], row[:], O[k][:], ALU.mult))
                link(v.tensor_reduce(slot[:, k, :], over[:], AX.X, ALU.add))
            link(v.tensor_copy(s.slot[:], slot[:]))
            link(v.tensor_scalar(thr[:], iota(NBLK), 1.0, float(CAP), ALU.add, ALU.mult))
            fl = slot[:].rearrange("p k t -> p (k t)")
            bl, rl = blk[:].rearrange("p k t -> p (k t)"), rk[:].rearrange("p k t -> p (k t)")
            link(v.tensor_tensor(cmpb[:], bcast(fl, NBLK, 2), bcast(thr[:], 2 * TILES, 1), ALU.is_ge))
            link(v.tensor_reduce(bl, cmpb[:], AX.X, ALU.add))
            link(v.tensor_scalar(rl, bl, -float(CAP), None, ALU.mult))
            link(v.tensor_tensor(rl, rl, fl, ALU.add))
            link(v.tensor_tensor(Rk[:], bcast(iota(CAP), 2 * TILES, 1), bcast(rl, CAP, 2), ALU.is_equal))
            link(v.tensor_tensor(Bk[:], bcast(iota(NBLK), 2 * TILES, 1), bcast(bl, NBLK, 2), ALU.is_equal))
            for k in range(2):
                last = v.tensor_tensor(Bk[:, TILES * k:TILES * k + TILES, :], Bk[:, TILES * k:TILES * k + TILES, :],
                                       bcast(s.c[:, C_TOK:C_THR], NBLK, 2), ALU.mult)
                link(last)
            dve.sem_inc(tab_in, 1)
            cmpe = cmp[:].rearrange("p a b -> p (a b)").rearrange("p (b e) -> p b e", b=NX)
            link(v.tensor_tensor(cmpe, bcast(Xi[:], NX, 1), bcast(iota(NX), NE, 2), ALU.is_le))
            link(v.tensor_reduce(eid[:, 0:NX], cmpe, AX.X, ALU.add))
            link(v.tensor_scalar(eid[:, 0:NX], eid[:, 0:NX], float(NE - 1), None, ALU.min))
            link(v.tensor_copy(eid[:, NX:NX + 1], Xi[:, NE - 1:NE]))
            link(v.tensor_copy(s.ctl[:], eid[0:1, :]))
            dve.wait_ge(tabled, 1)
            link(v.tensor_copy(s.table[:], TB[:]))


HW = DE // 2


def experts(nc, io, s):
    with ExitStack() as ctx:
        sb = lambda n, sh, dt=F32: ctx.enter_context(nc.sbuf_tensor("e_" + n, sh, dt))
        ps = lambda n, sh: ctx.enter_context(nc.psum_tensor("e_" + n, sh, F32))
        sem = lambda n: ctx.enter_context(nc.semaphore("e_" + n))
        idx = sb("idx", [CAP, 2], I32)
        xg = [sb(f"xg{n}", [CAP, D]) for n in range(2)]
        xT = sb("xT", [128, 2, KD, CAP])
        sig, den, a = sb("sig", [128, HW]), sb("den", [128, HW]), sb("a", [128, HW])
        aT = sb("aT", [128, 2, 128])
        y = [sb(f"y{n}", [128, W]) for n in range(2)]
        TX, AT = ps("TX", [128, KD, CAP]), ps("AT", [128, 2, 128])
        G, U, Y = ([ps(f"{k}{n}", [128, w]) for n in range(2)] for k, w in (("G", W), ("U", W), ("Y", W)))
        (x_turned, xT_out, g_done, u_done, gated, chain, a_ready, a_turned, aT_out, d_done, y_out, idx_ready, x_started, idx_seen) = map(sem, (
            "x_turned xT_out g_done u_done gated chain a_ready a_turned aT_out d_done y_out idx_ready x_started idx_seen").split())
        xg_in = [sem(f"xg_in{n}") for n in range(2)]
        y_stored = [sem(f"y_stored{n}") for n in range(2)]
        block = ctx.enter_context(nc.Block())

        def pe_block(pe, e, it, j, first):
            pe.wait_ge(xg_in[j], it * 16 + 16)
            if not (first and j == 0):
                pe.wait_ge(xT_out, e)
            pe.sem_inc(x_started, 1)
            for b in range(KD):
                last = nc.tensor.transpose(TX[:, b, :], xg[j][:, 128 * b:128 * b + 128], s.ident[0:CAP, 0:CAP])
            last.then_inc(x_turned, 1)
            pe.wait_ge(xT_out, e + 1)
            if not first:
                pe.wait_ge(a_ready, e - 1)
            for n, (bank, done) in enumerate(((G[j], g_done), (U[j], u_done))):
                pe.wait_ge(s.ew_in[n][j], it * 16 + 16)
                for b in range(KD):
                    for h in range(2):
                        last = nc.tensor.matmul(bank[CAP * h:CAP * h + CAP, 0:HW], xT[:, j, b, :], s.ew[n][:, j, b, HW * h:HW * h + HW],
                                                start=b == 0, stop=b == KD - 1)
                last.then_inc(done, 1)
            pe.wait_ge(a_ready, e + 1)
            if not (first and j == 0):
                pe.wait_ge(aT_out, e)
            for b in range(2):
                last = nc.tensor.transpose(AT[:, b, :], a[:, 128 * b:128 * b + 128], s.ident[:])
            last.then_inc(a_turned, 1)
            pe.wait_ge(aT_out, e + 1)
            pe.wait_ge(s.ew_in[2][j], it * 16 + 16)
            if not first:
                pe.wait_ge(y_out, e - 1)
            for b in range(4):
                for h in range(2):
                    last = nc.tensor.matmul(Y[j][CAP * h:CAP * h + CAP, :], aT[:, b % 2, CAP * (b // 2):CAP * (b // 2) + CAP],
                                            s.ew[2][:, j, b, W * h:W * h + W], start=b == 0, stop=b == 3)
            last.then_inc(d_done, 1)

        def act_block(act, e, it, j, first):
            act.wait_ge(g_done, e + 1)
            if not (first and j == 0):
                act.wait_ge(a_ready, e)
            nc.scalar.activation(sig[:], G[j][:, 0:HW], ACT.Sigmoid).then_inc(gated, 1)
            act.wait_ge(d_done, e + 1)
            if not first:
                act.wait_ge(y_stored[j], it * 32)
            nc.scalar.copy(y[j][:], Y[j][:]).then_inc(y_out, 1)
            act.wait_ge(y_out, e + 1)
            for h in range(2):
                act.dma_start(s.out_rows(e)[:, W * h:W * h + W], y[j][CAP * h:CAP * h + CAP, :]).then_inc(y_stored[j], 16)

        def dve_block(dve, e, it, j, first):
            v = nc.vector
            dve.wait_ge(x_turned, e + 1)
            if not first:
                dve.wait_ge(u_done, e - 1)
            v.tensor_tensor(xT[:, j], TX[:], bcast(s.gffn[:], CAP, 2), ALU.mult).then_inc(xT_out, 1)
            dve.wait_ge(gated, e + 1)
            v.tensor_tensor(den[:], sig[:], G[j][:, 0:HW], ALU.mult).then_inc(chain, 1)
            dve.wait_ge(chain, e + 1)
            dve.wait_ge(u_done, e + 1)
            if not (first and j == 0):
                dve.wait_ge(a_turned, e)
            v.tensor_tensor(a[:], den[:], U[j][:, 0:HW], ALU.mult).then_inc(a_ready, 1)
            dve.wait_ge(a_turned, e + 1)
            if not (first and j == 0):
                dve.wait_ge(d_done, e)
            v.tensor_copy(aT[:], AT[:]).then_inc(aT_out, 1)

        def pool_block(pool, e, it, j, first):
            if not first:
                pool.wait_ge(x_turned, e - 1)
            nc.gpsimd.tensor_copy(idx[:, j:j + 1], s.table[:, bass.ds(e, 1)]).then_inc(idx_ready, 1)
            pool.wait_ge(idx_ready, e + 1)
            pool.sem_inc(idx_seen, 1)
            nc.gpsimd.indirect_dma_start(out=xg[j][:], out_offset=None, in_=s.rows[:, :],
                                         in_offset=bass.IndirectOffsetOnAxis(ap=idx[:, j:j + 1], axis=0)).then_inc(xg_in[j], 16)

        def sp_block(sp, e, it, j, first):
            for n, (wt, done) in enumerate((("w_gate", g_done), ("w_up", u_done), ("w_down", d_done))):
                sp.wait_ge(done, e - 1)
                sp.dma_start(s.ew[n][:, j], s.expert(io[wt], e, n)).then_inc(s.ew_in[n][j], 16)

        def run(eng, step, peel=True):
            if peel:
                for j in range(2):
                    step(eng, j, 0, j, True)
            with eng.Fori(1, NE // 2) as it:
                for j in range(2):
                    step(eng, it * 2 + j, it, j, False)

        def extra(eng, step):
            n = eng.value_load(s.ctl[0:1, NX:NX + 1], min_val=0, max_val=NX)
            with eng.If(n > 0):
                with eng.Fori(0, n) as b:
                    step(eng, b)
                eng.nop()
            eng.nop()

        @block.sync
        def _(sp):
            run(sp, sp_block, peel=False)

            def step(sp, b):
                e = sp.value_load(s.ctl[0:1, bass.ds(b, 1)], min_val=0, max_val=NE - 1)
                sp.wait_ge(y_out, b + NE)
                for n, wt in enumerate(("w_gate", "w_up", "w_down")):
                    sp.dma_start(s.ew[n][:, 0], s.expert(io[wt], e, n)).then_inc(s.ew_in[n][0], 16)
                sp.nop()
            extra(sp, step)
            sp.wait_ge(y_stored[1], NE * 16)
            sp.wait_ge(y_stored[0], NE * 16)

        @block.tensor
        def _(pe):
            run(pe, pe_block)

            def step(pe, b):
                pe.wait_ge(xg_in[0], b * 16 + NE * 8 + 16)
                pe.wait_ge(y_out, b + NE)
                pe.sem_inc(x_started, 1)
                for k in range(KD):
                    last = nc.tensor.transpose(TX[:, k, :], xg[0][:, 128 * k:128 * k + 128], s.ident[0:CAP, 0:CAP])
                last.then_inc(x_turned, 1)
                pe.wait_ge(xT_out, b + NE + 1)
                for n, (bank, done) in enumerate(((G[0], g_done), (U[0], u_done))):
                    pe.wait_ge(s.ew_in[n][0], b * 16 + NE * 8 + 16)
                    for k in range(KD):
                        for h in range(2):
                            last = nc.tensor.matmul(bank[CAP * h:CAP * h + CAP, 0:HW], xT[:, 0, k, :], s.ew[n][:, 0, k, HW * h:HW * h + HW],
                                                    start=k == 0, stop=k == KD - 1)
                    last.then_inc(done, 1)
                pe.wait_ge(a_ready, b + NE + 1)
                for k in range(2):
                    last = nc.tensor.transpose(AT[:, k, :], a[:, 128 * k:128 * k + 128], s.ident[:])
                last.then_inc(a_turned, 1)
                pe.wait_ge(aT_out, b + NE + 1)
                pe.wait_ge(s.ew_in[2][0], b * 16 + NE * 8 + 16)
                for k in range(4):
                    for h in range(2):
                        last = nc.tensor.matmul(Y[0][CAP * h:CAP * h + CAP, :], aT[:, k % 2, CAP * (k // 2):CAP * (k // 2) + CAP],
                                                s.ew[2][:, 0, k, W * h:W * h + W], start=k == 0, stop=k == 3)
                last.then_inc(d_done, 1)
                pe.nop()
            extra(pe, step)

        @block.scalar
        def _(act):
            run(act, act_block)

            def step(act, b):
                act.wait_ge(g_done, b + NE + 1)
                nc.scalar.activation(sig[:], G[0][:, 0:HW], ACT.Sigmoid).then_inc(gated, 1)
                act.wait_ge(d_done, b + NE + 1)
                act.wait_ge(y_stored[0], b * 32 + NE * 16)
                nc.scalar.copy(y[0][:], Y[0][:]).then_inc(y_out, 1)
                act.wait_ge(y_out, b + NE + 1)
                for h in range(2):
                    act.dma_start(s.out_rows(b + NE)[:, W * h:W * h + W], y[0][CAP * h:CAP * h + CAP, :]).then_inc(y_stored[0], 16)
                act.wait_ge(y_stored[0], b * 32 + NE * 16 + 32)
                act.nop()
            extra(act, step)

        @block.vector
        def _(dve):
            run(dve, dve_block)

            def step(dve, b):
                v = nc.vector
                dve.wait_ge(x_turned, b + NE + 1)
                v.tensor_tensor(xT[:, 0], TX[:], bcast(s.gffn[:], CAP, 2), ALU.mult).then_inc(xT_out, 1)
                dve.wait_ge(gated, b + NE + 1)
                v.tensor_tensor(den[:], sig[:], G[0][:, 0:HW], ALU.mult).then_inc(chain, 1)
                dve.wait_ge(chain, b + NE + 1)
                dve.wait_ge(u_done, b + NE + 1)
                v.tensor_tensor(a[:], den[:], U[0][:, 0:HW], ALU.mult).then_inc(a_ready, 1)
                dve.wait_ge(a_turned, b + NE + 1)
                v.tensor_copy(aT[:], AT[:]).then_inc(aT_out, 1)
                dve.nop()
            extra(dve, step)

        @block.gpsimd
        def _(pool):
            run(pool, pool_block)

            def step(pool, b):
                pool.wait_ge(x_turned, b + NE)
                nc.gpsimd.tensor_copy(idx[:, 0:1], s.table[:, bass.ds(b + NE, 1)]).then_inc(idx_ready, 1)
                pool.wait_ge(idx_ready, b + NE + 1)
                pool.sem_inc(idx_seen, 1)
                nc.gpsimd.indirect_dma_start(out=xg[0][:], out_offset=None, in_=s.rows[:, :],
                                             in_offset=bass.IndirectOffsetOnAxis(ap=idx[:, 0:1], axis=0)).then_inc(xg_in[0], 16)
                pool.nop()
            extra(pool, step)


def combine_experts(nc, io, s):
    with ExitStack() as ctx:
        sem = lambda n: ctx.enter_context(nc.semaphore("c_" + n))
        yg = [[ctx.enter_context(nc.sbuf_tensor(f"c_yg{i}{k}", [128, D], F32)) for k in range(2)] for i in range(TILES)]
        rows_in = [sem(f"rows_in{i}") for i in range(TILES)]
        chain, done, stored = sem("chain"), sem("done"), sem("stored")
        block = ctx.enter_context(nc.Block())

        @block.gpsimd
        def _(pool):
            for i, p in enumerate(ROWS):
                for k in range(2):
                    nc.gpsimd.indirect_dma_start(out=yg[i][k][0:p, :], out_offset=None, in_=s.eout[:, :],
                                                 in_offset=bass.IndirectOffsetOnAxis(ap=s.slot[0:p, k, i:i + 1], axis=0)).then_inc(rows_in[i], 16)

        @block.vector
        def _(dve):
            for i, p in enumerate(ROWS):
                dve.wait_ge(rows_in[i], 32)
                xs = s.x[0:p, i, :]
                nc.vector.scalar_tensor_tensor(xs, yg[i][0][0:p, :], s.wt[0:p, 0, i:i + 1], xs, ALU.mult, ALU.add).then_inc(chain, 1)
                dve.wait_ge(chain, i + 1)
                nc.vector.scalar_tensor_tensor(xs, yg[i][1][0:p, :], s.wt[0:p, 1, i:i + 1], xs, ALU.mult, ALU.add).then_inc(done, 1)

        @block.sync
        def _(sp):
            for i, p in enumerate(ROWS):
                sp.wait_ge(done, i + 1)
                dst = io["y_p"][128 * i:128 * i + p, :] if i < NT else io["y_s"]
                sp.dma_start(dst, s.x[0:p, i, :]).then_inc(stored, 16)
            sp.wait_ge(stored, 16 * TILES)


class State:
    pass


def step_kernel(nc, io):
    s = State()
    s.pool = io["cache_idx_k"].shape[1]
    s.rows = nc.dram_tensor("token_rows", (TOK, D), F32, kind="Internal").ap()
    s.eout = nc.dram_tensor("expert_rows", (NBLK * CAP, D), F32, kind="Internal").ap()
    s.out_rows = lambda e: s.eout.rearrange("(b c) d -> b c d", c=CAP)[e]
    s.expert = lambda ap, e, n: ap[0, e].rearrange("(p j) c -> p j c", j=KD) if n < 2 else ap[0, e].rearrange("(j p) c -> p j c", p=128)

    def tensors(stack, prefix):
        return lambda n, sh, dt=F32: stack.enter_context(nc.sbuf_tensor(prefix + n, sh, dt))

    with ExitStack() as top:
        sb = tensors(top, "k_")
        s.x = sb("x", [128, TILES, D])
        s.c = sb("c", [128, C_END])
        s.ident = s.c[:, C_ID:C_LT]
        with ExitStack() as mix:
            sb = tensors(mix, "m_")
            s.w_in = [mix.enter_context(nc.semaphore(f"w_in{n}")) for n in range(2)]
            s.xT = sb("xT", [128, KD, TOK])
            s.w = sb("w", [128, 2, KD, W])
            s.oT = {k: sb("oT" + k, [128, NB, TOK]) for k in "ds"}
            s.neglam, s.gsub = sb("neglam", [128, 1]), sb("gsub", [128, 1])
            s.row = {k: sb("row" + k, [NS, W]) for k in NORMED + ("vs", "vd")}
            s.sel_s = sb("sel_s", [NS, PAST + 1])
            with ExitStack() as att:
                sb = tensors(att, "t_")
                s.T = {k: sb("T" + k, [128, NB, SEQ]) for k in NORMED}
                s.v = {k: sb("v" + k, [128, NT, W]) for k in ("vs", "vd")}
                s.sel = [None] + [sb(f"sel{t}", [128, 128 * (t + 1)]) for t in range(1, NT)]
                with ExitStack() as pr:
                    sb = tensors(pr, "q_")
                    s.gmix = sb("gmix", [128, KD])
                    s.gains = sb("gains", [128, 4, DH])
                    s.rope = sb("rope", [128, 2, TILES, DH])
                    s.rg = sb("rg", [128, 4, 2, TILES, DH])
                    normalise_inputs(nc, io, s)
                    project(nc, io, s)
                attend_prompt(nc, io, s)
            merge(nc, io, s)
        with ExitStack() as moe:
            sb = tensors(moe, "x_")
            s.gffn = sb("gffn", [128, KD])
            s.wt, s.slot = sb("wt", [128, 2, TILES]), sb("slot", [128, 2, TILES], I32)
            s.table, s.ctl = sb("table", [CAP, NBLK], I32), sb("ctl", [1, NX + 1], I32)
            with ExitStack() as ring:
                s.ew = [ring.enter_context(nc.sbuf_tensor(f"x_ew{n}", [128, 2, *sh], F32)) for n, sh in enumerate(((KD, DE), (KD, DE), (4, D)))]
                s.ew_in = [[ring.enter_context(nc.semaphore(f"ew_in{n}{j}")) for j in range(2)] for n in range(3)]
                route(nc, io, s)
                experts(nc, io, s)
            combine_experts(nc, io, s)


INPUTS = ["x_prompt", "x_sample", "cache_diff_k", "cache_diff_v", "cache_dsa_k", "cache_dsa_v", "cache_idx_k", "page_table", "g_mix",
          "w_in", "g_q_diff", "g_k_diff", "lam_q1", "lam_k1", "lam_q2", "lam_k2", "g_subln", "g_q_dsa", "g_k_dsa", "w_o_diff",
          "w_o_dsa", "w_out", "g_ffn", "w_group", "w_router", "w_gate", "w_up", "w_down"]
KEPT = [("kd", W, (4, 2, DH)), ("vd", W, (4, 2 * DH)), ("ks", W, (H, DH)), ("vs", W, (H, DH)), ("ki", DH, (DH,))]
OUTPUTS = ([("y_p", (SEQ, D), (1, SEQ, D)), ("y_s", (NS, D), (NS, 1, D))]
           + [(f"new_{n}_p", (SEQ, w), (1, 1, SEQ, *sh)) for n, w, sh in KEPT]
           + [(f"new_{n}_s", (NS, w), (1, NS, 1, *sh)) for n, w, sh in KEPT])


def kernel(**inputs):
    import concourse.bacc as bacc
    from concourse.bass_utils import run_bass_kernel_spmd

    nc = bacc.Bacc("TRN2", target_bir_lowering=False, num_devices=1)
    arrays = {f"in_{name}": np.ascontiguousarray(inputs[name]) for name in INPUTS}
    arrays["in_consts"] = constants()
    arrays["in_rope"] = rope_table().reshape(128, 2, TILES, DH)
    io = {n[3:]: nc.dram_tensor(n, a.shape, mybir.dt.from_np(a.dtype), kind="ExternalInput").ap() for n, a in arrays.items()}
    for name, shape, _ in OUTPUTS:
        io[name] = nc.dram_tensor("out_" + name, shape, F32, kind="ExternalOutput").ap()
    step_kernel(nc, io)
    got = run_bass_kernel_spmd(nc, [arrays], core_ids=[0]).results[0]
    return tuple(got["out_" + name].reshape(full) for name, _, full in OUTPUTS)
```

```python
import concourse.bass as bass
from concourse import mybir
from contextlib import ExitStack
import numpy as np

F32, I32 = mybir.dt.float32, mybir.dt.int32
ALU = mybir.AluOpType
ACT = mybir.ActivationFunctionType
AX = mybir.AxisListType

D = 1024
KD = D // 128
SEQ, NS = 512, 8
NT = SEQ // 128
TILES = NT + 1
TOK = SEQ + NS
ROWS = [128] * NT + [NS]
H, DH = 8, 64
W = H * DH
NB = W // 128
PAGE, NPAGE = 128, 4
PAST = PAGE * NPAGE
TOPK = 128
P_TOTAL = 7 * W + DH + H + 2 * D
OFF = dict(qd=0, kd=W, vd=2 * W, qs=3 * W, ks=4 * W, vs=5 * W, qi=6 * W, kw=7 * W,
           gd=7 * W + DH + H, gs=7 * W + DH + H + D)
NG, EG = 4, 8
NE = NG * EG
DE = 512
CAP = 64
NX = 2 * TOK // CAP
NBLK = NE + NX
EPS = 1e-6
LAM_INIT = 0.2
MASKED, TAKEN = -2.0e38, -3.0e38

C_ID, C_LT, C_ONE, C_CM = 0, 128, 256, 384
C_E, C_ET, C_HM, C_IOTA, C_TOK, C_THR, C_MH, C_PAR = 896, 960, 968, 976, 1040, 1045, 1061, 1069
C_DH, C_DB, C_SB, C_END = 1070, 1074, 1082, 1086


def constants():
    c = np.zeros((128, C_END), np.float32)
    p = np.arange(128)
    c[:, C_ID:C_LT] = np.eye(128)
    c[:, C_LT:C_ONE] = p[:, None] < p[None, :]
    c[:, C_ONE:C_CM] = 1
    c[:, C_CM + 384:C_E] = np.where(p[None, :] <= p[:, None], 0, MASKED)
    for b in range(NS):
        c[b, C_E + 8 * b:C_E + 8 * b + 8] = 1
    c[:64, C_ET:C_HM] = (p[:64, None] // 8) == np.arange(8)
    c[:, C_HM:C_IOTA] = (p[:, None] % 8) == np.arange(8)
    c[:, C_IOTA:C_TOK] = np.arange(64)
    c[:, C_TOK:C_THR] = p[:, None] + 128 * np.arange(TILES)
    c[:, C_THR:C_MH] = CAP * (1 + np.arange(16))
    c[:, C_MH:C_PAR] = -0.5
    c[:, C_PAR] = p % 2
    c[:, C_DH:C_DB] = (p[:, None] % 4) == np.arange(4)
    c[:, C_DB:C_SB] = (p[:, None] % 32 // 4) == np.arange(8)
    c[:, C_SB:C_END] = (p[:, None] % 32 // 8) == np.arange(4)
    return c


def rope_table():
    pos = np.full(128 * TILES, PAST, np.float32)
    pos[:SEQ] = np.arange(SEQ)
    inv = np.power(np.float32(10000.0), -np.arange(DH // 2, dtype=np.float32) / np.float32(DH // 2))
    ang = (pos[:, None] * inv[None]).astype(np.float32)
    t = np.stack([np.cos(ang), np.cos(ang), np.sin(ang), np.sin(ang)], 1).astype(np.float32)
    return np.ascontiguousarray(t.reshape(TILES, 128, 2, DH).transpose(1, 2, 0, 3).reshape(128, -1))


class Chain:

    def __init__(self, eng, sem):
        self.eng, self.sem, self.n = eng, sem, 0

    def __call__(self, ins):
        self.n += 1
        ins.then_inc(self.sem, 1)
        self.eng.wait_ge(self.sem, self.n)


def bcast(ap, n, axis):
    shape = list(ap.shape)
    return ap.unsqueeze(axis).to_broadcast(shape[:axis] + [n] + shape[axis:])


ORDER = ["qi", "kw", "ks", "qs", "vs", "kd", "qd", "vd"]
UNITS = [(k, i) for k in ORDER for i in range(TILES)]
NORMED = ("ks", "qs", "kd", "qd")
TURNED = ("qi", "kw") + NORMED
STORED = ("kw", "ks", "kd", "vs", "vd")
WIDTH = {k: W for k in ORDER} | {"kw": DH + H}


def is_turned(unit):
    return unit[0] in TURNED and (unit[1] < NT or unit[0] in ("qi", "kw"))


def turned_before(u):
    return sum(is_turned(v) for v in UNITS[:u])


def normed_before(u):
    return sum(k in NORMED for k, _ in UNITS[:u])


def small_product(nc, bank, xT, w, steps):
    for j in range(steps):
        for g in range(NB):
            last = nc.tensor.matmul(bank[32 * g:32 * g + NS, 0:128], xT[:, j, 0:NS], w[:, j, 128 * g:128 * g + 128],
                                    start=j == 0, stop=j == steps - 1)
    return last


def normalise_inputs(nc, io, s):
    with ExitStack() as ctx:
        sq = ctx.enter_context(nc.sbuf_tensor("n_sq", [128, D], F32))
        ms = ctx.enter_context(nc.sbuf_tensor("n_ms", [128, TILES], F32))
        rs = ctx.enter_context(nc.sbuf_tensor("n_rs", [128, TILES], F32))
        xn = ctx.enter_context(nc.sbuf_tensor("n_xn", [128, 2, D], F32))
        tp = ctx.enter_context(nc.psum_tensor("n_tp", [128, 2, 4, 128], F32))
        sem = lambda n: ctx.enter_context(nc.semaphore("n_" + n))
        x_in = [sem("x_first"), sem("x_rest")]
        consts_in, x_sq, x_scaled, turned, evicted, tables_in, scales = map(
            sem, ["consts_in", "x_sq", "x_scaled", "turned", "evicted", "tables_in", "scales"])
        block = ctx.enter_context(nc.Block())

        @block.sync
        def _(sp):
            sp.dma_start(s.x[:, 0, :], io["x_prompt"][0, 0:128, :]).then_inc(x_in[0], 16)
            sp.dma_start(s.c[:], io["consts"]).then_inc(consts_in, 16)
            sp.dma_start(s.gmix[:], io["g_mix"][0].rearrange("(j p) -> p j", p=128), allow_slow_non_contiguous=True).then_inc(consts_in, 16)
            sp.dma_start(s.x[:, 1:NT, :], io["x_prompt"][0, 128:SEQ, :].rearrange("(i p) d -> p i d", p=128)).then_inc(x_in[1], 16)
            sp.dma_start(s.x[0:NS, NT, :], io["x_sample"][:, 0, :]).then_inc(x_in[1], 16)
            sp.dma_start(s.rope[:], io["rope"]).then_inc(tables_in, 16)
            for n, g in enumerate(("g_k_dsa", "g_q_dsa", "g_k_diff", "g_q_diff")):
                sp.dma_start(s.gains[:, n, :], io[g].to_broadcast([128, DH])).then_inc(tables_in, 16)
            for n in range(2):
                k = ORDER[n]
                sp.dma_start(s.w[:, n, :, 0:WIDTH[k]], io["w_in"][0][:, OFF[k]:OFF[k] + WIDTH[k]]
                             .rearrange("(j p) c -> p j c", p=128)).then_inc(s.w_in[n], 16)

        @block.scalar
        def _(act):
            for i, p in enumerate(ROWS):
                act.wait_ge(x_in[i > 0], 32 if i else 16)
                if i:
                    act.wait_ge(x_sq, i)
                nc.scalar.activation(sq[0:p, :], s.x[0:p, i, :], ACT.Square, accum_out=ms[0:p, i:i + 1]).then_inc(x_sq, 1)

        @block.gpsimd
        def _(pool):
            pool.wait_ge(consts_in, 32)
            for i, p in enumerate(ROWS):
                pool.wait_ge(x_sq, i + 1)
                nc.gpsimd.tensor_scalar(rs[0:p, i:i + 1], ms[0:p, i:i + 1], 1.0 / D, EPS, ALU.mult, ALU.add).then_inc(scales, 1)
                pool.wait_ge(scales, 2 * i + 1)
                nc.gpsimd.tensor_tensor(rs[0:p, i:i + 1], rs[0:p, i:i + 1], s.c[0:p, C_MH:C_MH + 1], ALU.pow).then_inc(scales, 1)

        @block.vector
        def _(dve):
            for i, p in enumerate(ROWS):
                dve.wait_ge(x_in[i > 0], 32 if i else 16)
                dve.wait_ge(scales, 2 * i + 2)
                if i >= 2:
                    dve.wait_ge(turned, 2 * (i - 1))
                nc.vector.tensor_scalar(xn[0:p, i % 2, :], s.x[0:p, i, :], rs[0:p, i:i + 1], None, ALU.mult).then_inc(x_scaled, 1)
                if i:
                    dve.wait_ge(tables_in, 80)
                    for e in range(2):
                        nc.vector.tensor_tensor(s.rg[:, i - 1, e], s.rope[:, e], bcast(s.gains[:, i - 1, :], TILES, 1), ALU.mult)
                for h in range(2):
                    dve.wait_ge(turned, 2 * i + h + 1)
                    nc.vector.tensor_tensor(s.xT[:, 4 * h:4 * h + 4, 128 * i:128 * i + p], tp[:, h, :, 0:p],
                                            bcast(s.gmix[:, 4 * h:4 * h + 4], p, 2), ALU.mult).then_inc(evicted, 1)

        @block.tensor
        def _(pe):
            pe.wait_ge(consts_in, 32)
            for i, p in enumerate(ROWS):
                pe.wait_ge(x_scaled, i + 1)
                for h in range(2):
                    if i:
                        pe.wait_ge(evicted, 2 * (i - 1) + h + 1)
                    for j in range(4):
                        last = nc.tensor.transpose(tp[:, h, j, 0:p], xn[0:p, i % 2, (4 * h + j) * 128:(4 * h + j + 1) * 128],
                                                   s.ident[0:p, 0:p])
                    last.then_inc(turned, 1)


IDX_FROM = 12
IDX_STEPS = [(t, h) for t in range(1, NT) for h in range(H)]
TK_ROUNDS = TOPK // 8


def project(nc, io, s):
    U = len(UNITS)
    with ExitStack() as ctx:
        sb = lambda n, sh, dt=F32: ctx.enter_context(nc.sbuf_tensor("p_" + n, sh, dt))
        ps = lambda n, sh: ctx.enter_context(nc.psum_tensor("p_" + n, sh, F32))
        sem = lambda n: ctx.enter_context(nc.semaphore("p_" + n))
        sq = sb("sq", [128, 2, W])
        ms, rs = sb("ms", [128, 2, H]), sb("rs", [128, 2, H])
        t0, ta, tb = sb("t0", [128, W]), sb("ta", [128, W]), sb("tb", [128, W])
        y = sb("y", [128, 4, W])
        qiT, kiT = sb("qiT", [128, NB, SEQ]), sb("kiT", [128, SEQ])
        kiTs = sb("kiTs", [128, NS])
        wi = sb("wi", [128, TILES, H])
        relu = sb("relu", [128, 2, W])
        m8 = sb("m8", [128, 8])
        score, score_s = [t for t in s.sel[1:]], s.sel_s
        zs = sb("zs", [NS, W])
        pages_i = s.oT["d"][:].rearrange("p j t -> p (j t)")[:, 0:NS * NPAGE * DH].rearrange("p (b n d) -> p b n d", b=NS, n=NPAGE)
        kTi = s.oT["s"][0:DH].rearrange("p j t -> p (j t)")[:, 0:2 * PAST].rearrange("p (a k) -> p a k", a=2)
        qblk = sb("qblk", [DH, 72 * NS])
        relu_s = sb("relu_s", [64, PAST + 1])
        wcol, wtmp, ew = sb("wcol", [64, 1]), sb("wtmp", [64, H]), sb("ew", [64, NS])
        ptab = sb("ptab", [1, NS * NPAGE], I32)
        z = [ps(f"z{n}", [128, W]) for n in range(3)]
        tp = [ps(f"tp{n}", [128, W]) for n in range(2)]
        xs = [ps(f"xs{n}", [128, W]) for n in range(2)]
        ss = ps("ss", [64, PAST])
        (proj, z_free, squared, ms_ready, rs_ready, y_ready, turned, turn_out, pool_chain, chain, x_ready, x_free, relu_done, relu_used,
         wi_ready, ptab_in, pages_in, kTi_ready, ss_ready, samp, blk0, zs_ready) = map(sem, (
             "proj z_free squared ms_ready rs_ready y_ready turned turn_out pool_chain chain x_ready x_free relu_done "
             "relu_used wi_ready ptab_in pages_in kTi_ready ss_ready samp blk0 zs_ready").split())
        stored = [sem(f"stored{n}") for n in range(4)]
        v_stored, zeroed, rest_zeroed = sem("v_stored"), sem("zeroed"), sem("rest_zeroed")
        zero = s.oT["s"][:].rearrange("p j t -> p (j t)")[:, 2 * PAST:2 * PAST + 256]
        block = ctx.enter_context(nc.Block())
        extras = {IDX_FROM + n // 2: IDX_STEPS[n:n + 2] for n in range(0, len(IDX_STEPS), 2)}
        SAMPLE_AT = IDX_FROM + len(IDX_STEPS) // 2
        y_of = {}
        slot_stores = [0, 0, 0, 0]
        for u, (k, i) in enumerate(UNITS):
            if k in STORED and k[0] == "k":
                slot_stores[u % 4] += 1
            y_of[u] = slot_stores[u % 4]
        out_of = dict(kw="ki", ks="ks", kd="kd", vs="vs", vd="vd")

        @block.sync
        def _(sp):
            sp.dma_start(ptab[:], io["page_table"].rearrange("b n -> (b n)").unsqueeze(0)).then_inc(ptab_in, 16)
            sp.wait_ge(ptab_in, 16)
            n_v = 0
            for b in range(NS):
                for n in range(NPAGE):
                    page = sp.value_load(ptab[0:1, b * NPAGE + n:b * NPAGE + n + 1], min_val=0, max_val=s.pool - 1)
                    sp.dma_start(pages_i[:, b, n, :], io["cache_idx_k"][0, page]).then_inc(pages_in, 16)
            for u, (k, i) in enumerate(UNITS):
                p = ROWS[i]
                if k in STORED:
                    sp.wait_ge(y_ready, u + 1)
                    dst = io["new_%s_%s" % (out_of[k], "p" if i < NT else "s")]
                    dst = dst[128 * i:128 * i + p] if i < NT else dst[:]
                    if k[0] == "v":
                        sp.dma_start(dst, s.v[k][:, i, :] if i < NT else s.row[k][:]).then_inc(v_stored, 16)
                        n_v += 1
                    else:
                        n = DH if k == "kw" else W
                        sp.dma_start(dst, y[0:p, u % 4, 0:n]).then_inc(stored[u % 4], 16)
                c = u // TILES
                if i == NT and c + 2 < len(ORDER):
                    sp.wait_ge(proj, u + 1)
                    k2 = ORDER[c + 2]
                    sp.dma_start(s.w[:, c % 2, :, 0:WIDTH[k2]], io["w_in"][0][:, OFF[k2]:OFF[k2] + WIDTH[k2]]
                                 .rearrange("(j p) c -> p j c", p=128)).then_inc(s.w_in[c % 2], 16)
            for n in range(4):
                sp.wait_ge(stored[n], 16 * slot_stores[n])
            sp.wait_ge(v_stored, 16 * n_v)

        @block.tensor
        def _(pe):
            nt = ne = 0

            def turn(u):
                nonlocal nt
                if u < 0 or not is_turned(UNITS[u]):
                    return
                k, i = UNITS[u]
                p = ROWS[i]
                pe.wait_ge(y_ready, u + 1)
                if nt >= 2:
                    pe.wait_ge(turn_out, nt - 1)
                bank = tp[nt % 2]
                if k == "qi" and i == NT:
                    for h in range(H):
                        last = nc.tensor.transpose(bank[0:DH, NS * h:NS * h + NS], y[0:p, u % 4, DH * h:DH * h + DH], s.ident[0:p, 0:p])
                else:
                    for j in range(1 if k == "kw" else NB):
                        last = nc.tensor.transpose(bank[:, p * j:p * j + p], y[0:p, u % 4, 128 * j:128 * j + 128], s.ident[0:p, 0:p])
                last.then_inc(turned, 1)
                nt += 1

            def take_bank():
                nonlocal ne
                n_p = len(IDX_STEPS)
                if 2 <= ne < n_p + 2:
                    pe.wait_ge(x_free, ne - 1)
                elif n_p + 2 <= ne < n_p + NS + 2:
                    pe.wait_ge(kTi_ready, ne - 1 - n_p)
                elif ne >= n_p + NS + 2:
                    pe.wait_ge(x_free, ne - 1 - NS)
                ne += 1
                return xs[(ne - 1) % 2]

            for u in range(U + 2):
                if u < U:
                    k, i = UNITS[u]
                    c, p = u // TILES, ROWS[i]
                    if i == 0:
                        pe.wait_ge(s.w_in[c % 2], 16 * (c // 2 + 1))
                    if u >= 3:
                        pe.wait_ge(z_free, u - 2)
                    if i == NT and k != "kw":
                        last = small_product(nc, z[u % 3], s.xT[:, :, SEQ:TOK], s.w[:, c % 2], KD)
                    else:
                        for j in range(KD):
                            last = nc.tensor.matmul(z[u % 3][0:p, 0:WIDTH[k]], s.xT[:, j, 128 * i:128 * i + p],
                                                    s.w[:, c % 2, j, 0:WIDTH[k]], start=j == 0, stop=j == KD - 1)
                    last.then_inc(proj, 1)
                turn(u - 2)
                if u == IDX_FROM:
                    pe.wait_ge(turn_out, turned_before(2 * TILES))
                for t, h in extras.get(u, ()):
                    bank, r = take_bank(), 64 * (h % 2)
                    nc.tensor.matmul(bank[:, 0:128 * (t + 1)], qiT[r:r + 64, h // 2, 128 * t:128 * t + 128],
                                     kiT[r:r + 64, 0:128 * (t + 1)], start=True, stop=True).then_inc(x_ready, 1)
                if u == SAMPLE_AT:
                    pe.wait_ge(pages_in, 16 * NS * NPAGE)
                    pe.wait_ge(blk0, 2)
                    for step in range(NS + 1):
                        if step < NS:
                            bank = take_bank()
                            for n in range(NPAGE):
                                last = nc.tensor.transpose(bank[0:DH, 128 * n:128 * n + 128], pages_i[:, step, n, :], s.ident[:])
                            last.then_inc(x_ready, 1)
                        if step == 0:
                            continue
                        b = step - 1
                        pe.wait_ge(kTi_ready, b + 1)
                        last = nc.tensor.matmul(ss[:], qblk[:, 64 * b:64 * b + 64], kTi[:, b % 2, :], start=b == 0, stop=b == NS - 1)
                        last.then_inc(ss_ready, 1)
                    bank = take_bank()
                    for b in range(NS):
                        nc.tensor.matmul(bank[0:64, 0:1], qblk[:, 64 * b:64 * b + 64], kiTs[0:DH, b:b + 1], start=b == 0, stop=b == NS - 1)
                    pe.wait_ge(wi_ready, TILES)
                    nc.tensor.matmul(bank[0:64, 8:16], s.c[0:NS, C_E:C_ET], wi[0:NS, NT, :], start=True, stop=True).then_inc(x_ready, 1)
                if u == SAMPLE_AT + 1:
                    pe.wait_ge(samp, 3)
                    bank = take_bank()
                    nc.tensor.matmul(bank[0:NS, :], ew[:], relu_s[:, 0:PAST], start=True, stop=True).then_inc(x_ready, 1)
                    bank = take_bank()
                    nc.tensor.matmul(bank[0:NS, 0:1], ew[:], relu_s[:, PAST:PAST + 1], start=True, stop=True).then_inc(x_ready, 1)

        @block.scalar
        def _(act):
            ns = nt = nx = nz = 0
            for u in range(U + 2):
                if u < U and UNITS[u][1] == NT and UNITS[u][0] != "kw":
                    act.wait_ge(proj, u + 1)
                    if u >= TILES:
                        act.wait_ge(y_ready, u - TILES + 1)
                    for g in range(NB):
                        nc.scalar.copy(zs[:, 128 * g:128 * g + 128], z[u % 3][32 * g:32 * g + NS, 0:128]).then_inc(zs_ready, 1)
                    nz += NB
                    act.wait_ge(zs_ready, nz)
                if u < U and UNITS[u][0] in NORMED:
                    p = ROWS[UNITS[u][1]]
                    act.wait_ge(proj, u + 1)
                    if ns >= 2:
                        act.wait_ge(ms_ready, ns - 1)
                    nc.scalar.activation(sq[0:p, ns % 2, :], (z[u % 3][0:p, :] if p > NS else zs[:]), ACT.Square).then_inc(squared, 1)
                    ns += 1
                v = u - 2
                if v >= 0 and is_turned(UNITS[v]):
                    k, i = UNITS[v]
                    p = ROWS[i]
                    act.wait_ge(turned, nt + 1)
                    bank = tp[nt % 2]
                    if k == "kw":
                        ins = nc.scalar.copy(kiT[:, 128 * i:128 * i + 128] if i < NT else kiTs[:], bank[:, 0:p])
                    elif k == "qi" and i == NT:
                        act.wait_ge(blk0, 1)
                        ins = nc.scalar.copy(qblk[:].rearrange("d (b c) -> d b c", c=72)[:, :, 0:H],
                                             bank[0:DH, 0:NS * H].rearrange("d (h b) -> d b h", h=H))
                        ins.then_inc(blk0, 1)
                    else:
                        dst = (qiT if k == "qi" else s.T[k])[:, :, 128 * i:128 * i + p]
                        ins = nc.scalar.copy(dst, bank[:, 0:NB * p].rearrange("f (j t) -> f j t", j=NB))
                    if not (k == "qi" and i == NT):
                        ins.then_inc(turn_out, 1)
                    else:
                        act.wait_ge(blk0, 2)
                        act.sem_inc(turn_out, 1)
                    nt += 1
                for t, h in extras.get(u, ()):
                    act.wait_ge(x_ready, nx + 1)
                    if nx >= 2:
                        act.wait_ge(relu_used, nx - 1)
                    n = 128 * (t + 1)
                    nc.scalar.activation(relu[:, nx % 2, 0:n], xs[nx % 2][:, 0:n], ACT.Relu, scale=DH ** -0.5).then_inc(relu_done, 1)
                    nx += 1
                if u == SAMPLE_AT:
                    for b in range(NS):
                        act.wait_ge(x_ready, nx + 1)
                        if b >= 2:
                            act.wait_ge(ss_ready, b - 1)
                        nc.scalar.copy(kTi[:, b % 2, :], xs[nx % 2][0:DH, :]).then_inc(kTi_ready, 1)
                        nx += 1
                    act.wait_ge(ss_ready, NS)
                    nc.scalar.activation(relu_s[:, 0:PAST], ss[:], ACT.Relu, scale=DH ** -0.5).then_inc(samp, 1)
                    act.wait_ge(x_ready, nx + 1)
                    nc.scalar.activation(relu_s[:, PAST:PAST + 1], xs[nx % 2][0:64, 0:1], ACT.Relu, scale=DH ** -0.5).then_inc(samp, 1)

        @block.gpsimd
        def _(pool):
            n = 0
            nc.gpsimd.memset(qblk[:], 0.0).then_inc(blk0, 1)
            nc.gpsimd.memset(zero, 0.0).then_inc(zeroed, 1)
            pool.wait_ge(zeroed, 1)
            rest = s.eout[NE * CAP:NBLK * CAP, :].rearrange("(p r) (q c) -> p (r q) c", p=128, c=256)
            pool.dma_start(rest, bcast(zero, rest.shape[1], 1)).then_inc(rest_zeroed, 16)
            for u, (k, i) in enumerate(UNITS):
                if k in NORMED:
                    p = ROWS[i]
                    pool.wait_ge(ms_ready, n + 1)
                    if n >= 2:
                        pool.wait_ge(z_free, u - 1)
                    nc.gpsimd.tensor_scalar(rs[0:p, n % 2, :], ms[0:p, n % 2, :], 1.0 / DH, EPS, ALU.mult, ALU.add).then_inc(pool_chain, 1)
                    pool.wait_ge(pool_chain, n + 1)
                    nc.gpsimd.tensor_tensor(rs[0:p, n % 2, :], rs[0:p, n % 2, :], s.c[0:p, C_MH:C_MH + H], ALU.pow).then_inc(rs_ready, 1)
                    n += 1
            pool.wait_ge(rest_zeroed, 16)

        @block.vector
        def _(dve):
            link = Chain(dve, chain)
            nm = nr = nx = 0
            nturn = 0
            heads = lambda ap: ap.rearrange("p (h d) -> p h d", h=H)

            def sums(u):
                nonlocal nm
                k, i = UNITS[u]
                if k in NORMED:
                    p = ROWS[i]
                    dve.wait_ge(squared, nm + 1)
                    if nm >= 2:
                        dve.wait_ge(rs_ready, nm - 1)
                    nc.vector.tensor_reduce(ms[0:p, nm % 2, :], heads(sq[0:p, nm % 2, :]), AX.X, ALU.add).then_inc(ms_ready, 1)
                    nm += 1

            def finish(u):
                nonlocal nr
                k, i = UNITS[u]
                p = ROWS[i]
                bank = z[u % 3]
                dve.wait_ge(proj, u + 1)
                if i == NT and k != "kw":
                    bank = zs
                    dve.wait_ge(zs_ready, NB * sum(j == NT and q != "kw" for q, j in UNITS[:u + 1]))
                if u >= 4:
                    dve.wait_ge(turned, turned_before(u - 3))
                    if y_of[u - 4]:
                        dve.wait_ge(stored[u % 4], 16 * y_of[u - 4])
                if k[0] == "v":
                    nc.vector.tensor_copy(s.v[k][:, i, :] if i < NT else s.row[k][:], bank[0:p, :]).then_inc(z_free, 1)
                    dve.wait_ge(z_free, u + 1)
                    dve.sem_inc(y_ready, 1)
                    return
                if k == "kw":
                    n, hh = DH, 1
                    src = bank[0:p, 0:DH].unsqueeze(1)
                    cos, sin = s.rope[0:p, 0, i, :], s.rope[0:p, 1, i, :]
                elif k == "qi":
                    n, hh = W, H
                    src = heads(bank[0:p, :])
                    cos, sin = s.rope[0:p, 0, i, :], s.rope[0:p, 1, i, :]
                else:
                    n, hh = W, H
                    g = ("ks", "qs", "kd", "qd").index(k)
                    cos, sin = s.rg[0:p, g, 0, i, :], s.rg[0:p, g, 1, i, :]
                    dve.wait_ge(rs_ready, nr + 1)
                    nc.vector.tensor_tensor(heads(t0[0:p, :]), heads(bank[0:p, :]), bcast(rs[0:p, nr % 2, :], DH, 2), ALU.mult).then_inc(z_free, 1)
                    dve.wait_ge(z_free, u + 1)
                    nr += 1
                    src = heads(t0[0:p, :])
                va = ta[0:p, 0:n].rearrange("p (h d) -> p h d", h=hh)
                vb = tb[0:p, 0:n].rearrange("p (h d) -> p h d", h=hh)
                vy = y[0:p, u % 4, 0:n].rearrange("p (h d) -> p h d", h=hh)
                nc.vector.tensor_tensor(va, src, bcast(cos, hh, 1), ALU.mult)
                if k == "kw":
                    nc.vector.tensor_scalar(wi[0:p, i, :], bank[0:p, DH:DH + H], float(np.float32(H ** -0.5)), None, ALU.mult).then_inc(wi_ready, 1)
                last = nc.vector.tensor_tensor(vb, src, bcast(sin, hh, 1), ALU.mult)
                if k in NORMED:
                    link(last)
                else:
                    last.then_inc(z_free, 1)
                    dve.wait_ge(z_free, u + 1)
                hd = DH // 2
                link(nc.vector.tensor_tensor(vy[:, :, 0:hd], va[:, :, 0:hd], vb[:, :, hd:DH], ALU.subtract))
                link(nc.vector.tensor_tensor(vy[:, :, hd:DH], va[:, :, hd:DH], vb[:, :, 0:hd], ALU.add))
                if k == "kw":
                    link(nc.vector.tensor_copy(y[0:p, u % 4, DH:2 * DH], y[0:p, u % 4, 0:DH]))
                if i == NT and k in NORMED:
                    link(nc.vector.tensor_copy(s.row[k][:], y[0:NS, u % 4, :]))
                dve.sem_inc(y_ready, 1)

            rounds = []

            def take8(buf):
                link(nc.vector.max(m8[0:buf.shape[0], :], buf))
                link(nc.vector.match_replace(buf, m8[0:buf.shape[0], :], buf, TAKEN))

            for u in range(U + 1):
                if u < U:
                    sums(u)
                if u >= 1:
                    finish(u - 1)
                for t, h in extras.get(u, ()):
                    n = 128 * (t + 1)
                    if nx == 0:
                        dve.wait_ge(wi_ready, TILES)
                    dve.wait_ge(relu_done, nx + 1)
                    acc = score[t - 1]
                    ins = nc.vector.scalar_tensor_tensor(acc[:], relu[:, nx % 2, 0:n], wi[:, t, h:h + 1],
                                                         s.c[:, C_E - n:C_E] if h == 0 else acc[:], ALU.mult, ALU.add)
                    ins.then_inc(relu_used, 1)
                    dve.wait_ge(relu_used, nx + 1)
                    dve.sem_inc(x_free, 1)
                    nx += 1
                    if h == H - 1:
                        rounds += [score[t - 1][:]] * TK_ROUNDS
                if u == SAMPLE_AT:
                    nx += NS
                    dve.wait_ge(x_ready, nx + 1)
                    dve.wait_ge(samp, 2)
                    link(nc.vector.tensor_tensor(wtmp[:], xs[nx % 2][0:64, 8:16], s.c[0:64, C_HM:C_IOTA], ALU.mult))
                    link(nc.vector.tensor_reduce(wcol[:], wtmp[:], AX.X, ALU.add))
                    link(nc.vector.tensor_scalar(ew[:], s.c[0:64, C_ET:C_HM], wcol[:], None, ALU.mult))
                    dve.sem_inc(samp, 1)
                    dve.sem_inc(x_free, 1)
                if u == SAMPLE_AT + 1:
                    dve.wait_ge(x_ready, nx + 2)
                    link(nc.vector.tensor_copy(score_s[:, 0:PAST], xs[(nx + 1) % 2][0:NS, :]))
                    dve.wait_ge(x_ready, nx + 3)
                    link(nc.vector.tensor_copy(score_s[:, PAST:PAST + 1], xs[nx % 2][0:NS, 0:1]))
                    rounds += [score_s[:]] * TK_ROUNDS
                for _ in range(3):
                    if rounds:
                        take8(rounds.pop(0))
            while rounds:
                take8(rounds.pop(0))
            for t in range(1, NT):
                nc.vector.tensor_scalar(score[t - 1][:], score[t - 1][:], TAKEN, MASKED, ALU.not_equal, ALU.mult)
            nc.vector.tensor_scalar(score_s[:], score_s[:], TAKEN, MASKED, ALU.not_equal, ALU.mult)


KQV = dict(d=("qd", "kd", "vd"), s=("qs", "ks", "vs"))
A_UNITS = [(t, kind, h) for t in range(NT) for kind in "ds" for h in range(H)]
JOBS = [(t, kind, h if kind == "s" else h // 2, n) for n, (t, kind, h) in enumerate(A_UNITS) if kind == "s" or h % 2]
JOB_OF = {n: next(q for q, j in enumerate(JOBS) if j[3] >= n) for n in range(len(A_UNITS))}
LAG = 3


def attend_prompt(nc, io, s):
    UN, JN = len(A_UNITS), len(JOBS)
    with ExitStack() as ctx:
        sb = lambda n, sh, dt=F32: ctx.enter_context(nc.sbuf_tensor("a_" + n, sh, dt))
        ps = lambda n, sh: ctx.enter_context(nc.psum_tensor("a_" + n, sh, F32))
        sem = lambda n: ctx.enter_context(nc.semaphore("a_" + n))
        lams, lprod, lsum, lexp = sb("lams", [128, 4, DH]), sb("lprod", [128, 2, DH]), sb("lsum", [128, 2]), sb("lexp", [128, 2])
        masked, prob, mix, pT = sb("masked", [128, 3, W]), sb("prob", [128, 4, W]), sb("mix", [128, 2, W]), sb("pT", [128, 2, W])
        scaled = sb("scaled", [128, W])
        mx, nb, sums, inv = (sb(n, [128, UN]) for n in ("mx", "nb", "sums", "inv"))
        osq, on = sb("osq", [128, W]), sb("on", [128, 2, W])
        oms, ors = sb("oms", [128, 4]), sb("ors", [128, 4])
        S = [ps(f"S{n}", [128, W]) for n in range(3)]
        T = [ps(f"T{n}", [128, W]) for n in range(2)]
        O = [ps(f"O{n}", [128, W]) for n in range(2)]
        OT = ps("OT", [128, W])
        (lams_in, lam_sum, lam_exp, chain, scored, max_ready, p_ready, combined, turned, copied, pv_done, o_sq, o_ms, o_rs,
         pool_chain, o_ready, o_turned, o_done) = map(sem, (
             "lams_in lam_sum lam_exp chain scored max_ready p_ready combined turned copied pv_done o_sq o_ms o_rs "
             "pool_chain o_ready o_turned o_done").split())
        block = ctx.enter_context(nc.Block())
        pairs_before = lambda n: sum(k == "d" and h % 2 for _, k, h in A_UNITS[:n])
        last_job = {g: max(q for q, j in enumerate(JOBS) if 2 * j[0] + (j[1] == "s") == g) for g in range(2 * NT)}

        @block.sync
        def _(sp):
            for n, l in enumerate(("lam_q1", "lam_q2", "lam_k1", "lam_k2")):
                sp.dma_start(lams[:, n, :], io[l].to_broadcast([128, DH])).then_inc(lams_in, 16)
            sp.dma_start(s.gsub[:], io["g_subln"].rearrange("a p -> p a"), allow_slow_non_contiguous=True).then_inc(lams_in, 16)
            for n, k in enumerate(("gd", "gs")):
                sp.dma_start(s.w[:, n], io["w_in"][0][:, OFF[k]:OFF[k] + W].rearrange("(j p) c -> p j c", p=128)).then_inc(s.w_in[n], 16)

        @block.tensor
        def _(pe):
            def turn(q):
                t, kind, h, n = JOBS[q]
                if kind == "d":
                    pe.wait_ge(combined, pairs_before(n + 1))
                    src = mix[:, (pairs_before(n + 1) - 1) % 2, :]
                else:
                    pe.wait_ge(p_ready, n + 1)
                    src = prob[:, n % 4, :]
                if q >= 2:
                    pe.wait_ge(copied, q - 1)
                for b in range(t + 1):
                    last = nc.tensor.transpose(T[q % 2][:, 128 * b:128 * b + 128], src[:, 128 * b:128 * b + 128], s.ident[:])
                last.then_inc(turned, 1)

            def values(q):
                t, kind, h, n = JOBS[q]
                g = 2 * t + (kind == "s")
                pe.wait_ge(copied, q + 1)
                if h == 0 and g >= 2:
                    pe.wait_ge(o_ready, g - 1)
                w = W // (4 if kind == "d" else 8)
                for b in range(t + 1):
                    last = nc.tensor.matmul(O[g % 2][:, w * h:w * h + w], pT[:, q % 2, 128 * b:128 * b + 128],
                                            s.v[KQV[kind][2]][:, b, w * h:w * h + w], start=b == 0, stop=b == t)
                last.then_inc(pv_done, 1)

            def turn_output(g):
                pe.wait_ge(o_ready, g + 1)
                if g:
                    pe.wait_ge(o_done, g)
                for j in range(NB):
                    last = nc.tensor.transpose(OT[:, 128 * j:128 * j + 128], on[:, g % 2, 128 * j:128 * j + 128], s.ident[:])
                last.then_inc(o_turned, 1)

            q = 0
            late = {}
            for n in range(UN + LAG + 1):
                if n < UN:
                    t, kind, h = A_UNITS[n]
                    kq, kk, _ = KQV[kind]
                    r = 64 * (h % 2)
                    if n >= 3:
                        pe.wait_ge(max_ready, n - 2)
                    nc.tensor.matmul(S[n % 3][:, 0:128 * (t + 1)], s.T[kq][r:r + 64, h // 2, 128 * t:128 * t + 128],
                                     s.T[kk][r:r + 64, h // 2, 0:128 * (t + 1)], start=True, stop=True).then_inc(scored, 1)
                while q < JN and JOBS[q][3] <= n - LAG:
                    turn(q)
                    if q:
                        values(q - 1)
                    q += 1
                    for g in [g for g in range(2 * NT) if last_job[g] == q - 4]:
                        turn_output(g)
            values(JN - 1)
            for g in [g for g in range(2 * NT) if last_job[g] > JN - 4]:
                turn_output(g)

        @block.scalar
        def _(act):
            act.wait_ge(lam_sum, 1)
            nc.scalar.activation(lexp[:], lsum[:], ACT.Exp).then_inc(lam_exp, 1)
            q = 0

            def copy(q):
                t = JOBS[q][0]
                act.wait_ge(turned, q + 1)
                if q >= 2:
                    act.wait_ge(pv_done, q - 1)
                nc.scalar.copy(pT[:, q % 2, 0:128 * (t + 1)], T[q % 2][:, 0:128 * (t + 1)]).then_inc(copied, 1)

            def square(g):
                act.wait_ge(pv_done, last_job[g] + 1)
                if g >= 2:
                    act.wait_ge(o_ms, g // 2)
                nc.scalar.activation(osq[:], O[g % 2][:], ACT.Square).then_inc(o_sq, 1)

            for n in range(UN + LAG + 1):
                if n < UN:
                    t, kind, h = A_UNITS[n]
                    act.wait_ge(max_ready, n + 1)
                    if n >= 4:
                        if A_UNITS[n - 4][1] == "d":
                            act.wait_ge(combined, pairs_before(n - 3) + (A_UNITS[n - 4][2] % 2 == 0))
                        else:
                            act.wait_ge(turned, JOB_OF[n - 4] + 1)
                    w = 128 * (t + 1)
                    nc.scalar.activation(prob[:, n % 4, 0:w], masked[:, n % 3, 0:w], ACT.Exp, bias=nb[:, n:n + 1], scale=DH ** -0.5,
                                         accum_out=sums[:, n:n + 1]).then_inc(p_ready, 1)
                while q < JN and JOBS[q][3] <= n - LAG:
                    copy(q)
                    q += 1
                    for g in [g for g in range(0, 2 * NT, 2) if last_job[g] == q - 3]:
                        square(g)

        @block.gpsimd
        def _(pool):
            for t in range(NT):
                pool.wait_ge(o_ms, t + 1)
                if t:
                    pool.wait_ge(o_ready, 2 * t - 1)
                nc.gpsimd.tensor_scalar(ors[:], oms[:], 1.0 / (2 * DH), EPS, ALU.mult, ALU.add).then_inc(pool_chain, 1)
                pool.wait_ge(pool_chain, t + 1)
                nc.gpsimd.tensor_tensor(ors[:], ors[:], s.c[:, C_MH:C_MH + 4], ALU.pow).then_inc(o_rs, 1)

        @block.vector
        def _(dve):
            link = Chain(dve, chain)
            dve.wait_ge(lams_in, 80)
            link(nc.vector.tensor_tensor(lprod[:], lams[:, 0:2, :], lams[:, 2:4, :], ALU.mult))
            nc.vector.tensor_reduce(lsum[:], lprod[:], AX.X, ALU.add).then_inc(lam_sum, 1)
            dve.wait_ge(lam_exp, 1)
            link(nc.vector.tensor_tensor(s.neglam[:], lexp[:, 1:2], lexp[:, 0:1], ALU.subtract))
            link(nc.vector.tensor_scalar(s.neglam[:], s.neglam[:], -LAM_INIT, None, ALU.add))
            link(nc.vector.tensor_scalar(s.gsub[:], s.gsub[:], 1.0 - LAM_INIT, None, ALU.mult))

            def combine(n):
                t, w = A_UNITS[n][0], 128 * (A_UNITS[n][0] + 1)
                m = pairs_before(n + 1)
                dve.wait_ge(p_ready, n + 1)
                if m > 2:
                    q2 = [q for q, j in enumerate(JOBS) if j[1] == "d"][m - 3]
                    dve.wait_ge(turned, q2 + 1)
                link(nc.vector.reciprocal(inv[:, n - 1:n + 1], sums[:, n - 1:n + 1]))
                link(nc.vector.tensor_scalar(inv[:, n:n + 1], inv[:, n:n + 1], s.neglam[:], None, ALU.mult))
                link(nc.vector.tensor_scalar(scaled[:, 0:w], prob[:, n % 4, 0:w], inv[:, n:n + 1], None, ALU.mult))
                nc.vector.scalar_tensor_tensor(mix[:, (m - 1) % 2, 0:w], prob[:, (n - 1) % 4, 0:w], inv[:, n - 1:n], scaled[:, 0:w],
                                               ALU.mult, ALU.add).then_inc(combined, 1)

            def output(g):
                t, d = g // 2, g % 2 == 0
                if d:
                    dve.wait_ge(o_sq, t + 1)
                    nc.vector.tensor_reduce(oms[:], osq[:].rearrange("p (h e) -> p h e", h=4), AX.X, ALU.add).then_inc(o_ms, 1)
                    dve.wait_ge(o_rs, t + 1)
                    scale, w = ors[:], 2 * DH
                else:
                    dve.wait_ge(pv_done, last_job[g] + 1)
                    n = 16 * t + 8
                    link(nc.vector.reciprocal(inv[:, n:n + H], sums[:, n:n + H]))
                    scale, w = inv[:, n:n + H], DH
                if g >= 2:
                    dve.wait_ge(o_turned, g - 1)
                nc.vector.tensor_tensor(on[:, g % 2, :].rearrange("p (h e) -> p h e", e=w), O[g % 2][:].rearrange("p (h e) -> p h e", e=w),
                                        bcast(scale, w, 2), ALU.mult).then_inc(o_ready, 1)

            def output_turned(g):
                t, d = g // 2, g % 2 == 0
                dve.wait_ge(o_turned, g + 1)
                dst = s.oT["ds"[g % 2]][:, :, 128 * t:128 * t + 128]
                src = OT[:].rearrange("p (j q) -> p j q", j=NB)
                if d:
                    nc.vector.tensor_scalar(dst, src, s.gsub[:], None, ALU.mult).then_inc(o_done, 1)
                else:
                    nc.vector.tensor_copy(dst, src).then_inc(o_done, 1)

            q = 0
            for n in range(UN + LAG + 1):
                if n < UN:
                    t, kind, h = A_UNITS[n]
                    w = 128 * (t + 1)
                    dve.wait_ge(scored, n + 1)
                    if n >= 3:
                        dve.wait_ge(p_ready, n - 2)
                    mask = s.sel[t][:] if kind == "s" and t else s.c[:, C_E - w:C_E]
                    link(nc.vector.tensor_tensor_reduce(out=masked[:, n % 3, 0:w], in0=S[n % 3][:, 0:w], in1=mask, scale=1.0, scalar=-3.4e38,
                                                        op0=ALU.add, op1=ALU.max, accum_out=mx[:, n:n + 1]))
                    nc.vector.tensor_scalar(nb[:, n:n + 1], mx[:, n:n + 1], -DH ** -0.5, None, ALU.mult).then_inc(max_ready, 1)
                if n >= 1 and n - 1 < UN and A_UNITS[n - 1][1] == "d" and A_UNITS[n - 1][2] % 2:
                    combine(n - 1)
                while q < JN and JOBS[q][3] <= n - LAG:
                    q += 1
                    for g in [g for g in range(2 * NT) if last_job[g] == q - 3]:
                        output(g)
                    for g in [g for g in range(2 * NT) if last_job[g] == q - 5]:
                        output_turned(g)
            for g in [g for g in range(2 * NT) if last_job[g] > JN - 3]:
                output(g)
            for g in [g for g in range(2 * NT) if last_job[g] > JN - 5]:
                output_turned(g)


PASSES = [(k, c) for c in range(2) for k in range(2)]
SLOTS_A = len(PASSES) * NT
RING = 3
PRODUCTS = [(q, i, r) for q in range(4) for i, r in [(i, r) for i in range(NT) for r in "gy"] + [(NT, "g")]]
PRODUCTS += [(q, NT, "y") for q in range(4)]
PLACES = 4
CACHE = dict(kd="cache_diff_k", ks="cache_dsa_k", vd="cache_diff_v", vs="cache_dsa_v")
KEYS_AT, VALUES_AT = {}, {}
for _k, _first, _counts in (("kd", 0, (2, 1, 2, 1, 2)), ("ks", 5, (2, 2, 1, 2, 1))):
    for _n, _c in enumerate(_counts):
        KEYS_AT[_first + _n] = (_k, list(range(sum(_counts[:_n]), sum(_counts[:_n]) + _c)))
for _b in range(NS // 2):
    VALUES_AT[7 + _b] = ("vd", [2 * _b, 2 * _b + 1])
    VALUES_AT[12 + _b] = ("vs", [2 * _b, 2 * _b + 1])
SOFTMAX_AT = {5: "d", 10: "s"}
OD_AT = 11
PAGES = []
for _sl in range(SLOTS_A):
    _v, _vb = VALUES_AT.get(_sl, ("", []))
    _k, _kb = KEYS_AT.get(_sl, ("", []))
    PAGES += [(c, b, n) for c, bs in ((_v, _vb[:1]), (_k, _kb), (_v, _vb[1:])) for b in bs for n in range(NPAGE)]
PAGES = {x: [pg for pg in PAGES if pg[0][0] == x] for x in "kv"} | dict(all=PAGES)
OUT_TILES = [0, 1, NT, 2, 3]
OUT = [("turn", 0, 0), ("turn", 0, 1), ("turn", 1, 0), ("turn", 1, 1), ("sum", 0, 0), ("extract", NT, 0), ("sum", 1, 0),
       ("branches", NT, 0), ("sum", 0, 1),
       ("turn", NT, 0), ("turn", NT, 1), ("sum", 1, 1), ("turn", 2, 0), ("turn", 2, 1), ("sum", NT, 0), ("sum", NT, 1),
       ("turn", 3, 0), ("turn", 3, 1), ("sum", 2, 0), ("sum", 2, 1), ("sum", 3, 0), ("sum", 3, 1)]


def merge(nc, io, s):
    R = NS * H
    with ExitStack() as ctx:
        sb = lambda n, sh, dt=F32: ctx.enter_context(nc.sbuf_tensor("g_" + n, sh, dt))
        ps = lambda n, sh: ctx.enter_context(nc.psum_tensor("g_" + n, sh, F32))
        sem = lambda n: ctx.enter_context(nc.semaphore("g_" + n))
        wo = [sb("wo" + k, [128, NB, D]) for k in "ds"]
        merged = sb("merged", [128, NT, D])
        merged_s = sb("merged_s", [NS, D])
        gate = sb("gate", [128, 2, W])
        gate_s = sb("gate_s", [NS, 4, W])
        branch = sb("branch", [128, W])
        ring = [ps(f"ring{n}", [128, W]) for n in range(RING)]
        B = [ps(f"B{n}", [128, W]) for n in range(2)]
        page = dict(k=sb("page_k", [128, PLACES, W]), v=sb("page_v", [128, PLACES, W]))
        ptab = sb("ptab", [1, NS * NPAGE], I32)
        prods = [sb(f"prod{n}", [128, W]) for n in range(2)]
        prod = prods[0]
        sT = {k: sb("sT" + k, [128, NPAGE, R]) for k in "ds"}
        nk, nkh, snew = sb("nk", [NS, 2, H]), sb("nkh", [R, 2, H]), sb("snew", [R, 2])
        sc, pr, selb = sb("sc", [R, PAST + 1]), sb("pr", [R, PAST + 1]), sb("selb", [R, PAST + 1])
        aZ = sb("aZ", [128, NPAGE, NS, 32])
        aN = dict(d=sb("aNd", [NS, R // 2]), s=sb("aNs", [NS, R]))
        dg = sb("dg", [R, R])
        mx, nb, sm, cf = (sb(n, [R, 2]) for n in ("mx", "nb", "sm", "cf"))
        od, oq, orr, orx = (sb(n, [128, NB * NS]) for n in ("od", "oq", "orr", "orx"))
        mh = sb("mh", [128, NB * NS])
        mT = [page["k"][:, 2 * n:2 * n + 2, :].rearrange("p a (j q) -> p (a j) q", j=4) for n in range(2)]
        S0, P, O = ps("S0", [128, W]), ps("P", [128, W]), ps("O", [128, W])
        S = [S0, P]
        (wo_in, made, g_exp, y_read, chain, merged_ready, turned, mt_out, summed, x_done, ptab_in, sel_up, sel_read, nk_ready, nk_up,
         nk_read, qb_ready, k_used, k_summed, sT_ready, sc_ready, max_ready, p_ready, weights, p_turned, a_ready, v_used, o_ready, ov_ready, ext_ready,
         oq_ready, o_sum, orr_ready, o_rs, oT_ready, ms_ready, zeros_ready) = map(sem, (
             "wo_in made g_exp y_read chain merged_ready turned mt_out summed x_done ptab_in sel_up sel_read nk_ready nk_up "
             "nk_read qb_ready k_used k_summed sT_ready sc_ready max_ready p_ready weights p_turned a_ready v_used o_ready ov_ready ext_ready "
             "oq_ready o_sum orr_ready o_rs oT_ready ms_ready zeros_ready").split())
        w_more = [sem(f"w_more{n}") for n in range(2)]
        page_in = {x: [sem(f"page_in_{x}{n}") for n in range(PLACES)] for x in "kv"}
        block = ctx.enter_context(nc.Block())
        made_after = lambda q: 9 * (q + 1)
        exps = lambda m: sum(r == "g" for _, _, r in PRODUCTS[:m])
        reads = lambda m: sum(r == "y" for _, _, r in PRODUCTS[:m])
        m_of = {pr_: m for m, pr_ in enumerate(PRODUCTS)}
        upto = lambda kind, i, h: [st for st in OUT if st[0] == kind].index((kind, i, h)) + 1
        before = lambda i, n: OUT_TILES[OUT_TILES.index(i) - n]

        @block.sync
        def _(sp):
            sp.dma_start(ptab[:], io["page_table"].rearrange("b n -> (b n)").unsqueeze(0)).then_inc(ptab_in, 16)
            sp.wait_ge(ptab_in, 16)
            ids = [sp.value_load(ptab[0:1, x:x + 1], min_val=0, max_val=s.pool - 1) for x in range(NS * NPAGE)]
            for c, b, n in PAGES["all"]:
                x = c[0]
                m = PAGES[x].index((c, b, n))
                if m >= PLACES:
                    sp.wait_ge(k_used if x == "k" else v_used, m - PLACES + 1)
                src = io[CACHE[c]][0, ids[NPAGE * b + n]]
                src = src.rearrange("p h c d -> p (h c d)") if c == "kd" else src.rearrange("p h d -> p (h d)")
                sp.dma_start(page[x][:, m % PLACES, :], src).then_inc(page_in[x][m % PLACES], 16)

        @block.gpsimd
        def _(pool):
            for k, name in enumerate(("w_o_diff", "w_o_dsa")):
                pool.dma_start(wo[k][:], io[name][0].rearrange("(j p) c -> p j c", p=128)).then_inc(wo_in, 16)
            nc.gpsimd.memset(aZ[:], 0.0).then_inc(zeros_ready, 1)
            nc.gpsimd.memset(mh[:], -0.5).then_inc(zeros_ready, 1)
            for q in range(2):
                pool.wait_ge(made, made_after(q))
                off = OFF[("gd", "gs")[q]] + W
                pool.dma_start(s.w[:, q], io["w_in"][0][:, off:off + W].rearrange("(j p) c -> p j c", p=128)).then_inc(w_more[q], 16)
            for h in range(2):
                if h == 0:
                    pool.wait_ge(v_used, NPAGE * NS)
                    nc.gpsimd.memset(aZ[:], 0.0).then_inc(zeros_ready, 1)
                if h == 1:
                    pool.wait_ge(zeros_ready, 2)
                    pool.wait_ge(orr_ready, 1)
                    nc.gpsimd.tensor_tensor(orx[:], orr[:], mh[:], ALU.pow).then_inc(o_rs, 1)
                pool.wait_ge(made, made_after(2 + h))
                pool.dma_start(s.w[:, h], io["w_out"][0][:, W * h:W * h + W].rearrange("(j p) c -> p j c", p=128)).then_inc(w_more[h], 16)

        @block.tensor
        def _(pe):
            def product(m):
                q, i, r = PRODUCTS[m]
                k, c = PASSES[q][0], PASSES[q][1]
                f = m - RING
                if f >= 0:
                    if PRODUCTS[f][2] == "g":
                        pe.wait_ge(g_exp, exps(f + 1))
                    else:
                        pe.wait_ge(y_read, reads(f + 1))
                bank = ring[m % RING]
                if r == "g":
                    if i == 0:
                        pe.wait_ge(*((s.w_in[q], 80) if q < 2 else (w_more[q - 2], 16)))
                    x, w, steps = s.xT, s.w[:, q % 2], KD
                else:
                    if m < 2 or m == 10:
                        pe.wait_ge(wo_in, 32)
                    x, w, steps = s.oT["ds"[k]], wo[k][:, :, W * c:W * c + W], NB
                if i == NT:
                    last = small_product(nc, bank, x[:, :, SEQ:TOK], w, steps)
                else:
                    for j in range(steps):
                        last = nc.tensor.matmul(bank[:], x[:, j, 128 * i:128 * i + 128], w[:, j, :], start=j == 0, stop=j == steps - 1)
                last.then_inc(made, 1)

            def turn(i, h):
                p = ROWS[i]
                src = merged[:, i] if i < NT else merged_s[:]
                if i == NT:
                    pe.wait_ge(ms_ready, 1)
                else:
                    pe.wait_ge(merged_ready, NT + i + 1)
                if i == 0:
                    pe.wait_ge(k_used, len(PAGES["k"]))
                else:
                    pe.wait_ge(mt_out, upto("turn", before(i, 1), h))
                for j in range(4):
                    last = nc.tensor.transpose(B[h][:, 128 * j:128 * j + p], src[:, 128 * (4 * h + j):128 * (4 * h + j) + 128],
                                               s.ident[0:p, 0:p])
                last.then_inc(turned, 1)

            def summing(i, h):
                pe.wait_ge(mt_out, upto("turn", i, 1))
                if i == 0:
                    pe.wait_ge(w_more[h], 32)
                else:
                    pe.wait_ge(x_done, upto("sum", before(i, 1), h))
                x = mT[OUT_TILES.index(i) % 2]
                if i == NT:
                    last = small_product(nc, S[h], x, s.w[:, h], KD)
                else:
                    for j in range(KD):
                        last = nc.tensor.matmul(S[h][:], x[:, j, :], s.w[:, h, j, :], start=j == 0, stop=j == KD - 1)
                last.then_inc(summed, 1)

            def queries(n, c, b):
                if n >= 2:
                    pe.wait_ge(k_used, NPAGE * (n - 1))
                nc.tensor.matmul(B[n % 2][:], s.ident[0:NS, b:b + 1].to_broadcast([NS, 128]), s.row["q" + c[1]][:],
                                 start=True, stop=True).then_inc(qb_ready, 1)

            def values(c, b):
                k = c[1]
                acc = P if k == "s" and b >= NS // 2 else O
                group = NS if k == "d" else NS // 2
                if b == 0:
                    pe.wait_ge(a_ready, 1 + "ds".index(k))
                    if k == "s":
                        pe.wait_ge(ov_ready, 1)
                for n in range(NPAGE):
                    m = PAGES["v"].index((c, b, n))
                    pe.wait_ge(page_in["v"][m % PLACES], 16 * (m // PLACES + 1))
                    nc.tensor.matmul(acc[32 * n:32 * n + 32, :], aZ[:, n, b, :], page["v"][:, m % PLACES, :], start=b % group == 0,
                                     stop=n > 0 and b % group == group - 1, skip_group_check=True).then_inc(v_used, 1)
                if b % group == group - 1:
                    nc.tensor.matmul(acc[0:32, :], aN[k][:, 32 * (b // group):32 * (b // group) + 32], s.row["v" + k][:], start=False,
                                     stop=True, skip_group_check=True).then_inc(o_ready, 1)

            def extract(n):
                pe.wait_ge(ov_ready, n + 1)
                if n == 1:
                    pe.wait_ge(orr_ready, 1)
                dst, e, w = ((S0[:, 0:32], C_DB, NS), (S0[:, 128:144], C_SB, 4), (O[:, 0:16], C_SB, 4))[n]
                for j in range(NB):
                    last = nc.tensor.matmul(dst[:, w * j:w * j + w], prod[:, 128 * j:128 * j + 128], s.c[:, e:e + w], start=True, stop=True)
                last.then_inc(ext_ready, 1)

            nc.tensor.matmul(P[0:R, :], s.c[0:NS, C_E:C_ET], s.sel_s[:, 0:PAST], start=True, stop=True)
            nc.tensor.matmul(O[0:R, 0:1], s.c[0:NS, C_E:C_ET], s.sel_s[:, PAST:PAST + 1], start=True, stop=True).then_inc(sel_up, 1)
            nq = m = 0
            for sl in range(SLOTS_A):
                if sl == SLOTS_A - 1:
                    turn(0, 0)
                    turn(0, 1)
                v, vb = VALUES_AT.get(sl, ("", []))
                product(m)
                if vb:
                    if sl == min(VALUES_AT):
                        pe.wait_ge(nk_read, 1)
                    values(v, vb[0])
                product(m + 1)
                m += 2
                if sl % NT == NT - 1:
                    product(m)
                    m += 1
                if sl in KEYS_AT:
                    for b in KEYS_AT[sl][1]:
                        queries(nq, KEYS_AT[sl][0], b)
                        nq += 1
                if sl == 1:
                    pe.wait_ge(sel_read, 1)
                    pe.wait_ge(nk_ready, 1)
                    nc.tensor.matmul(O[0:R, 16:32], s.c[0:NS, C_E:C_ET], nk[:].rearrange("b c h -> b (c h)"), start=True, stop=True).then_inc(nk_up, 1)
                if vb:
                    values(v, vb[1])
                if sl == OD_AT:
                    extract(0)
                if sl == OD_AT + 3:
                    extract(1)
                if sl == OD_AT + 2:
                    pe.wait_ge(oq_ready, 1)
                    nc.tensor.matmul(S0[:, 64:64 + NB * NS], s.c[:, C_ONE:C_CM], oq[:], start=True, stop=True).then_inc(o_sum, 1)
                if sl in SOFTMAX_AT:
                    k = SOFTMAX_AT[sl]
                    pe.wait_ge(sT_ready, 1 + "ds".index(k))
                    for n in range(NPAGE):
                        last = nc.tensor.transpose(P[0:R, 128 * n:128 * n + 128], sT[k][:, n, :], s.ident[:])
                    last.then_inc(sc_ready, 1)
                if sl - 1 in SOFTMAX_AT:
                    i = "ds".index(SOFTMAX_AT[sl - 1])
                    pe.wait_ge(weights, 2 * i + 2)
                    for n in range(NPAGE):
                        nc.tensor.transpose(P[:, 64 * n:64 * n + R], pr[:, 128 * n:128 * n + 128], s.ident[0:R, 0:R])
                    nc.tensor.matmul(P[0:NS, 256:256 + R], s.c[0:R, C_ET:C_HM], dg[:], start=True, stop=True).then_inc(p_turned, 1)
            for what, i, h in OUT[2:]:
                if what == "turn":
                    turn(i, h)
                elif what == "sum":
                    if (i, h) == (0, 0):
                        pe.wait_ge(oT_ready, 2)
                    summing(i, h)
                elif what == "extract":
                    extract(2)
                else:
                    pe.wait_ge(oT_ready, 3)
                    while m < len(PRODUCTS):
                        product(m)
                        m += 1

        @block.scalar
        def _(act):
            def exp(m):
                q, i, r = PRODUCTS[m]
                act.wait_ge(made, m + 1)
                bank = ring[m % RING]
                if i < NT:
                    n = exps(m) - q
                    if n >= 2:
                        act.wait_ge(y_read, n - 1)
                    nc.scalar.activation(gate[:, n % 2, :], bank[:], ACT.Sigmoid).then_inc(g_exp, 1)
                else:
                    for g in range(NB):
                        ins = nc.scalar.activation(gate_s[:, q, 128 * g:128 * g + 128], bank[32 * g:32 * g + NS, 0:128], ACT.Sigmoid)
                    ins.then_inc(g_exp, 1)

            def copy(i, h):
                p = ROWS[i]
                act.wait_ge(turned, upto("turn", i, h))
                if OUT_TILES.index(i) >= 2:
                    act.wait_ge(summed, max(upto("sum", before(i, 2), e) for e in range(2)))
                x = mT[OUT_TILES.index(i) % 2]
                nc.scalar.copy(x[:, 4 * h:4 * h + 4, 0:p], B[h][:].rearrange("p (j q) -> p j q", j=4)[:, :, 0:p]).then_inc(mt_out, 1)

            for sl in range(SLOTS_A):
                if sl == SLOTS_A - 1:
                    act.wait_ge(k_used, len(PAGES["k"]))
                    copy(0, 0)
                    copy(0, 1)
                if sl - 1 in SOFTMAX_AT:
                    i = "ds".index(SOFTMAX_AT[sl - 1])
                    act.wait_ge(max_ready, i + 1)
                    nc.scalar.activation(pr[:], sc[:], ACT.Exp, bias=nb[:, i:i + 1], scale=DH ** -0.5, accum_out=sm[:, i:i + 1]).then_inc(p_ready, 1)
                q, i = divmod(sl, NT)
                exp(m_of[(q, i, "g")])
                if i == NT - 1:
                    exp(m_of[(q, NT, "g")])
            for what, i, h in OUT[2:]:
                if what == "turn":
                    copy(i, h)

        @block.vector
        def _(dve):
            link = Chain(dve, chain)
            v = nc.vector

            def merge_tile(q, i):
                k, c = PASSES[q]
                m = m_of[(q, i, "g")]
                n = NT * q + i
                dve.wait_ge(g_exp, exps(m + 1))
                g = gate[:, n % 2, :]
                dve.wait_ge(made, m + 2)
                if k and NT * c + i:
                    dve.wait_ge(merged_ready, NT * c + i)
                dst = merged[:, i, W * c:W * c + W]
                v.tensor_tensor(branch[:] if k else dst, ring[(m + 1) % RING][:], g, ALU.mult).then_inc(y_read, 1)
                if k:
                    dve.wait_ge(y_read, n + 1)
                    v.tensor_tensor(dst, dst, branch[:], ALU.add).then_inc(merged_ready, 1)

            def add_x(i, h):
                dve.wait_ge(summed, upto("sum", i, h))
                if i < NT:
                    xs = s.x[:, i, W * h:W * h + W]
                    v.tensor_tensor(xs, S[h][:], xs, ALU.add).then_inc(x_done, 1)
                else:
                    for g in range(NB):
                        xs = s.x[0:NS, NT, W * h + 128 * g:W * h + 128 * g + 128]
                        ins = v.tensor_tensor(xs, S[h][32 * g:32 * g + NS, 0:128], xs, ALU.add)
                    ins.then_inc(x_done, 1)

            def keys(c, b):
                k = c[1]
                nq = NS * "ds".index(k) + b
                dve.wait_ge(qb_ready, nq + 1)
                for n0 in range(0, NPAGE, 2):
                    m0 = PAGES["k"].index((c, b, n0))
                    for m in (m0, m0 + 1):
                        dve.wait_ge(page_in["k"][m % PLACES], 16 * (m // PLACES + 1))
                        if m >= 2:
                            dve.wait_ge(k_summed, m - 1)
                        v.tensor_tensor(prods[m % 2][:], page["k"][:, m % PLACES, :], B[nq % 2][:], ALU.mult).then_inc(k_used, 1)
                    for m in (m0, m0 + 1):
                        dve.wait_ge(k_used, m + 1)
                        v.tensor_reduce(sT[k][:, n0 + m - m0, H * b:H * b + H], prods[m % 2][:].rearrange("p (h d) -> p h d", h=H),
                                        AX.X, ALU.add).then_inc(k_summed, 1)
                dve.wait_ge(k_summed, NPAGE * (nq + 1))
                if b == NS - 1:
                    dve.sem_inc(sT_ready, 1)

            def largest(k):
                i = "ds".index(k)
                dve.wait_ge(sc_ready, i + 1)
                if k == "d":
                    link(v.tensor_copy(sc[:, 0:PAST], P[0:R, :]))
                    link(v.tensor_copy(sc[:, PAST:PAST + 1], snew[:, i:i + 1]))
                else:
                    link(v.tensor_tensor(sc[:, 0:PAST], P[0:R, :], selb[:, 0:PAST], ALU.add))
                    link(v.tensor_tensor(sc[:, PAST:PAST + 1], snew[:, i:i + 1], selb[:, PAST:PAST + 1], ALU.add))
                link(v.tensor_reduce(mx[:, i:i + 1], sc[:], AX.X, ALU.max))
                v.tensor_scalar(nb[:, i:i + 1], mx[:, i:i + 1], -DH ** -0.5, None, ALU.mult).then_inc(max_ready, 1)

            def weigh(k):
                i = "ds".index(k)
                dve.wait_ge(p_ready, i + 1)
                link(v.reciprocal(cf[:, i:i + 1], sm[:, i:i + 1]))
                if k == "d":
                    link(v.tensor_scalar(mx[:, 0:1], s.neglam[0:R, :], -1.0, None, ALU.add))
                    link(v.tensor_tensor(mx[:, 0:1], mx[:, 0:1], s.c[0:R, C_PAR:C_PAR + 1], ALU.mult))
                    link(v.tensor_scalar(mx[:, 0:1], mx[:, 0:1], 1.0, None, ALU.add))
                    link(v.tensor_tensor(cf[:, 0:1], cf[:, 0:1], mx[:, 0:1], ALU.mult))
                v.tensor_scalar(pr[:], pr[:], cf[:, i:i + 1], None, ALU.mult).then_inc(weights, 1)
                dve.wait_ge(weights, 2 * i + 1)
                v.tensor_scalar(dg[:], s.ident[0:R, 0:R], pr[:, PAST:PAST + 1], None, ALU.mult).then_inc(weights, 1)

            def weights_turned(k):
                dve.wait_ge(p_turned, 1 + "ds".index(k))
                dve.wait_ge(zeros_ready, 1 if k == "d" else 3)
                if k == "d":
                    for b in range(NS):
                        v.tensor_reduce(aZ[:, :, b, 4 * b:4 * b + 4],
                                        P[:, 0:NPAGE * R].rearrange("p (n b h c) -> p n b h c", n=NPAGE, b=NS, c=2)[:, :, b], AX.X, ALU.add)
                    v.tensor_reduce(aN[k][:], P[0:NS, 256:256 + R].rearrange("p (h c) -> p h c", c=2), AX.X, ALU.add).then_inc(a_ready, 1)
                else:
                    for b in range(4):
                        for c in range(2):
                            v.tensor_copy(aZ[:, :, 4 * c + b, 8 * b:8 * b + 8],
                                          P[:, 0:NPAGE * R].rearrange("p (n b h) -> p n b h", n=NPAGE, b=NS)[:, :, 4 * c + b])
                    v.tensor_copy(aN[k][:], P[0:NS, 256:256 + R]).then_inc(a_ready, 1)

            def own_heads(n):
                dve.wait_ge(o_ready, n + 1)
                if n:
                    dve.wait_ge(ext_ready, n)
                acc, mask, h = ((O, C_DH, 4), (O, C_HM, 8), (P, C_HM, 8))[n]
                v.tensor_tensor(prod[:].rearrange("p (h d) -> p h d", h=h), acc[:].rearrange("p (h d) -> p h d", h=h),
                                bcast(s.c[:, mask:mask + h], W // h, 2), ALU.mult).then_inc(ov_ready, 1)

            def samples_out(n, src):
                dve.wait_ge(ext_ready, n + 2)
                v.tensor_copy(s.oT["s"][:, :, SEQ + 4 * n:SEQ + 4 * n + 4], src.rearrange("p (j b) -> p j b", j=NB)).then_inc(oT_ready, 1)

            dve.wait_ge(sel_up, 1)
            link(v.tensor_copy(selb[:, 0:PAST], P[0:R, :]))
            link(v.tensor_copy(selb[:, PAST:PAST + 1], O[0:R, 0:1]))
            dve.sem_inc(sel_read, 1)
            for i, k in enumerate("ds"):
                link(v.tensor_tensor(prod[0:NS, :], s.row["q" + k][:], s.row["k" + k][:], ALU.mult))
                link(v.tensor_reduce(nk[:, i, :], prod[0:NS, :].rearrange("p (h d) -> p h d", h=H), AX.X, ALU.add))
            dve.sem_inc(nk_ready, 1)
            jb = lambda ap: ap.rearrange("p (j b) -> p j b", j=NB)
            for sl in range(SLOTS_A):
                if sl - 1 in SOFTMAX_AT:
                    largest(SOFTMAX_AT[sl - 1])
                if sl == OD_AT:
                    own_heads(0)
                if sl == OD_AT + 1:
                    dve.wait_ge(ext_ready, 1)
                    link(v.tensor_copy(od[:], S0[:, 0:NB * NS]))
                    v.tensor_tensor(oq[:], od[:], od[:], ALU.mult).then_inc(oq_ready, 1)
                if sl == OD_AT + 3:
                    dve.wait_ge(o_sum, 1)
                    v.tensor_scalar(orr[:], S0[:, 64:64 + NB * NS], 1.0 / (2 * DH), EPS, ALU.mult, ALU.add).then_inc(orr_ready, 1)
                    own_heads(1)
                if sl == OD_AT + 4:
                    dve.wait_ge(o_rs, 1)
                    link(v.tensor_scalar(orr[:], orx[:], s.gsub[:], None, ALU.mult))
                    v.tensor_tensor(s.oT["d"][:, :, SEQ:TOK], jb(od[:]), jb(orr[:]), ALU.mult).then_inc(oT_ready, 1)
                    samples_out(0, S0[:, 128:144])
                if sl - 1 in SOFTMAX_AT:
                    weigh(SOFTMAX_AT[sl - 1])
                merge_tile(*divmod(sl, NT))
                if sl == 2:
                    dve.wait_ge(nk_up, 1)
                    link(v.tensor_tensor(nkh[:], O[0:R, 16:32].rearrange("r (c h) -> r c h", c=2), bcast(s.c[0:R, C_HM:C_IOTA], 2, 1), ALU.mult))
                    link(v.tensor_reduce(snew[:], nkh[:], AX.X, ALU.add))
                    dve.sem_inc(nk_read, 1)
                kk, kb = KEYS_AT.get(sl, ("", []))
                for b in kb[:1]:
                    keys(kk, b)
                if sl - 1 in SOFTMAX_AT:
                    weights_turned(SOFTMAX_AT[sl - 1])
                for b in kb[1:]:
                    keys(kk, b)
            own_heads(2)
            for what, i, h in OUT:
                if what == "sum":
                    add_x(i, h)
                elif what == "extract":
                    samples_out(1, O[:, 0:16])
                elif what == "branches":
                    for q, (k, c) in enumerate(PASSES):
                        m = m_of[(q, NT, "y")]
                        dve.wait_ge(made, m + 1)
                        dst = merged_s[:, W * c:W * c + W]
                        for g in range(NB):
                            cols = slice(128 * g, 128 * g + 128)
                            ins = v.tensor_tensor((branch[0:NS, :] if k else dst)[:, cols], ring[m % RING][32 * g:32 * g + NS, 0:128],
                                                  gate_s[:, q, cols], ALU.mult)
                        ins.then_inc(y_read, 1)
                        dve.wait_ge(y_read, reads(m + 1))
                        if k:
                            link(v.tensor_tensor(dst, dst, branch[0:NS, :], ALU.add))
                    dve.sem_inc(ms_ready, 1)


def route(nc, io, s):
    with ExitStack() as ctx:
        sb = lambda n, sh, dt=F32: ctx.enter_context(nc.sbuf_tensor("r_" + n, sh, dt))
        ps = lambda n, sh: ctx.enter_context(nc.psum_tensor("r_" + n, sh, F32))
        sem = lambda n: ctx.enter_context(nc.semaphore("r_" + n))
        sq = sb("sq", [128, D])
        ms, rs = sb("ms", [128, TILES]), sb("rs", [128, TILES])
        hn = sb("hn", [128, TILES, KD, 128])
        hT = sb("hT", [128, 2, KD, 128])
        wr = sb("wr", [128, KD, NG + NE])
        L = sb("L", [128, TILES, NG + NE])
        T = [ps(f"T{n}", [128, 4, 128]) for n in range(2)]
        LG = ps("LG", [128, TILES, 64])
        RK, CT, TB = ps("RK", [128, TILES, NE]), ps("CT", [128, NE]), ps("TB", [CAP, NBLK])
        small = {}

        def sm(name, *shape):
            small[name] = sb(name, [128, *shape])
            return small[name]
        gm, gs, gmin, gw = (sm(n, TILES) for n in ("gm", "gs", "gmin", "gw"))
        gexp, geq, gcand, goh = (sm(n, TILES, NG) for n in ("gexp", "geq", "gcand", "goh"))
        tmp = sm("tmp", TILES, NG, EG)
        ein, eeq, ecand = (sm(n, TILES, EG) for n in ("ein", "eeq", "ecand"))
        eoh = [sm(f"eoh{k}", TILES, EG) for k in range(2)]
        ev = [sm(f"ev{k}", TILES) for k in range(2)]
        emin, dl, valid = sm("emin", TILES), sm("dl", TILES), sm("valid", TILES)
        O = [sm(f"O{k}", TILES, NE) for k in range(2)]
        C = sm("C", TILES, NE)
        cnt, xe, Xi, shift, base = (sm(n, NE) for n in ("cnt", "xe", "Xi", "shift", "base"))
        cmp = sm("cmp", NE, NX)
        row, over = sm("row", TILES, NE), sm("over", TILES, NE)
        slot = sm("slot", 2, TILES)
        blk, rk, thr = sm("blk", 2, TILES), sm("rk", 2, TILES), sm("thr", NBLK)
        cmpb = sm("cmpb", 2 * TILES, NBLK)
        Bk, Rk = sm("Bk", 2 * TILES, NBLK), sm("Rk", 2 * TILES, CAP)
        eid = sm("eid", NX + 1)
        stored = [sem(f"stored{n}") for n in range(2)]
        (wr_in, x_sq, pool_chain, rms, hn_ready, turned, hT_ready, logits, chain, gd, gx, ranked, counted, cdone, tab_in,
         tabled, elx, wx) = map(sem, ("wr_in x_sq pool_chain rms hn_ready turned hT_ready logits chain gd gx ranked counted "
                                  "cdone tab_in tabled elx wx").split())
        block = ctx.enter_context(nc.Block())

        @block.sync
        def _(sp):
            sp.dma_start(s.gffn[:], io["g_ffn"][0].rearrange("(p j) -> p j", j=KD)).then_inc(wr_in, 16)
            sp.dma_start(wr[:, :, 0:NG], io["w_group"][0].rearrange("(p j) c -> p j c", j=KD)).then_inc(wr_in, 16)
            sp.dma_start(wr[:, :, NG:NG + NE], io["w_router"][0].rearrange("(p j) c -> p j c", j=KD)).then_inc(wr_in, 16)
            for e in range(2):
                for n, wt in enumerate(("w_gate", "w_up", "w_down")):
                    sp.dma_start(s.ew[n][:, e], s.expert(io[wt], e, n)).then_inc(s.ew_in[n][e], 16)
            for i, p in enumerate(ROWS):
                sp.wait_ge(hn_ready, i + 1)
                sp.dma_start(s.rows[128 * i:128 * i + p, :], hn[0:p, i].rearrange("p j q -> p (j q)")).then_inc(stored[i % 2], 16)
            for n in range(2):
                sp.wait_ge(stored[n], 16 * len(range(n, TILES, 2)))

        @block.scalar
        def _(act):
            for i, p in enumerate(ROWS):
                if i:
                    act.wait_ge(x_sq, i)
                nc.scalar.activation(sq[0:p, :], s.x[0:p, i, :], ACT.Square, accum_out=ms[0:p, i:i + 1]).then_inc(x_sq, 1)
            act.wait_ge(gd, 1)
            nc.scalar.activation(gexp[:], gexp[:], ACT.Exp).then_inc(gx, 1)
            act.wait_ge(gd, 2)
            nc.scalar.activation(dl[:], dl[:], ACT.Exp).then_inc(gx, 1)

        @block.gpsimd
        def _(pool):
            for i, p in enumerate(ROWS):
                pool.wait_ge(x_sq, i + 1)
                nc.gpsimd.tensor_scalar(rs[0:p, i:i + 1], ms[0:p, i:i + 1], 1.0 / D, EPS, ALU.mult, ALU.add).then_inc(pool_chain, 1)
                pool.wait_ge(pool_chain, i + 1)
                nc.gpsimd.tensor_tensor(rs[0:p, i:i + 1], rs[0:p, i:i + 1], s.c[0:p, C_MH:C_MH + 1], ALU.pow).then_inc(rms, 1)

        @block.tensor
        def _(pe):
            pe.wait_ge(wr_in, 48)
            for i, p in enumerate(ROWS):
                pe.wait_ge(hn_ready, i + 1)
                for h in range(2):
                    if i:
                        pe.wait_ge(hT_ready, 2 * i - 1 + h)
                    for j in range(4):
                        last = nc.tensor.transpose(T[h][:, j, 0:p], hn[0:p, i, 4 * h + j, :], s.ident[0:p, 0:p])
                    last.then_inc(turned, 1)
                pe.wait_ge(hT_ready, 2 * i + 2)
                for j in range(KD):
                    last = nc.tensor.matmul(LG[0:p, i, 0:NG + NE], hT[:, i % 2, j, 0:p], wr[:, j, :], start=j == 0, stop=j == KD - 1)
                last.then_inc(logits, 1)
            pe.wait_ge(cdone, 1)
            for j in range(TILES):
                last = nc.tensor.matmul(CT[:], s.c[:, C_ONE:C_CM], C[:, j, :], start=j == 0, stop=j == TILES - 1)
            last.then_inc(counted, 1)
            for i in range(TILES):
                for j in range(i + 1):
                    last = nc.tensor.matmul(RK[:, i, :], s.c[:, C_LT:C_ONE] if j == i else s.c[:, C_ONE:C_CM], C[:, j, :],
                                            start=j == 0, stop=j == i)
            last.then_inc(ranked, 1)
            pe.wait_ge(tab_in, 1)
            for m in range(2 * TILES):
                p = ROWS[m % TILES]
                last = nc.tensor.matmul(TB[:], Rk[0:p, m, :], Bk[0:p, m, :], start=m == 0, stop=m == 2 * TILES - 1)
            last.then_inc(tabled, 1)

        @block.vector
        def _(dve):
            link = Chain(dve, chain)
            v = nc.vector
            iota = lambda n: s.c[:, C_IOTA:C_IOTA + n]
            link(v.memset(L[:], 0.0))
            dve.wait_ge(wr_in, 48)
            for i, p in enumerate(ROWS):
                dve.wait_ge(rms, i + 1)
                v.tensor_scalar(hn[0:p, i], s.x[0:p, i, :].rearrange("t (p j) -> t j p", j=KD), rs[0:p, i:i + 1], None,
                                ALU.mult).then_inc(hn_ready, 1)
                for h in range(2):
                    dve.wait_ge(turned, 2 * i + h + 1)
                    if i >= 2:
                        dve.wait_ge(logits, i - 1)
                    v.tensor_tensor(hT[:, i % 2, 4 * h:4 * h + 4, 0:p], T[h][:, :, 0:p], bcast(s.gffn[:, 4 * h:4 * h + 4], p, 2),
                                    ALU.mult).then_inc(hT_ready, 1)
            dve.wait_ge(logits, TILES)
            link(v.tensor_copy(L[:, 0:NT, :], LG[:, 0:NT, 0:NG + NE]))
            link(v.tensor_copy(L[0:NS, NT, :], LG[0:NS, NT, 0:NG + NE]))
            Lg, Le = L[:, :, 0:NG], L[:, :, NG:NG + NE].rearrange("p t (g e) -> p t g e", g=NG)

            def first_max(src, n, top, eq, cand, low, onehot):
                link(v.tensor_reduce(top[:], src, AX.X, ALU.max))
                link(v.tensor_tensor(eq[:], src, bcast(top[:], n, 2), ALU.is_equal))
                link(v.tensor_scalar(eq[:], eq[:], -99.0, None, ALU.mult))
                link(v.tensor_tensor(cand[:], eq[:], bcast(iota(n), TILES, 1), ALU.add))
                link(v.tensor_reduce(low[:], cand[:], AX.X, ALU.min))
                link(v.tensor_tensor(onehot[:], cand[:], bcast(low[:], n, 2), ALU.is_equal))

            first_max(Lg, NG, gm, geq, gcand, gmin, goh)
            v.tensor_tensor(gexp[:], Lg, bcast(gm[:], NG, 2), ALU.subtract).then_inc(gd, 1)
            link(v.tensor_tensor(tmp[:], Le, bcast(goh[:], EG, 3), ALU.mult))
            link(v.tensor_reduce(ein[:], tmp[:].rearrange("p t g e -> p t e g"), AX.X, ALU.add))
            first_max(ein[:], EG, ev[0], eeq, ecand, emin, eoh[0])
            link(v.tensor_scalar(eeq[:], eoh[0][:], MASKED, None, ALU.mult))
            link(v.tensor_tensor(ein[:], ein[:], eeq[:], ALU.add))
            first_max(ein[:], EG, ev[1], eeq, ecand, emin, eoh[1])
            v.tensor_tensor(dl[:], ev[1][:], ev[0][:], ALU.subtract).then_inc(gd, 1)
            link(v.tensor_scalar(valid[:], s.c[:, C_TOK:C_THR], float(TOK), None, ALU.is_lt))
            link(v.tensor_tensor(goh[:], goh[:], bcast(valid[:], NG, 2), ALU.mult))
            for k in range(2):
                for g in range(NG):
                    link(v.tensor_tensor(O[k][:, :, EG * g:EG * g + EG], eoh[k][:], bcast(goh[:, :, g], EG, 2), ALU.mult))
            v.tensor_tensor(C[:], O[0][:], O[1][:], ALU.add).then_inc(cdone, 1)
            dve.wait_ge(counted, 1)
            link(v.tensor_copy(cnt[:], CT[:]))
            link(v.tensor_tensor(cmp[:], bcast(cnt[:], NX, 2), bcast(s.c[:, C_THR:C_MH], NE, 1), ALU.is_gt))
            link(v.tensor_reduce(xe[:], cmp[:], AX.X, ALU.add))
            link(v.tensor_tensor_scan(Xi[:], s.c[:, C_ONE:C_ONE + NE], xe[:], 0.0, ALU.mult, ALU.add))
            link(v.tensor_tensor(shift[:], Xi[:], xe[:], ALU.subtract))
            link(v.tensor_tensor(shift[:], shift[:], iota(NE), ALU.subtract))
            link(v.tensor_scalar(shift[:], shift[:], float(NE - 1), float(CAP), ALU.add, ALU.mult))
            link(v.tensor_scalar(base[:], iota(NE), float(CAP), None, ALU.mult))
            dve.wait_ge(ranked, 1)
            link(v.tensor_scalar(over[:], RK[:], float(CAP), None, ALU.is_ge))
            link(v.tensor_tensor(over[:], over[:], bcast(shift[:], TILES, 1), ALU.mult))
            link(v.tensor_tensor(row[:], RK[:], bcast(base[:], TILES, 1), ALU.add))
            link(v.tensor_tensor(row[:], row[:], over[:], ALU.add))
            for k in range(2):
                link(v.tensor_tensor(over[:], row[:], O[k][:], ALU.mult))
                link(v.tensor_reduce(slot[:, k, :], over[:], AX.X, ALU.add))
            link(v.tensor_copy(s.slot[:], slot[:]))
            link(v.tensor_scalar(thr[:], iota(NBLK), 1.0, float(CAP), ALU.add, ALU.mult))
            fl = slot[:].rearrange("p k t -> p (k t)")
            bl, rl = blk[:].rearrange("p k t -> p (k t)"), rk[:].rearrange("p k t -> p (k t)")
            link(v.tensor_tensor(cmpb[:], bcast(fl, NBLK, 2), bcast(thr[:], 2 * TILES, 1), ALU.is_ge))
            link(v.tensor_reduce(bl, cmpb[:], AX.X, ALU.add))
            link(v.tensor_scalar(rl, bl, -float(CAP), None, ALU.mult))
            link(v.tensor_tensor(rl, rl, fl, ALU.add))
            link(v.tensor_tensor(Rk[:], bcast(iota(CAP), 2 * TILES, 1), bcast(rl, CAP, 2), ALU.is_equal))
            link(v.tensor_tensor(Bk[:], bcast(iota(NBLK), 2 * TILES, 1), bcast(bl, NBLK, 2), ALU.is_equal))
            for k in range(2):
                last = v.tensor_tensor(Bk[:, TILES * k:TILES * k + TILES, :], Bk[:, TILES * k:TILES * k + TILES, :],
                                       bcast(s.c[:, C_TOK:C_THR], NBLK, 2), ALU.mult)
                link(last)
            dve.sem_inc(tab_in, 1)
            cmpe = cmp[:].rearrange("p a b -> p (a b)").rearrange("p (b e) -> p b e", b=NX)
            link(v.tensor_tensor(cmpe, bcast(Xi[:], NX, 1), bcast(iota(NX), NE, 2), ALU.is_le))
            link(v.tensor_reduce(eid[:, 0:NX], cmpe, AX.X, ALU.add))
            link(v.tensor_scalar(eid[:, 0:NX], eid[:, 0:NX], float(NE - 1), None, ALU.min))
            link(v.tensor_copy(eid[:, NX:NX + 1], Xi[:, NE - 1:NE]))
            link(v.tensor_copy(s.ctl[:], eid[0:1, :]))
            dve.wait_ge(gx, 2)
            link(v.tensor_reduce(gs[:], gexp[:], AX.X, ALU.add))
            link(v.reciprocal(gw[:], gs[:]))
            link(v.tensor_scalar(gs[:], dl[:], 1.0, None, ALU.add))
            link(v.reciprocal(gs[:], gs[:]))
            link(v.tensor_tensor(s.wt[:, 0, :], gs[:], gw[:], ALU.mult))
            link(v.tensor_tensor(s.wt[:, 1, :], s.wt[:, 0, :], dl[:], ALU.mult))
            dve.wait_ge(tabled, 1)
            link(v.tensor_copy(s.table[:], TB[:]))


HW = DE // 2


def experts(nc, io, s):
    with ExitStack() as ctx:
        sb = lambda n, sh, dt=F32: ctx.enter_context(nc.sbuf_tensor("e_" + n, sh, dt))
        ps = lambda n, sh: ctx.enter_context(nc.psum_tensor("e_" + n, sh, F32))
        sem = lambda n: ctx.enter_context(nc.semaphore("e_" + n))
        idx = sb("idx", [CAP, 2], I32)
        xg = [sb(f"xg{n}", [CAP, D]) for n in range(2)]
        xT = sb("xT", [128, 2, KD, CAP])
        sig, den, a = sb("sig", [128, HW]), sb("den", [128, HW]), sb("a", [128, HW])
        aT = sb("aT", [128, 2, 128])
        y = [sb(f"y{n}", [128, W]) for n in range(2)]
        TX, AT = ps("TX", [128, KD, CAP]), ps("AT", [128, 2, 128])
        G, U, Y = ([ps(f"{k}{n}", [128, w]) for n in range(2)] for k, w in (("G", W), ("U", W), ("Y", W)))
        (x_turned, xT_out, g_done, u_done, gated, chain, a_ready, a_turned, aT_out, d_done, y_out, idx_ready, x_started, idx_seen) = map(sem, (
            "x_turned xT_out g_done u_done gated chain a_ready a_turned aT_out d_done y_out idx_ready x_started idx_seen").split())
        xg_in = [sem(f"xg_in{n}") for n in range(2)]
        y_stored = [sem(f"y_stored{n}") for n in range(2)]
        block = ctx.enter_context(nc.Block())

        def pe_block(pe, e, it, j, first):
            pe.wait_ge(xg_in[j], it * 16 + 16)
            if not (first and j == 0):
                pe.wait_ge(xT_out, e)
            pe.sem_inc(x_started, 1)
            for b in range(KD):
                last = nc.tensor.transpose(TX[:, b, :], xg[j][:, 128 * b:128 * b + 128], s.ident[0:CAP, 0:CAP])
            last.then_inc(x_turned, 1)
            pe.wait_ge(xT_out, e + 1)
            if not first:
                pe.wait_ge(a_ready, e - 1)
            for n, (bank, done) in enumerate(((G[j], g_done), (U[j], u_done))):
                pe.wait_ge(s.ew_in[n][j], it * 16 + 16)
                for b in range(KD):
                    for h in range(2):
                        last = nc.tensor.matmul(bank[CAP * h:CAP * h + CAP, 0:HW], xT[:, j, b, :], s.ew[n][:, j, b, HW * h:HW * h + HW],
                                                start=b == 0, stop=b == KD - 1)
                last.then_inc(done, 1)
            pe.wait_ge(a_ready, e + 1)
            if not (first and j == 0):
                pe.wait_ge(aT_out, e)
            for b in range(2):
                last = nc.tensor.transpose(AT[:, b, :], a[:, 128 * b:128 * b + 128], s.ident[:])
            last.then_inc(a_turned, 1)
            pe.wait_ge(aT_out, e + 1)
            pe.wait_ge(s.ew_in[2][j], it * 16 + 16)
            if not first:
                pe.wait_ge(y_out, e - 1)
            for b in range(4):
                for h in range(2):
                    last = nc.tensor.matmul(Y[j][CAP * h:CAP * h + CAP, :], aT[:, b % 2, CAP * (b // 2):CAP * (b // 2) + CAP],
                                            s.ew[2][:, j, b, W * h:W * h + W], start=b == 0, stop=b == 3)
            last.then_inc(d_done, 1)

        def act_block(act, e, it, j, first):
            act.wait_ge(g_done, e + 1)
            if not (first and j == 0):
                act.wait_ge(a_ready, e)
            nc.scalar.activation(sig[:], G[j][:, 0:HW], ACT.Sigmoid).then_inc(gated, 1)
            act.wait_ge(d_done, e + 1)
            if not first:
                act.wait_ge(y_stored[j], it * 32)
            nc.scalar.copy(y[j][:], Y[j][:]).then_inc(y_out, 1)
            act.wait_ge(y_out, e + 1)
            for h in range(2):
                act.dma_start(s.out_rows(e)[:, W * h:W * h + W], y[j][CAP * h:CAP * h + CAP, :]).then_inc(y_stored[j], 16)

        def dve_block(dve, e, it, j, first):
            v = nc.vector
            dve.wait_ge(x_turned, e + 1)
            if not first:
                dve.wait_ge(u_done, e - 1)
            v.tensor_tensor(xT[:, j], TX[:], bcast(s.gffn[:], CAP, 2), ALU.mult).then_inc(xT_out, 1)
            dve.wait_ge(gated, e + 1)
            v.tensor_tensor(den[:], sig[:], G[j][:, 0:HW], ALU.mult).then_inc(chain, 1)
            dve.wait_ge(chain, e + 1)
            dve.wait_ge(u_done, e + 1)
            if not (first and j == 0):
                dve.wait_ge(a_turned, e)
            v.tensor_tensor(a[:], den[:], U[j][:, 0:HW], ALU.mult).then_inc(a_ready, 1)
            dve.wait_ge(a_turned, e + 1)
            if not (first and j == 0):
                dve.wait_ge(d_done, e)
            v.tensor_copy(aT[:], AT[:]).then_inc(aT_out, 1)

        def pool_block(pool, e, it, j, first):
            if not first:
                pool.wait_ge(x_turned, e - 1)
            nc.gpsimd.tensor_copy(idx[:, j:j + 1], s.table[:, bass.ds(e, 1)]).then_inc(idx_ready, 1)
            pool.wait_ge(idx_ready, e + 1)
            pool.sem_inc(idx_seen, 1)
            nc.gpsimd.indirect_dma_start(out=xg[j][:], out_offset=None, in_=s.rows[:, :],
                                         in_offset=bass.IndirectOffsetOnAxis(ap=idx[:, j:j + 1], axis=0)).then_inc(xg_in[j], 16)

        def sp_block(sp, e, it, j, first):
            for n, (wt, done) in enumerate((("w_gate", g_done), ("w_up", u_done), ("w_down", d_done))):
                sp.wait_ge(done, e - 1)
                sp.dma_start(s.ew[n][:, j], s.expert(io[wt], e, n)).then_inc(s.ew_in[n][j], 16)

        def run(eng, step, peel=True):
            if peel:
                for j in range(2):
                    step(eng, j, 0, j, True)
            with eng.Fori(1, NE // 2) as it:
                for j in range(2):
                    step(eng, it * 2 + j, it, j, False)

        def extra(eng, step):
            n = eng.value_load(s.ctl[0:1, NX:NX + 1], min_val=0, max_val=NX)
            with eng.If(n > 0):
                with eng.Fori(0, n) as b:
                    step(eng, b)
                eng.nop()
            eng.nop()

        @block.sync
        def _(sp):
            run(sp, sp_block, peel=False)

            def step(sp, b):
                e = sp.value_load(s.ctl[0:1, bass.ds(b, 1)], min_val=0, max_val=NE - 1)
                sp.wait_ge(y_out, b + NE)
                for n, wt in enumerate(("w_gate", "w_up", "w_down")):
                    sp.dma_start(s.ew[n][:, 0], s.expert(io[wt], e, n)).then_inc(s.ew_in[n][0], 16)
                sp.nop()
            extra(sp, step)
            sp.wait_ge(y_stored[1], NE * 16)
            sp.wait_ge(y_stored[0], NE * 16)

        @block.tensor
        def _(pe):
            run(pe, pe_block)

            def step(pe, b):
                pe.wait_ge(xg_in[0], b * 16 + NE * 8 + 16)
                pe.wait_ge(y_out, b + NE)
                pe.sem_inc(x_started, 1)
                for k in range(KD):
                    last = nc.tensor.transpose(TX[:, k, :], xg[0][:, 128 * k:128 * k + 128], s.ident[0:CAP, 0:CAP])
                last.then_inc(x_turned, 1)
                pe.wait_ge(xT_out, b + NE + 1)
                for n, (bank, done) in enumerate(((G[0], g_done), (U[0], u_done))):
                    pe.wait_ge(s.ew_in[n][0], b * 16 + NE * 8 + 16)
                    for k in range(KD):
                        for h in range(2):
                            last = nc.tensor.matmul(bank[CAP * h:CAP * h + CAP, 0:HW], xT[:, 0, k, :], s.ew[n][:, 0, k, HW * h:HW * h + HW],
                                                    start=k == 0, stop=k == KD - 1)
                    last.then_inc(done, 1)
                pe.wait_ge(a_ready, b + NE + 1)
                for k in range(2):
                    last = nc.tensor.transpose(AT[:, k, :], a[:, 128 * k:128 * k + 128], s.ident[:])
                last.then_inc(a_turned, 1)
                pe.wait_ge(aT_out, b + NE + 1)
                pe.wait_ge(s.ew_in[2][0], b * 16 + NE * 8 + 16)
                for k in range(4):
                    for h in range(2):
                        last = nc.tensor.matmul(Y[0][CAP * h:CAP * h + CAP, :], aT[:, k % 2, CAP * (k // 2):CAP * (k // 2) + CAP],
                                                s.ew[2][:, 0, k, W * h:W * h + W], start=k == 0, stop=k == 3)
                last.then_inc(d_done, 1)
                pe.nop()
            extra(pe, step)

        @block.scalar
        def _(act):
            run(act, act_block)

            def step(act, b):
                act.wait_ge(g_done, b + NE + 1)
                nc.scalar.activation(sig[:], G[0][:, 0:HW], ACT.Sigmoid).then_inc(gated, 1)
                act.wait_ge(d_done, b + NE + 1)
                act.wait_ge(y_stored[0], b * 32 + NE * 16)
                nc.scalar.copy(y[0][:], Y[0][:]).then_inc(y_out, 1)
                act.wait_ge(y_out, b + NE + 1)
                for h in range(2):
                    act.dma_start(s.out_rows(b + NE)[:, W * h:W * h + W], y[0][CAP * h:CAP * h + CAP, :]).then_inc(y_stored[0], 16)
                act.wait_ge(y_stored[0], b * 32 + NE * 16 + 32)
                act.nop()
            extra(act, step)

        @block.vector
        def _(dve):
            run(dve, dve_block)

            def step(dve, b):
                v = nc.vector
                dve.wait_ge(x_turned, b + NE + 1)
                v.tensor_tensor(xT[:, 0], TX[:], bcast(s.gffn[:], CAP, 2), ALU.mult).then_inc(xT_out, 1)
                dve.wait_ge(gated, b + NE + 1)
                v.tensor_tensor(den[:], sig[:], G[0][:, 0:HW], ALU.mult).then_inc(chain, 1)
                dve.wait_ge(chain, b + NE + 1)
                dve.wait_ge(u_done, b + NE + 1)
                v.tensor_tensor(a[:], den[:], U[0][:, 0:HW], ALU.mult).then_inc(a_ready, 1)
                dve.wait_ge(a_turned, b + NE + 1)
                v.tensor_copy(aT[:], AT[:]).then_inc(aT_out, 1)
                dve.nop()
            extra(dve, step)

        @block.gpsimd
        def _(pool):
            run(pool, pool_block)

            def step(pool, b):
                pool.wait_ge(x_turned, b + NE)
                nc.gpsimd.tensor_copy(idx[:, 0:1], s.table[:, bass.ds(b + NE, 1)]).then_inc(idx_ready, 1)
                pool.wait_ge(idx_ready, b + NE + 1)
                pool.sem_inc(idx_seen, 1)
                nc.gpsimd.indirect_dma_start(out=xg[0][:], out_offset=None, in_=s.rows[:, :],
                                             in_offset=bass.IndirectOffsetOnAxis(ap=idx[:, 0:1], axis=0)).then_inc(xg_in[0], 16)
                pool.nop()
            extra(pool, step)


def combine_experts(nc, io, s):
    with ExitStack() as ctx:
        sem = lambda n: ctx.enter_context(nc.semaphore("c_" + n))
        yg = [[ctx.enter_context(nc.sbuf_tensor(f"c_yg{i}{k}", [128, D], F32)) for k in range(2)] for i in range(TILES)]
        rows_in = [sem(f"rows_in{i}") for i in range(TILES)]
        chain, done, stored = sem("chain"), sem("done"), sem("stored")
        block = ctx.enter_context(nc.Block())

        @block.gpsimd
        def _(pool):
            for i, p in enumerate(ROWS):
                for k in range(2):
                    nc.gpsimd.indirect_dma_start(out=yg[i][k][0:p, :], out_offset=None, in_=s.eout[:, :],
                                                 in_offset=bass.IndirectOffsetOnAxis(ap=s.slot[0:p, k, i:i + 1], axis=0)).then_inc(rows_in[i], 16)

        @block.vector
        def _(dve):
            for i, p in enumerate(ROWS):
                dve.wait_ge(rows_in[i], 32)
                xs = s.x[0:p, i, :]
                nc.vector.scalar_tensor_tensor(xs, yg[i][0][0:p, :], s.wt[0:p, 0, i:i + 1], xs, ALU.mult, ALU.add).then_inc(chain, 1)
                dve.wait_ge(chain, i + 1)
                nc.vector.scalar_tensor_tensor(xs, yg[i][1][0:p, :], s.wt[0:p, 1, i:i + 1], xs, ALU.mult, ALU.add).then_inc(done, 1)

        @block.sync
        def _(sp):
            for i, p in enumerate(ROWS):
                sp.wait_ge(done, i + 1)
                dst = io["y_p"][128 * i:128 * i + p, :] if i < NT else io["y_s"]
                sp.dma_start(dst, s.x[0:p, i, :]).then_inc(stored, 16)
            sp.wait_ge(stored, 16 * TILES)


class State:
    pass


def step_kernel(nc, io):
    s = State()
    s.pool = io["cache_idx_k"].shape[1]
    s.rows = nc.dram_tensor("token_rows", (TOK, D), F32, kind="Internal").ap()
    s.eout = nc.dram_tensor("expert_rows", (NBLK * CAP, D), F32, kind="Internal").ap()
    s.out_rows = lambda e: s.eout.rearrange("(b c) d -> b c d", c=CAP)[e]
    s.expert = lambda ap, e, n: ap[0, e].rearrange("(p j) c -> p j c", j=KD) if n < 2 else ap[0, e].rearrange("(j p) c -> p j c", p=128)

    def tensors(stack, prefix):
        return lambda n, sh, dt=F32: stack.enter_context(nc.sbuf_tensor(prefix + n, sh, dt))

    with ExitStack() as top:
        sb = tensors(top, "k_")
        s.x = sb("x", [128, TILES, D])
        s.c = sb("c", [128, C_END])
        s.ident = s.c[:, C_ID:C_LT]
        with ExitStack() as mix:
            sb = tensors(mix, "m_")
            s.w_in = [mix.enter_context(nc.semaphore(f"w_in{n}")) for n in range(2)]
            s.xT = sb("xT", [128, KD, TOK])
            s.w = sb("w", [128, 2, KD, W])
            s.oT = {k: sb("oT" + k, [128, NB, TOK]) for k in "ds"}
            s.neglam, s.gsub = sb("neglam", [128, 1]), sb("gsub", [128, 1])
            s.row = {k: sb("row" + k, [NS, W]) for k in NORMED + ("vs", "vd")}
            s.sel_s = sb("sel_s", [NS, PAST + 1])
            with ExitStack() as att:
                sb = tensors(att, "t_")
                s.T = {k: sb("T" + k, [128, NB, SEQ]) for k in NORMED}
                s.v = {k: sb("v" + k, [128, NT, W]) for k in ("vs", "vd")}
                s.sel = [None] + [sb(f"sel{t}", [128, 128 * (t + 1)]) for t in range(1, NT)]
                with ExitStack() as pr:
                    sb = tensors(pr, "q_")
                    s.gmix = sb("gmix", [128, KD])
                    s.gains = sb("gains", [128, 4, DH])
                    s.rope = sb("rope", [128, 2, TILES, DH])
                    s.rg = sb("rg", [128, 4, 2, TILES, DH])
                    normalise_inputs(nc, io, s)
                    project(nc, io, s)
                attend_prompt(nc, io, s)
            merge(nc, io, s)
        with ExitStack() as moe:
            sb = tensors(moe, "x_")
            s.gffn = sb("gffn", [128, KD])
            s.wt, s.slot = sb("wt", [128, 2, TILES]), sb("slot", [128, 2, TILES], I32)
            s.table, s.ctl = sb("table", [CAP, NBLK], I32), sb("ctl", [1, NX + 1], I32)
            with ExitStack() as ring:
                s.ew = [ring.enter_context(nc.sbuf_tensor(f"x_ew{n}", [128, 2, *sh], F32)) for n, sh in enumerate(((KD, DE), (KD, DE), (4, D)))]
                s.ew_in = [[ring.enter_context(nc.semaphore(f"ew_in{n}{j}")) for j in range(2)] for n in range(3)]
                route(nc, io, s)
                experts(nc, io, s)
            combine_experts(nc, io, s)


INPUTS = ["x_prompt", "x_sample", "cache_diff_k", "cache_diff_v", "cache_dsa_k", "cache_dsa_v", "cache_idx_k", "page_table", "g_mix",
          "w_in", "g_q_diff", "g_k_diff", "lam_q1", "lam_k1", "lam_q2", "lam_k2", "g_subln", "g_q_dsa", "g_k_dsa", "w_o_diff",
          "w_o_dsa", "w_out", "g_ffn", "w_group", "w_router", "w_gate", "w_up", "w_down"]
KEPT = [("kd", W, (4, 2, DH)), ("vd", W, (4, 2 * DH)), ("ks", W, (H, DH)), ("vs", W, (H, DH)), ("ki", DH, (DH,))]
OUTPUTS = ([("y_p", (SEQ, D), (1, SEQ, D)), ("y_s", (NS, D), (NS, 1, D))]
           + [(f"new_{n}_p", (SEQ, w), (1, 1, SEQ, *sh)) for n, w, sh in KEPT]
           + [(f"new_{n}_s", (NS, w), (1, NS, 1, *sh)) for n, w, sh in KEPT])


def kernel(**inputs):
    import concourse.bacc as bacc
    from concourse.bass_utils import run_bass_kernel_spmd

    nc = bacc.Bacc("TRN2", target_bir_lowering=False, num_devices=1)
    arrays = {f"in_{name}": np.ascontiguousarray(inputs[name]) for name in INPUTS}
    arrays["in_consts"] = constants()
    arrays["in_rope"] = rope_table().reshape(128, 2, TILES, DH)
    io = {n[3:]: nc.dram_tensor(n, a.shape, mybir.dt.from_np(a.dtype), kind="ExternalInput").ap() for n, a in arrays.items()}
    for name, shape, _ in OUTPUTS:
        io[name] = nc.dram_tensor("out_" + name, shape, F32, kind="ExternalOutput").ap()
    step_kernel(nc, io)
    got = run_bass_kernel_spmd(nc, [arrays], core_ids=[0]).results[0]
    return tuple(got["out_" + name].reshape(full) for name, _, full in OUTPUTS)
```
